# Optimizing a Trainium2 kernel written in Bass

```python
import jax
import jax.numpy as jnp
from jax import lax
import numpy as np

D_MODEL = 1024
BATCH = 1
SEQ = 1024
DEPTH = 1

N_META = 16
CHUNK = 64
N_PAD = CHUNK - N_META
EPS = 1e-6

HG_HEADS = 4
HG_EXPAND = 128
HG_VDIM = 128
HG_FDIM = HG_HEADS * HG_EXPAND
HG_WIDTH = HG_HEADS * HG_VDIM

ML_HEADS = 4
ML_QKDIM = 64
ML_VDIM = 128
ML_WIDTH = ML_HEADS * ML_VDIM
ML_CONV = 4

N_BRANCH = 2
IN_SPLITS = (
    HG_FDIM,
    2 * HG_FDIM,
    2 * HG_FDIM + HG_WIDTH,
    2 * HG_FDIM + 2 * HG_WIDTH,
    2 * HG_FDIM + 2 * HG_WIDTH + ML_WIDTH,
    2 * HG_FDIM + 2 * HG_WIDTH + 2 * ML_WIDTH,
    2 * HG_FDIM + 2 * HG_WIDTH + 2 * ML_WIDTH + 2 * ML_HEADS,
)
IN_TOTAL = IN_SPLITS[-1] + N_BRANCH * D_MODEL

N_EXPERTS = 32
TOP_K = 4
D_FF = 1024
SWIGLU_LIMIT = 7.0
SWIGLU_ALPHA = 1.702
MOE_BLOCK = 128

kernel_name = 'hybrid_hgrn2_mlstm_moe'

def _rms(x):
    xf = x.astype(jnp.float32)
    y = xf * lax.rsqrt(jnp.mean(xf * xf, axis=-1, keepdims=True) + EPS)
    return y.astype(x.dtype)

def rmsnorm(x, w):
    return _rms(x) * w

def head_rmsnorm(o, w):
    b, t, h, d = o.shape
    return _rms(o).reshape(b, t, h * d) * w

def to_chunks(a):
    b, t = a.shape[:2]
    a = a.reshape((b, t // CHUNK, CHUNK) + a.shape[2:])
    perm = (1, 0, 3, 2) + tuple(range(4, a.ndim))
    return a.transpose(perm)

def from_chunks(o):
    nc, b, h, l, d = o.shape
    return o.transpose(1, 0, 3, 2, 4).reshape(b, nc * l, h, d)

def causal_depthwise_conv(u, w, bias):
    c = u.shape[-1]
    y = lax.conv_general_dilated(
        u, w[:, None, :].astype(u.dtype), window_strides=(1,),
        padding=[(ML_CONV - 1, 0)], dimension_numbers=('NWC', 'WIO', 'NWC'),
        feature_group_count=c)
    return y + bias

def hgrn2_chunkwise(q, k, v, log_f):
    f32 = jnp.float32
    qc, kc, vc, gc = (to_chunks(a.astype(f32)) for a in (q, k, v, log_f))
    cum = jnp.cumsum(gc, axis=-2)
    causal = jnp.tril(jnp.ones((CHUNK, CHUNK), bool))[:, :, None]

    def step(state, inp):
        q_, k_, v_, b_ = inp
        diff = b_[..., :, None, :] - b_[..., None, :, :]
        decay = jnp.exp(jnp.where(causal, diff, -jnp.inf))
        scores = jnp.einsum('bhtd,bhsd,bhtsd->bhts', q_, k_, decay)
        o = (jnp.einsum('bhts,bhsv->bhtv', scores, v_)
             + jnp.einsum('bhtd,bhdv->bhtv', q_ * jnp.exp(b_), state))
        b_last = b_[..., -1:, :]
        new_state = (jnp.exp(b_last[..., 0, :])[..., None] * state
                     + jnp.einsum('bhsd,bhsv->bhdv', k_ * jnp.exp(b_last - b_), v_))
        return new_state, o

    bsz, _, heads, dk = q.shape
    state0 = jnp.zeros((bsz, heads, dk, v.shape[-1]), f32)
    _, o = lax.scan(step, state0, (qc, kc, vc, cum))
    return from_chunks(o)

def mlstm_chunkwise(q, k, v, log_i, log_f):
    f32 = jnp.float32
    dk = q.shape[-1]
    qc, kc, vc = (to_chunks(a.astype(f32)) for a in (q * (dk ** -0.5), k, v))
    ic, fc = (to_chunks(a.astype(f32)) for a in (log_i, log_f))
    cum = jnp.cumsum(fc, axis=-1)
    causal = jnp.tril(jnp.ones((CHUNK, CHUNK), bool))

    def step(carry, inp):
        s, n, m = carry
        q_, k_, v_, li, b_ = inp
        d = jnp.where(causal, b_[..., :, None] - b_[..., None, :] + li[..., None, :], -jnp.inf)
        a = b_ + m[..., None]
        m_t = jnp.maximum(a, jnp.max(d, axis=-1))
        w_intra = jnp.exp(d - m_t[..., None])
        w_inter = jnp.exp(a - m_t)
        qk = jnp.einsum('bhtd,bhsd->bhts', q_, k_) * w_intra
        num = (jnp.einsum('bhts,bhsv->bhtv', qk, v_)
               + w_inter[..., None] * jnp.einsum('bhtd,bhdv->bhtv', q_, s))
        den = jnp.sum(qk, axis=-1) + w_inter * jnp.einsum('bhtd,bhd->bht', q_, n)
        h = num / jnp.maximum(jnp.abs(den), jnp.exp(-m_t))[..., None]
        g_last = b_[..., -1]
        e = g_last[..., None] - b_ + li
        m_new = jnp.maximum(g_last + m, jnp.max(e, axis=-1))
        w_s = jnp.exp(e - m_new[..., None])
        w_p = jnp.exp(g_last + m - m_new)
        s_new = w_p[..., None, None] * s + jnp.einsum('bhs,bhsd,bhsv->bhdv', w_s, k_, v_)
        n_new = w_p[..., None] * n + jnp.einsum('bhs,bhsd->bhd', w_s, k_)
        return (s_new, n_new, m_new), h

    bsz, _, heads, _ = q.shape
    carry0 = (jnp.zeros((bsz, heads, dk, v.shape[-1]), f32),
              jnp.zeros((bsz, heads, dk), f32),
              jnp.zeros((bsz, heads), f32))
    _, h = lax.scan(step, carry0, (qc, kc, vc, ic, cum))
    return from_chunks(h)

def moe_ffn(xn, router_w, router_b, w_gu, b_gu, w_dn, b_dn):
    bsz, t, d = xn.shape
    n_tok = bsz * t
    xt = xn.reshape(n_tok, d)
    logits = (xt @ router_w + router_b).astype(jnp.float32)
    top_v, top_e = lax.top_k(logits, TOP_K)
    gate_w = jax.nn.softmax(top_v, axis=-1)
    n_assign = n_tok * TOP_K
    e_flat = top_e.reshape(n_assign).astype(jnp.int32)
    tok_flat = jnp.arange(n_assign, dtype=jnp.int32) // TOP_K
    w_flat = gate_w.reshape(n_assign)
    order = jnp.argsort(e_flat)
    e_sorted = e_flat[order]
    tok_sorted = tok_flat[order]
    w_sorted = w_flat[order]
    counts = jnp.bincount(e_flat, length=N_EXPERTS).astype(jnp.int32)
    starts = jnp.cumsum(counts) - counts
    padded = ((counts + MOE_BLOCK - 1) // MOE_BLOCK) * MOE_BLOCK
    pend = jnp.cumsum(padded)
    pstart = pend - padded
    dest = pstart[e_sorted] + (jnp.arange(n_assign, dtype=jnp.int32) - starts[e_sorted])
    n_blocks = -(-n_assign // MOE_BLOCK) + N_EXPERTS
    n_rows = n_blocks * MOE_BLOCK
    row_tok = jnp.full((n_rows,), n_tok, jnp.int32).at[dest].set(tok_sorted)
    row_w = jnp.zeros((n_rows,), jnp.float32).at[dest].set(w_sorted)
    block_e = jnp.minimum(
        jnp.searchsorted(pend, jnp.arange(n_blocks, dtype=jnp.int32) * MOE_BLOCK, side='right'),
        N_EXPERTS - 1)
    x_pad = jnp.concatenate([xt, jnp.zeros((1, d), xt.dtype)], axis=0)
    xb = x_pad[row_tok].reshape(n_blocks, MOE_BLOCK, d)

    def expert_block(args):
        xblk, e = args
        gu = xblk @ w_gu[e] + b_gu[e]
        gate = jnp.minimum(gu[:, 0::2], SWIGLU_LIMIT)
        up = jnp.clip(gu[:, 1::2], -SWIGLU_LIMIT, SWIGLU_LIMIT)
        act = (up + 1.0) * gate * jax.nn.sigmoid(SWIGLU_ALPHA * gate)
        return act @ w_dn[e] + b_dn[e]

    yb = lax.map(expert_block, (xb, block_e)).reshape(n_rows, d)
    y = jnp.zeros((n_tok + 1, d), jnp.float32).at[row_tok].add(
        yb.astype(jnp.float32) * row_w[:, None])
    return y[:n_tok].reshape(bsz, t, d).astype(xn.dtype)

def setup_inputs(seed: int = 0) -> dict:
    key = jax.random.key(seed)
    ks = jax.random.split(key, 32)
    f32 = jnp.float32

    def nrm(k, shape, scale):
        return jax.random.normal(k, shape, f32) * scale

    def gain(k, shape):
        return 1.0 + 0.02 * jax.random.normal(k, shape, f32)

    ml_gate_b = jnp.concatenate([
        nrm(ks[10], (DEPTH, ML_HEADS), 0.1),
        jnp.linspace(3.0, 6.0, ML_HEADS, dtype=f32)[None, :] + nrm(ks[11], (DEPTH, ML_HEADS), 0.1),
    ], axis=-1)
    return {
        'x': nrm(ks[0], (BATCH, SEQ, D_MODEL), 1.0),
        'meta_tokens': nrm(ks[1], (N_META, D_MODEL), 1.0),
        'hg_lb_logits': nrm(ks[2], (DEPTH + 1, HG_FDIM), 0.5),
        'norm_mix': gain(ks[3], (DEPTH, D_MODEL)),
        'w_in': nrm(ks[4], (DEPTH, D_MODEL, IN_TOTAL), D_MODEL ** -0.5),
        'hg_norm': gain(ks[5], (DEPTH, HG_WIDTH)),
        'ml_conv_w': nrm(ks[6], (DEPTH, ML_CONV, ML_WIDTH), ML_CONV ** -0.5),
        'ml_conv_b': nrm(ks[7], (DEPTH, ML_WIDTH), 0.01),
        'ml_wq': nrm(ks[8], (DEPTH, ML_HEADS, ML_VDIM, ML_QKDIM), ML_VDIM ** -0.5),
        'ml_wk': nrm(ks[9], (DEPTH, ML_HEADS, ML_VDIM, ML_QKDIM), ML_VDIM ** -0.5),
        'ml_wv': nrm(ks[12], (DEPTH, ML_HEADS, ML_VDIM, ML_VDIM), ML_VDIM ** -0.5),
        'ml_gate_b': ml_gate_b,
        'ml_norm': gain(ks[13], (DEPTH, ML_WIDTH)),
        'ml_skip': gain(ks[14], (DEPTH, ML_WIDTH)),
        'w_branch_hg': nrm(ks[15], (DEPTH, HG_WIDTH, D_MODEL), HG_WIDTH ** -0.5),
        'w_branch_ml': nrm(ks[16], (DEPTH, ML_WIDTH, D_MODEL), ML_WIDTH ** -0.5),
        'w_out': nrm(ks[17], (DEPTH, D_MODEL, D_MODEL), D_MODEL ** -0.5),
        'norm_ffn': gain(ks[18], (DEPTH, D_MODEL)),
        'router_w': nrm(ks[19], (DEPTH, D_MODEL, N_EXPERTS), D_MODEL ** -0.5),
        'router_b': nrm(ks[20], (DEPTH, N_EXPERTS), 0.01),
        'exp_w_gu': nrm(ks[21], (DEPTH, N_EXPERTS, D_MODEL, 2 * D_FF), D_MODEL ** -0.5),
        'exp_b_gu': nrm(ks[22], (DEPTH, N_EXPERTS, 2 * D_FF), 0.01),
        'exp_w_down': nrm(ks[23], (DEPTH, N_EXPERTS, D_FF, D_MODEL), D_FF ** -0.5),
        'exp_b_down': nrm(ks[24], (DEPTH, N_EXPERTS, D_MODEL), 0.01),
        'norm_final': gain(ks[25], (D_MODEL,)),
    }

def reference(x, meta_tokens, hg_lb_logits, norm_mix, w_in, hg_norm, ml_conv_w, ml_conv_b,
              ml_wq, ml_wk, ml_wv, ml_gate_b, ml_norm, ml_skip, w_branch_hg, w_branch_ml,
              w_out, norm_ffn, router_w, router_b, exp_w_gu, exp_b_gu, exp_w_down,
              exp_b_down, norm_final):
    f32 = jnp.float32
    bsz = x.shape[0]
    dt = x.dtype
    h = jnp.concatenate([
        jnp.zeros((bsz, N_PAD, D_MODEL), dt),
        jnp.broadcast_to(meta_tokens.astype(dt)[None], (bsz, N_META, D_MODEL)),
        x,
    ], axis=1)
    t = h.shape[1]
    valid = (jnp.arange(t) >= N_PAD)[None, :, None]
    lower_bounds = jnp.cumsum(jax.nn.softmax(hg_lb_logits.astype(f32), axis=0), axis=0)

    for l in range(DEPTH):
        xn = rmsnorm(h, norm_mix[l])
        proj = xn @ w_in[l]
        hq, hf, hi, hg, mm, mo, mif, gates = jnp.split(proj, IN_SPLITS, axis=-1)

        lb = lower_bounds[l]
        f = lb + (1.0 - lb) * jax.nn.sigmoid(hf.astype(f32))
        f = jnp.where(valid, f, 1.0)
        q_h = jax.nn.silu(hq).reshape(bsz, t, HG_HEADS, HG_EXPAND)
        k_h = (1.0 - f).reshape(bsz, t, HG_HEADS, HG_EXPAND)
        logf_h = jnp.log(f).reshape(bsz, t, HG_HEADS, HG_EXPAND)
        v_h = hi.reshape(bsz, t, HG_HEADS, HG_VDIM)
        o_h = hgrn2_chunkwise(q_h, k_h, v_h, logf_h).astype(dt)
        y_hg = head_rmsnorm(o_h, hg_norm[l]) * jax.nn.silu(hg)

        mm = jnp.where(valid, mm, 0.0)
        c = jax.nn.silu(causal_depthwise_conv(mm, ml_conv_w[l], ml_conv_b[l]))
        ch = c.reshape(bsz, t, ML_HEADS, ML_VDIM)
        mh = mm.reshape(bsz, t, ML_HEADS, ML_VDIM)
        q_m = jnp.einsum('bthc,hcd->bthd', ch, ml_wq[l])
        k_m = jnp.einsum('bthc,hcd->bthd', ch, ml_wk[l])
        v_m = jnp.einsum('bthc,hcd->bthd', mh, ml_wv[l])
        gi, gf = jnp.split(mif.astype(f32) + ml_gate_b[l].astype(f32), 2, axis=-1)
        log_i = jnp.where(valid, gi, -jnp.inf)
        log_fm = jnp.where(valid, jax.nn.log_sigmoid(gf), 0.0)
        o_m = mlstm_chunkwise(q_m, k_m, v_m, log_i, log_fm).astype(dt)
        y_ml = (head_rmsnorm(o_m, ml_norm[l]) + ml_skip[l] * c) * jax.nn.sigmoid(mo)

        g = jax.nn.sigmoid(gates).reshape(bsz, t, N_BRANCH, D_MODEL)
        merged = g[:, :, 0] * (y_hg @ w_branch_hg[l]) + g[:, :, 1] * (y_ml @ w_branch_ml[l])
        h = h + merged @ w_out[l]

        ffn_out = moe_ffn(rmsnorm(h[:, N_PAD:], norm_ffn[l]), router_w[l], router_b[l],
                          exp_w_gu[l], exp_b_gu[l], exp_w_down[l], exp_b_down[l])
        h = h.at[:, N_PAD:].add(ffn_out)

    return rmsnorm(h[:, N_PAD + N_META:], norm_final)


_drawn_inputs = setup_inputs


def setup_inputs(seed=0):
    import zlib

    import numpy as np

    out = dict(_drawn_inputs(seed))
    spreads = {}
    factors = {'ml_conv_b': 3.103,
     'ml_skip': 3.923,
     'exp_b_gu': 8.0,
     'exp_b_down': 8.0,
     'norm_final': 2.801}
    for name, (base, spread) in spreads.items():
        noise = np.random.default_rng([zlib.crc32(name.encode()), seed]).standard_normal(out[name].shape)
        drawn = base * np.exp(spread * noise) if base else spread * noise
        out[name] = jnp.asarray(drawn.astype(out[name].dtype))
    for name, factor in factors.items():
        out[name] = (out[name] * factor).astype(out[name].dtype)
    return out
```

```python
import numpy as np
import concourse.bass as bass
from concourse import mybir
from contextlib import ExitStack

F32 = mybir.dt.float32
I32 = mybir.dt.int32
U32 = mybir.dt.uint32
ALU = mybir.AluOpType
ACT = mybir.ActivationFunctionType
AX = mybir.AxisListType

P = 128
D = 1024
KD = D // P
META, SEQ = 16, 1024
CH = 128
NCH = 3
SPAN = NCH * CH
NSPAN = 3
ROWS = NSPAN * SPAN
LEAD = ROWS - SEQ
PAD = LEAD - META
H = 4
W = 512
QK = 64
SUB = 16
NSUB = CH // SUB
EPS = 1e-6
NEG = -1e30
BIG = 1e34

E = 32
TOPK = 4
FF = 1024
CAP = 1024
NT = SEQ // P
MAIN, TAIL = 160, 64
TAB = E * CAP + 256
LIMIT, ALPHA = 7.0, 1.702
NOROW = 1 << 20

WC = 256
NRING = 4
C_HQ, C_HF, C_HI, C_HG, C_MM, C_MO, C_IF, C_G0 = 0, 512, 1024, 1536, 2048, 2560, 3072, 3080
C_G1 = C_G0 + D


class Events:

    def __init__(self, nc, ctx):
        self.nc, self.ctx, self.made = nc, ctx, {}

    def __call__(self, name):
        if name not in self.made:
            self.made[name] = self.ctx.enter_context(self.nc.semaphore(name))
        return self.made[name]


class Banks:

    def __init__(self, nbanks):
        self.n, self.at, self.jobs, self.count, self.owner = nbanks, 0, {}, {"A": 0, "D": 0}, {}
        self.total = 0

    def add(self, name, engine, width=1):
        at = self.at if self.at + width <= self.n else 0
        before = [self.owner[b] for b in range(at, at + width) if b in self.owner]
        waits = {}
        for e, c in before:
            waits[e] = max(waits.get(e, 0), c)
        self.count[engine] += 1
        self.total += 1
        for b in range(at, at + width):
            self.owner[b] = (engine, self.count[engine])
        self.at = at + width
        self.jobs[name] = (at, self.total, waits, engine)

    def bank(self, name):
        return self.jobs[name][0]

    def ready(self, name):
        return self.jobs[name][1]


def span_jobs():
    b = Banks(8)
    for k in range(KD):
        b.add(("xT", k), "A")
    b.add("gi", "D")
    b.add("gf", "D")
    for j in range(H):
        b.add(("mm", j), "D")
    for j in range(H):
        b.add(("hf", j), "A")
    for u in range(2):
        for i in range(NCH):
            b.add(("hi", u, i), "A")
    for j in range(H):
        b.add(("hq", j), "D")
    for j in range(H):
        b.add(("hg", j), "D")
    for j in range(H):
        b.add(("mo", j), "A")
    for j in range(H):
        b.add(("qm", j), "A")
        b.add(("km", j), "A")
    for i in range(NCH):
        b.add(("kt", i), "A")
        b.add(("vm", i), "D")
    b.add("cols", "D")
    b.add("wp", "D")
    for c in range(NCH):
        b.add(("ko", c), "A")
        b.add(("mb", c), "D")
        b.add(("sc", c), "D")
        b.add(("qk", c), "D")
        b.add(("oh", c), "A")
        b.add(("ds", c), "D")
        b.add(("inter", c), "A", 2)
        b.add(("intra", c), "D", 2)
        b.add(("dm", c), "D", 2)
        b.add(("yh", c), "D")
        b.add(("ym", c), "D")
    for m in range(4):
        for j in range(2):
            b.add(("g0", m, j), "A")
        for j in range(2):
            b.add(("b0", m, j), "D")
        for j in range(2):
            b.add(("g1", m, j), "A")
        for j in range(2):
            b.add(("b1", m, j), "D")
    for u in range(4):
        for i in range(NCH):
            b.add(("wo", u, i), "D")
    for k in range(KD):
        b.add(("nT", k), "A")
    for i in range(NCH):
        b.add(("lg", i), "D")
    return b


def weight_chunks():
    out = []
    for name, c0 in (("mm", C_MM), ("hf", C_HF), ("hi", C_HI), ("hq", C_HQ), ("hg", C_HG), ("mo", C_MO)):
        for u in range(2):
            out.append((name, u, c0 + u * WC))
    for m in range(4):
        out += [("g0", m, C_G0 + m * WC), ("b0", m, m * WC), ("g1", m, C_G1 + m * WC), ("b1", m, m * WC)]
    for u in range(4):
        out.append(("wo", u, u * WC))
    return out


def build(nc, ins, out, dbg=None):
    with ExitStack() as top:
        ev = Events(nc, top)

        def dram(name, shape, dt=F32):
            return nc.dram_tensor(name, shape, dt, kind="ExternalOutput" if dbg else "Internal").ap()

        d = {
            "h": dram("h_rows", [ROWS, D]),
            "xn": dram("xn_rows", [ROWS, D]),
            "table": dram("row_table", [TAB, 2], I32),
            "y": dram("y_rows", [TOPK * SEQ, D]),
        }
        lg = top.enter_context(nc.sbuf_tensor("lg", [P, NSPAN * NCH, E], F32))
        ident = top.enter_context(nc.sbuf_tensor("ident", [P, P], F32))
        mixer(nc, ins, d, lg, ident, ev)
        if dbg != "mixer":
            from_routing(nc, ins, d, lg, ident, ev, out)


def mixer(nc, ins, d, lg, ident, ev):
    with ExitStack() as ctx:
        def sb(name, shape, dt=F32):
            return ctx.enter_context(nc.sbuf_tensor(name, shape, dt))

        xrow = sb("xrow", [P, NCH, D])
        region = sb("region", [P, H * NSUB * CH])
        xs = region[:, 0:NCH * D].rearrange("p (i n) -> p i n", i=NCH)
        kdec = region[:, :].rearrange("p (h i s) -> p h i s", h=H, i=NSUB)
        xT = sb("xT", [P, KD, SPAN])
        tmp = sb("tmp", [P, 2, H, SPAN])
        tmp1, kout = tmp[:, 0], tmp[:, 1]
        merged = tmp[:, :, :, :].rearrange("p a h s -> p (a h) s")
        qin, qdec, kh, bh = (sb(n, [P, H, SPAN]) for n in ("qin", "qdec", "kh", "bh"))
        sgh, conv, smo = (sb(n, [P, H, SPAN]) for n in ("sgh", "conv", "smo"))
        mmT = sb("mmT", [P, H, 3 + SPAN])
        qm, km = sb("qm", [QK, H, SPAN]), sb("km", [QK, H, SPAN])
        kt = sb("kt", [P, NCH, H, QK])
        VA = P + 2
        va = sb("va", [P, NCH, H, VA])
        vh = sb("vh", [P, NCH, W])
        sct, wgt, ktok = sb("sct", [P, H, CH]), sb("wgt", [P, H, CH]), sb("ktok", [P, H, CH])
        kw = sb("kw", [P, H, QK])
        nd = sb("nd", [P, H, VA])
        oh, om = sb("oh", [P, H, CH]), sb("om", [P, H, CH])
        ring = sb("ring", [P, NRING, KD, WC])
        sh, sm = sb("sh", [P, H, P]), sb("sm", [QK, H, VA])
        mst = sb("mst", [H, NCH + 1])
        ra, rb, rc, rm, rd = (sb(n, [H, SPAN]) for n in ("ra", "rb", "rc", "rm", "rd"))
        padneg, keep4 = sb("padneg", [H, SPAN]), sb("keep4", [H, SPAN])
        mneg = sb("mneg", [H, NCH])
        dwp = sb("dwp", [H, NCH, H])
        cols, wpb, ebl = sb("cols", [P, NCH, 4, H]), sb("wpb", [QK, NCH, H]), sb("ebl", [P, H, NCH])
        ss = sb("ss", [P, NCH, 4])
        hs = sb("hs", [P, 6, H])
        keep = sb("keep", [P, CH])
        mge = sb("mge", [P, CH])
        mask = sb("mask", [P, CH], I32)
        sel = sb("sel", [H, H, P])
        ones4 = sb("ones4", [H, QK])
        epsc = sb("epsc", [P, 1])
        wif = sb("wif", [P, KD, 2 * H])
        wq, wk, wv = sb("wq", [P, H, QK]), sb("wk", [P, H, QK]), sb("wv", [P, H, P])
        rw, rbias = sb("rw", [P, KD, E]), sb("rbias", [P, E])
        nmix, nffn = sb("nmix", [P, KD]), sb("nffn", [P, D])
        cw, cb = sb("cw", [P, 4, H]), sb("cb", [P, H])
        hgn, mln, skp = sb("hgn", [P, H]), sb("mln", [P, H]), sb("skp", [P, H])
        lb, oml, lgt = sb("lb", [P, H]), sb("oml", [P, H]), sb("lgt", [P, 2, H])
        gbi, gbf = sb("gbi", [H, 1]), sb("gbf", [H, 1])
        ps = ctx.enter_context(nc.psum_tensor("ps", [P, 8, 512], F32))

        gate0, gate1 = kh, bh

        def ml_gated(m):
            return (qin, qdec)[m // 4][:, m % 4]

        J = span_jobs()
        L = weight_chunks()
        at = {(n, u): i for i, (n, u, _) in enumerate(L)}

        def last_use(name, u):
            if name in ("hi", "wo"):
                return name, u, NCH - 1
            return (name, u, 1) if name in ("g0", "b0", "g1", "b1") else (name, 2 * u + 1)

        def slot(n, u):
            return ring[:, at[n, u] % NRING]

        def bank(name, parts=P, w=512):
            return ps[0:parts, J.bank(name), 0:w]

        def two(name, parts=P):
            b = J.bank(name)
            return ps[0:parts, b:b + 2, :].rearrange("p b (a v) -> p b a v", a=2)[:, :, :, 0:P + 1]

        SETUP = ("const", "smallw", "lbs")
        small = [
            (wif[:, :, :], ins["w_in"][:, :, C_IF:C_IF + 2 * H].rearrange("l (k p) n -> p (l k) n", p=P)),
            (wq[:, :, :], ins["ml_wq"].rearrange("l h c d -> c (l h) d")),
            (wk[:, :, :], ins["ml_wk"].rearrange("l h c d -> c (l h) d")),
            (wv[:, :, :], ins["ml_wv"].rearrange("l h c d -> c (l h) d")),
            (rw[:, :, :], ins["router_w"].rearrange("l (k p) e -> p (l k) e", p=P)),
            (rbias[:, :], ins["router_b"].broadcast_to([P, E])),
            (nffn[:, :], ins["norm_ffn"].broadcast_to([P, D])),
            (nmix[:, :], ins["norm_mix"].rearrange("l (k p) -> p (l k)", p=P)),
            (cb[:, :], ins["ml_conv_b"].rearrange("l (h p) -> p (l h)", p=P)),
            (hgn[:, :], ins["hg_norm"].rearrange("l (h p) -> p (l h)", p=P)),
            (mln[:, :], ins["ml_norm"].rearrange("l (h p) -> p (l h)", p=P)),
            (skp[:, :], ins["ml_skip"].rearrange("l (h p) -> p (l h)", p=P)),
            (gbi[:, :], ins["ml_gate_b"][0:1, 0:H].rearrange("l h -> h l")),
            (gbf[:, :], ins["ml_gate_b"][0:1, H:2 * H].rearrange("l h -> h l")),
        ] + [(cw[:, w], ins["ml_conv_w"][0, w].rearrange("(h p) -> p h", p=P)) for w in range(4)] \
          + [(lgt[:, r], ins["hg_lb_logits"][r].rearrange("(h p) -> p h", p=P)) for r in range(2)]

        ENGINES = 5

        def span_end(eng, s):
            eng.nop().then_inc(ev("span_ended"), 1)
            eng.wait_ge(ev("span_cleared"), s + 1)
            eng.nop()

        w_in = ins["w_in"].rearrange("l (k p) n -> p (l k) n", p=P)
        wbh = ins["w_branch_hg"].rearrange("l (k p) n -> p (l k) n", p=P)
        wbm = ins["w_branch_ml"].rearrange("l (k p) n -> p (l k) n", p=P)
        w_out = ins["w_out"].rearrange("l (k p) n -> p (l k) n", p=P)
        xin = ins["rows"].rearrange("(i p) n -> p i n", p=P)
        hrows = d["h"].rearrange("(i p) n -> p i n", p=P)
        nrows = d["xn"].rearrange("(i p) n -> p i n", p=P)

        block = ctx.enter_context(nc.Block())

        @block.gpsimd
        def _(pool):
            g = nc.gpsimd
            n = [0]

            def link(ins_):
                n[0] += 1
                ins_.then_inc(ev("pool_const"), 1)
                pool.wait_ge(ev("pool_const"), n[0])

            link(g.memset(ident[:], 0.0))
            link(g.affine_select(out=ident[:], in_=ident[:], compare_op=ALU.not_equal, fill=1.0, base=0,
                                 pattern=[[-1, P]], channel_multiplier=1))
            link(g.memset(mge[:], 0.0))
            link(g.affine_select(out=mge[:], in_=mge[:], compare_op=ALU.is_ge, fill=NEG, base=0,
                                 pattern=[[1, CH]], channel_multiplier=-1))
            link(g.memset(mask[:], 1))
            link(g.affine_select(out=mask[:], in_=mask[:], compare_op=ALU.is_ge, fill=0.0, base=0,
                                 pattern=[[1, CH]], channel_multiplier=-1))
            link(g.memset(keep[:], 1.0))
            link(g.memset(keep[:, 0:1], 0.0))
            link(g.memset(keep4[:], 1.0))
            for c in range(NCH):
                link(g.memset(keep4[:, c * CH:c * CH + 1], 0.0))
            link(g.memset(padneg[:], 0.0))
            link(g.memset(padneg[:, 0:PAD], NEG))
            link(g.memset(sel[:], 0.0))
            link(g.affine_select(out=sel[:], in_=sel[:], compare_op=ALU.not_equal, fill=-1.0, base=0,
                                 pattern=[[-1, H], [0, P]], channel_multiplier=1))
            link(g.memset(ones4[:], 1.0))
            link(g.memset(epsc[:], EPS))
            link(g.memset(sh[:], 0.0))
            link(g.memset(sm[:], 0.0))
            link(g.memset(mst[:], 0.0))
            link(g.memset(mmT[:], 0.0))
            link(g.memset(va[:], 1.0))
            g.memset(sct[:], 0.0).then_inc(ev("const"), 1)
            with pool.Fori(0, NSPAN) as s:
                pool.wait_ge(ev("ps_ready"), J.ready(("xT", KD - 1)))
                pool.wait_ge(ev("bh_ready"), 1)
                g.memset(region[:], 0.0).then_inc(ev("kdec_zero"), 1)
                pool.wait_ge(ev("kdec_zero"), 1)
                for c in range(NCH):
                    if c:
                        pool.wait_ge(ev("ps_ready"), J.ready(("sc", c - 1)))
                    for i in range(NSUB):
                        n_s = (i + 1) * SUB
                        ref = bh[:, :, c * CH + i * SUB + SUB // 2 - 1:c * CH + i * SUB + SUB // 2]
                        g.tensor_tensor(kdec[:, :, i, 0:n_s], ref.broadcast_to([P, H, n_s]),
                                        bh[:, :, c * CH:c * CH + n_s], ALU.subtract).then_inc(ev("kexp_arg"), 1)
                for m in range(8):
                    pool.wait_ge(ev("branches"), m + 1)
                    g.tensor_tensor(merged[:, m], merged[:, m], ml_gated(m), ALU.add).then_inc(ev("merged"), 1)
                span_end(pool, s)

        @block.vector
        def _(dve):
            v = nc.vector
            seq = [0]

            def link(ins_, *also):
                seq[0] += 1
                ins_.then_inc(ev("dve_step"), 1)
                dve.wait_ge(ev("dve_step"), seq[0])
                for name in also:
                    dve.sem_inc(ev(name), 1)

            def freed(name):
                assert J.jobs[name][3] == "D"
                dve.sem_inc(ev("D_freed"), 1)

            def ready(name):
                dve.wait_ge(ev("ps_ready"), J.ready(name))

            dve.wait_ge(ev("const"), 1)
            dve.wait_ge(ev("smallw"), 16 * len(small))
            v.tensor_tensor(lb[:], lgt[:, 1], lgt[:, 0], ALU.subtract).then_inc(ev("lbd"), 1)
            dve.wait_ge(ev("lbs"), 1)
            v.tensor_scalar(oml[:], lb[:], -1.0, 1.0, ALU.mult, ALU.add).then_inc(ev("oml"), 1)
            dve.wait_ge(ev("oml"), 1)
            with dve.Fori(0, NSPAN) as s:
                for i in range(NCH):
                    dve.wait_ge(ev("ss1"), i + 1)
                    link(v.reciprocal(ss[:, i, 1:2], ss[:, i, 0:1]))
                    link(v.tensor_scalar(xs[:, i], xrow[:, i], ss[:, i, 1:2], None, ALU.mult), "xs")
                ready("gi")
                link(v.scalar_tensor_tensor(rc[:], bank("gi", H, SPAN), gbi[:, 0:1], padneg[:], ALU.add, ALU.add))
                freed("gi")
                ready("gf")
                link(v.tensor_scalar(ra[:], bank("gf", H, SPAN), gbf[:, 0:1], None, ALU.add), "gf_sum")
                freed("gf")
                link(v.tensor_copy(mmT[:, :, 0:3], mmT[:, :, SPAN:SPAN + 3]))
                for j in range(H):
                    ready(("mm", j))
                    link(v.tensor_copy(mmT[:, j, 3:3 + SPAN], bank(("mm", j), P, SPAN)), "mmT")
                    freed(("mm", j))
                for j in range(H):
                    link(v.tensor_scalar(conv[:, j], mmT[:, j, 0:SPAN], cw[:, 0, j:j + 1], cb[:, j:j + 1],
                                         ALU.mult, ALU.add))
                    for w in range(1, 4):
                        link(v.scalar_tensor_tensor(conv[:, j], mmT[:, j, w:w + SPAN], cw[:, w, j:j + 1],
                                                    conv[:, j], ALU.mult, ALU.add))
                    dve.sem_inc(ev("conv_lin"), 1)
                for j in range(H):
                    dve.wait_ge(ev("hf_sig"), j + 1)
                    link(v.tensor_scalar(tmp1[:, j], tmp1[:, j], oml[:, j:j + 1], lb[:, j:j + 1], ALU.mult, ALU.add))
                dve.sem_inc(ev("f_ready"), 1)
                link(v.tensor_scalar(kh[:], tmp1, -1.0, 1.0, ALU.mult, ALU.add))
                for j in range(H):
                    dve.wait_ge(ev("conv_sig"), j + 1)
                    link(v.tensor_tensor(conv[:, j], conv[:, j], smo[:, j], ALU.mult), "conv_ready")
                for j in range(H):
                    dve.wait_ge(ev("hq_sig"), j + 1)
                    link(v.tensor_tensor(qin[:, j], bank(("hq", j), P, SPAN), qin[:, j], ALU.mult))
                    freed(("hq", j))
                for j in range(H):
                    dve.wait_ge(ev("hg_sig"), j + 1)
                    link(v.tensor_tensor(sgh[:, j], bank(("hg", j), P, SPAN), sgh[:, j], ALU.mult))
                    freed(("hg", j))
                dve.wait_ge(ev("logf"), 1)
                for j in range(H):
                    for c in range(NCH):
                        cs = slice(c * CH, (c + 1) * CH)
                        last = v.tensor_tensor_scan(bh[:, j, cs], keep[:], kout[:, j, cs], 0.0, ALU.mult, ALU.add)
                link(last, "bh_ready")
                b4 = bh[:].rearrange("p h (n s) -> p (h n) s", s=SUB)
                t4 = tmp1.rearrange("p h (n s) -> p (h n) s", s=SUB)
                mid = b4[:, :, SUB // 2 - 1:SUB // 2].broadcast_to([P, H * NCH * NSUB, SUB])
                link(v.tensor_tensor(t4, b4, mid, ALU.subtract), "qexp_arg")
                b3 = bh[:].rearrange("p h (n s) -> p (h n) s", s=CH)
                k3 = kout.rearrange("p h (n s) -> p (h n) s", s=CH)
                lastb = b3[:, :, CH - 1:CH].broadcast_to([P, H * NCH, CH])
                link(v.tensor_tensor(k3, lastb, b3, ALU.subtract), "kout_arg")
                dve.wait_ge(ev("qexp"), 1)
                link(v.scalar_tensor_tensor(qdec[:], tmp1, BIG, qin[:], ALU.min, ALU.mult), "qdec")
                dve.wait_ge(ev("qin_exp"), 1)
                link(v.tensor_tensor(qin[:], qin[:], tmp1, ALU.mult), "qin")
                dve.wait_ge(ev("kout_exp"), 1)
                link(v.tensor_tensor(kout, kout, kh[:], ALU.mult), "kout")
                dve.wait_ge(ev("lf_log"), 1)
                link(v.scalar_tensor_tensor(ra[:], ra[:], 0.0, rb[:], ALU.min, ALU.subtract))
                link(v.tensor_tensor_scan(rb[:], keep4[:], ra[:], 0.0, ALU.mult, ALU.add))
                link(v.tensor_tensor(rc[:], rc[:], rb[:], ALU.subtract))
                link(v.tensor_copy(mst[:, 0:1], mst[:, NCH:NCH + 1]))
                for c in range(NCH):
                    cs = slice(c * CH, (c + 1) * CH)
                    end = slice((c + 1) * CH - 1, (c + 1) * CH)
                    link(v.tensor_tensor_scan(rm[:, cs], rc[:, cs], rc[:, cs], mst[:, c:c + 1], ALU.max, ALU.max))
                    link(v.tensor_tensor(mst[:, c + 1:c + 2], rb[:, end], rm[:, end], ALU.add))
                    link(v.tensor_scalar(mneg[:, c:c + 1], rm[:, end], -1.0, None, ALU.mult))
                link(v.tensor_tensor(rb[:], rb[:], rm[:], ALU.add), "rows")
                link(v.memset(padneg[:], 0.0))
                dve.wait_ge(ev("row_exps"), 1)
                for c in range(NCH):
                    end = slice((c + 1) * CH - 1, (c + 1) * CH)
                    link(v.tensor_scalar(dwp[:, c], ident[0:H, 0:H], ra[:, end], None, ALU.mult))
                dve.sem_inc(ev("dwp"), 1)
                for i in range(NCH):
                    ready(("vm", i))
                    link(v.tensor_copy(va[:, i, :, 0:P], bank(("vm", i)).rearrange("p (h v) -> p h v", h=H)), "vm")
                    freed(("vm", i))
                ready("cols")
                link(v.tensor_copy(cols[:].rearrange("p c k h -> p (c k h)"), bank("cols", P, NCH * 16)), "cols")
                freed("cols")
                ready("wp")
                link(v.tensor_copy(wpb[:].rearrange("p c h -> p (c h)"), bank("wp", QK, NCH * H)))
                freed("wp")
                for j in range(H):
                    link(v.tensor_scalar(conv[:, j], conv[:, j], skp[:, j:j + 1], None, ALU.mult))

                for c in range(NCH):
                    cs = slice(c * CH, (c + 1) * CH)
                    for i in range(NSUB):
                        n_s = (i + 1) * SUB
                        dve.wait_ge(ev("kexp"), c * NSUB + i + 1)
                        link(v.scalar_tensor_tensor(kdec[:, :, i, 0:n_s], kdec[:, :, i, 0:n_s], BIG,
                                                    kh[:, :, c * CH:c * CH + n_s], ALU.min, ALU.mult))
                    dve.sem_inc(ev("kdec"), 1)
                    ready(("mb", c))
                    if c:
                        dve.wait_ge(ev("ps_ready"), J.ready(("intra", c - 1)))
                    for h in range(H):
                        link(v.scalar_tensor_tensor(wgt[:, h], bank(("mb", c)).rearrange("p (h t) -> p h t", h=H)[:, h],
                                                    cols[:, c, 0, h:h + 1], mge[:], ALU.add, ALU.min))
                    dve.sem_inc(ev("wexp_arg"), 1)
                    freed(("mb", c))
                    link(v.tensor_tensor(kw[:], kt[:, c], cols[:, c, 3].rearrange("p (h o) -> p h o", o=1)
                                         .broadcast_to([P, H, QK]), ALU.mult), "kw")
                    ready(("sc", c))
                    link(v.copy_predicated(sct[:], mask[:].rearrange("p (o t) -> p o t", o=1).broadcast_to([P, H, CH]),
                                           bank(("sc", c)).rearrange("p (h t) -> p h t", h=H)), "sct")
                    freed(("sc", c))
                    ready(("qk", c))
                    dve.wait_ge(ev("wexp"), c + 1)
                    link(v.tensor_tensor(wgt[:], wgt[:], bank(("qk", c)).rearrange("p (h t) -> p h t", h=H), ALU.mult),
                         "wgt")
                    freed(("qk", c))
                    ready(("ds", c))
                    for h in range(H):
                        link(v.scalar_tensor_tensor(sh[:, h], sh[:, h], ebl[:, h, c:c + 1],
                                                    bank(("ds", c)).rearrange("p (h t) -> p h t", h=H)[:, h],
                                                    ALU.mult, ALU.add))
                    dve.sem_inc(ev("sh_new"), 1)
                    freed(("ds", c))
                    dve.wait_ge(ev("inter_sc"), c + 1)
                    ready(("intra", c))
                    nd4 = nd[:].rearrange("p (b a) v -> p b a v", a=2)[:, :, :, 0:P + 1]
                    for b2 in range(2):
                        link(v.tensor_tensor(nd4[:, b2], nd4[:, b2], two(("intra", c))[:, b2], ALU.add))
                    freed(("intra", c))
                    ready(("dm", c))
                    for h in range(H):
                        link(v.scalar_tensor_tensor(sm[:, h, 0:P + 1], sm[:, h, 0:P + 1], wpb[:, c, h:h + 1],
                                                    two(("dm", c), QK)[:, h // 2, h % 2], ALU.mult, ALU.add))
                    dve.sem_inc(ev("sm_new"), 1)
                    freed(("dm", c))
                    den = nd[:, :, P:P + 1].rearrange("p h o -> p (h o)")
                    link(v.scalar_tensor_tensor(hs[:, 0], den, -1.0, den, ALU.mult, ALU.max))
                    link(v.tensor_tensor(hs[:, 0], hs[:, 0], cols[:, c, 2], ALU.max))
                    link(v.reciprocal(hs[:, 0], hs[:, 0]))
                    if c:
                        dve.wait_ge(ev("ps_ready"), J.ready(("ym", c - 1)))
                    link(v.tensor_tensor(om[:], nd[:, :, 0:P], hs[:, 0].rearrange("p (h o) -> p h o", o=1)
                                         .broadcast_to([P, H, P]), ALU.mult), "om")
                    dve.wait_ge(ev("o_rms"), 2 * c + 1)
                    link(v.tensor_tensor(oh[:], oh[:], hs[:, 2].rearrange("p (h o) -> p h o", o=1)
                                         .broadcast_to([P, H, P]), ALU.mult), "oh_n")
                    dve.wait_ge(ev("o_rms"), 2 * c + 2)
                    link(v.tensor_tensor(om[:], om[:], hs[:, 4].rearrange("p (h o) -> p h o", o=1)
                                         .broadcast_to([P, H, P]), ALU.mult), "om_n")
                    ready(("yh", c))
                    for h in range(H):
                        link(v.scalar_tensor_tensor(sgh[:, h, cs], bank(("yh", c))[:, h * P:(h + 1) * P],
                                                    hgn[:, h:h + 1], sgh[:, h, cs], ALU.mult, ALU.mult))
                    freed(("yh", c))
                    ready(("ym", c))
                    for h in range(H):
                        link(v.scalar_tensor_tensor(conv[:, h, cs], bank(("ym", c))[:, h * P:(h + 1) * P],
                                                    mln[:, h:h + 1], conv[:, h, cs], ALU.mult, ALU.add))
                    freed(("ym", c))
                    link(v.tensor_tensor(smo[:, :, cs], conv[:, :, cs], smo[:, :, cs], ALU.mult), "y_ready")

                for m in range(4):
                    for j in range(2):
                        t = 2 * m + j
                        ready(("b0", m, j))
                        dve.wait_ge(ev("gates"), 4 * m + j + 1)
                        link(v.tensor_tensor(merged[:, t], bank(("b0", m, j), P, SPAN), gate0[:, t % 4], ALU.mult))
                        freed(("b0", m, j))
                    for j in range(2):
                        t = 2 * m + j
                        ready(("b1", m, j))
                        dve.wait_ge(ev("gates"), 4 * m + 2 + j + 1)
                        link(v.tensor_tensor(ml_gated(t), bank(("b1", m, j), P, SPAN), gate1[:, t % 4], ALU.mult),
                             "branches")
                        freed(("b1", m, j))
                for u in range(4):
                    for i in range(NCH):
                        us = slice(u * WC, (u + 1) * WC)
                        ready(("wo", u, i))
                        link(v.tensor_tensor(xs[:, i, us], bank(("wo", u, i), P, WC), xrow[:, i, us], ALU.add))
                        freed(("wo", u, i))
                dve.sem_inc(ev("h_ready"), 1)
                for i in range(NCH):
                    dve.wait_ge(ev("ss2"), i + 1)
                    link(v.reciprocal(ss[:, i, 3:4], ss[:, i, 2:3]))
                    link(v.scalar_tensor_tensor(xrow[:, i], xs[:, i], ss[:, i, 3:4], nffn[:], ALU.mult, ALU.mult),
                         "xn_ready")
                for i in range(NCH):
                    ready(("lg", i))
                    link(v.tensor_tensor(lg[:, bass.ds(s * NCH + i, 1), :].rearrange("p o e -> p (o e)"),
                                         bank(("lg", i), P, E), rbias[:], ALU.add))
                    freed(("lg", i))
                span_end(dve, s)

        @block.scalar
        def _(act):
            a = nc.scalar
            seq = [0]

            def link(ins_, *also):
                seq[0] += 1
                ins_.then_inc(ev("act_step"), 1)
                act.wait_ge(ev("act_step"), seq[0])
                for name in also:
                    act.sem_inc(ev(name), 1)

            def freed(name):
                assert J.jobs[name][3] == "A"
                act.sem_inc(ev("A_freed"), 1)

            def ready(name):
                act.wait_ge(ev("ps_ready"), J.ready(name))

            act.wait_ge(ev("lbd"), 1)
            a.activation(lb[:], lb[:], ACT.Sigmoid, scale=-1.0).then_inc(ev("lbs"), 1)
            with act.Fori(0, NSPAN) as s:
                act.wait_ge(ev("x_loaded"), 16)
                for i in range(NCH):
                    link(a.activation(xs[:, i], xrow[:, i], ACT.Square, accum_out=ss[:, i, 0:1]))
                for i in range(NCH):
                    link(a.activation(ss[:, i, 0:1], ss[:, i, 0:1], ACT.Sqrt, scale=1.0 / D, bias=epsc[:, 0:1]), "ss1")
                for k in range(KD):
                    ready(("xT", k))
                    link(a.activation(xT[:, k], bank(("xT", k), P, SPAN), ACT.Copy, scale=nmix[:, k:k + 1]), "xT")
                    freed(("xT", k))
                for j in range(H):
                    ready(("hf", j))
                    link(a.activation(tmp1[:, j], bank(("hf", j), P, SPAN), ACT.Sigmoid), "hf_sig")
                    freed(("hf", j))
                for j in range(H):
                    act.wait_ge(ev("conv_lin"), j + 1)
                    link(a.activation(smo[:, j], conv[:, j], ACT.Sigmoid), "conv_sig")
                for u in range(2):
                    for i in range(NCH):
                        ready(("hi", u, i))
                        link(a.copy(vh[:, i, u * WC:(u + 1) * WC], bank(("hi", u, i), P, WC)), "vh")
                        freed(("hi", u, i))
                for j in range(H):
                    ready(("hq", j))
                    link(a.activation(qin[:, j], bank(("hq", j), P, SPAN), ACT.Sigmoid), "hq_sig")
                for j in range(H):
                    ready(("hg", j))
                    link(a.activation(sgh[:, j], bank(("hg", j), P, SPAN), ACT.Sigmoid), "hg_sig")
                act.wait_ge(ev("conv_ready"), H)
                for j in range(H):
                    ready(("mo", j))
                    link(a.activation(smo[:, j], bank(("mo", j), P, SPAN), ACT.Sigmoid))
                    freed(("mo", j))
                act.wait_ge(ev("f_ready"), 1)
                link(a.activation(kout, tmp1, ACT.Ln), "logf")
                act.wait_ge(ev("gf_sum"), 1)
                link(a.activation(rb[:], ra[:], ACT.Abs))
                link(a.activation(rb[:], rb[:], ACT.Exp, scale=-1.0))
                link(a.activation(rb[:], rb[:], ACT.Ln, bias=1.0), "lf_log")
                for j in range(H):
                    ready(("qm", j))
                    link(a.mul(qm[:, j], bank(("qm", j), QK, SPAN), QK ** -0.5))
                    freed(("qm", j))
                    ready(("km", j))
                    link(a.copy(km[:, j], bank(("km", j), QK, SPAN)), "qkm")
                    freed(("km", j))
                act.wait_ge(ev("qexp_arg"), 1)
                link(a.activation(tmp1, tmp1, ACT.Exp), "qexp")
                act.wait_ge(ev("kout_arg"), 1)
                link(a.activation(kout, kout, ACT.Exp), "kout_exp")
                act.wait_ge(ev("qdec"), 1)
                link(a.activation(tmp1, bh[:], ACT.Exp), "qin_exp")
                link(a.activation(ebl[:].rearrange("p h c -> p (h c)"),
                                  bh[:].rearrange("p h (n s) -> p (h n) s", s=CH)[:, :, CH - 1:CH]
                                  .rearrange("p n o -> p (n o)"), ACT.Exp))
                for i in range(NCH):
                    ready(("kt", i))
                    link(a.copy(kt[:, i].rearrange("p h d -> p (h d)"), bank(("kt", i), P, H * QK)), "kt")
                    freed(("kt", i))
                act.wait_ge(ev("rows"), 1)
                for c in range(NCH):
                    cs = slice(c * CH, (c + 1) * CH)
                    a.activation(ra[:, cs], rm[:, cs], ACT.Exp, scale=-1.0, bias=mst[:, c:c + 1])
                    a.activation(rd[:, cs], rc[:, cs], ACT.Exp, bias=mneg[:, c:c + 1])
                link(a.activation(rb[:], rb[:], ACT.Exp, scale=-1.0), "row_exps")

                for c in range(NCH):
                    for i in range(NSUB):
                        n_s = (i + 1) * SUB
                        act.wait_ge(ev("kexp_arg"), c * NSUB + i + 1)
                        link(a.activation(kdec[:, :, i, 0:n_s], kdec[:, :, i, 0:n_s], ACT.Exp), "kexp")
                    ready(("ko", c))
                    link(a.copy(ktok[:].rearrange("p h d -> p (h d)"), bank(("ko", c))), "ktok")
                    freed(("ko", c))
                    act.wait_ge(ev("wexp_arg"), c + 1)
                    link(a.activation(wgt[:], wgt[:], ACT.Exp), "wexp")
                    ready(("oh", c))
                    if c:
                        act.wait_ge(ev("ps_ready"), J.ready(("yh", c - 1)))
                    link(a.copy(oh[:].rearrange("p h d -> p (h d)"), bank(("oh", c))))
                    freed(("oh", c))
                    for h in range(H):
                        a.activation(tmp1[:, h, 0:CH], oh[:, h], ACT.Square, accum_out=hs[:, 1, h:h + 1])
                    link(a.activation(epsc[:, 0:1], epsc[:, 0:1], ACT.Copy))
                    link(a.activation(hs[:, 1], hs[:, 1], ACT.Ln, scale=1.0 / P, bias=epsc[:, 0:1]))
                    link(a.activation(hs[:, 2], hs[:, 1], ACT.Exp, scale=-0.5), "o_rms")
                    ready(("inter", c))
                    for h in range(H):
                        last = a.activation(nd[:, h, 0:P + 1], two(("inter", c))[:, h // 2, h % 2], ACT.Copy,
                                            scale=cols[:, c, 1, h:h + 1])
                    link(last, "inter_sc")
                    freed(("inter", c))
                    act.wait_ge(ev("om"), c + 1)
                    for h in range(H):
                        a.activation(tmp1[:, h, 0:CH], om[:, h], ACT.Square, accum_out=hs[:, 3, h:h + 1])
                    link(a.activation(epsc[:, 0:1], epsc[:, 0:1], ACT.Copy))
                    link(a.activation(hs[:, 3], hs[:, 3], ACT.Ln, scale=1.0 / P, bias=epsc[:, 0:1]))
                    link(a.activation(hs[:, 4], hs[:, 3], ACT.Exp, scale=-0.5), "o_rms")
                act.wait_ge(ev("y_ready"), NCH)
                for m in range(4):
                    if m >= 2:
                        act.wait_ge(ev("branches"), 2 * (m - 1))
                    for w, g in (("g0", gate0), ("g1", gate1)):
                        for j in range(2):
                            ready((w, m, j))
                            link(a.activation(g[:, (2 * m + j) % 4], bank((w, m, j), P, SPAN), ACT.Sigmoid), "gates")
                            freed((w, m, j))
                act.wait_ge(ev("h_ready"), 1)
                act.wait_ge(ev("merged"), 8)
                for i in range(NCH):
                    link(a.activation(merged[:, 0:8].rearrange("p m s -> p (m s)")[:, 0:D], xs[:, i], ACT.Square,
                                      accum_out=ss[:, i, 2:3]))
                for i in range(NCH):
                    link(a.activation(ss[:, i, 2:3], ss[:, i, 2:3], ACT.Sqrt, scale=1.0 / D, bias=epsc[:, 0:1]), "ss2")
                for k in range(KD):
                    ready(("nT", k))
                    link(a.copy(xT[:, k], bank(("nT", k), P, SPAN)), "nT")
                    freed(("nT", k))
                span_end(act, s)

        @block.tensor
        def _(pe):
            t = nc.tensor

            def begin(name):
                for e, c in J.jobs[name][2].items():
                    pe.wait_ge(ev(f"{e}_freed"), c)

            def done(last):
                last.then_inc(ev("ps_ready"), 1)

            def weights(name, u):
                n = at[name, u]
                pe.wait_ge(ev(f"w_loaded{n % NRING}"), 16 * (n // NRING + 1))

            pe.wait_ge(ev("const"), 1)
            pe.wait_ge(ev("smallw"), 16 * len(small))
            with pe.Fori(0, NSPAN) as s:
                pe.wait_ge(ev("xs"), NCH)
                for k in range(KD):
                    begin(("xT", k))
                    for i in range(NCH):
                        last = t.transpose(bank(("xT", k))[:, i * P:(i + 1) * P], xs[:, i, k * P:(k + 1) * P], ident[:])
                    done(last)
                pe.wait_ge(ev("xT"), KD)
                for name, o in (("gi", 0), ("gf", H)):
                    begin(name)
                    for k in range(KD):
                        last = t.matmul(bank(name, H, SPAN), wif[:, k, o:o + H], xT[:, k], start=k == 0, stop=k == KD - 1)
                    done(last)

                def project(name, u, jobs, kt_, rhs):
                    weights(name, u)
                    for j in range(2):
                        begin(jobs[j])
                        for k in range(kt_):
                            last = t.matmul(bank(jobs[j], P, SPAN), slot(name, u)[:, k, j * P:(j + 1) * P], rhs[:, k],
                                            start=k == 0, stop=k == kt_ - 1)
                        done(last)

                def rows(name, u, jobs, lhs):
                    weights(name, u)
                    for i in range(NCH):
                        begin(jobs[i])
                        for k in range(KD):
                            last = t.matmul(bank(jobs[i], P, WC), lhs[:, k, i * P:(i + 1) * P], slot(name, u)[:, k],
                                            start=k == 0, stop=k == KD - 1)
                        done(last)

                for name in ("mm", "hf", "hi", "hq", "hg", "mo"):
                    for u in range(2):
                        if name == "hi":
                            rows(name, u, [("hi", u, i) for i in range(NCH)], xT)
                        else:
                            project(name, u, [(name, 2 * u + j) for j in range(2)], KD, xT)
                pe.wait_ge(ev("conv_ready"), H)
                for h in range(H):
                    for name, w in (("qm", wq), ("km", wk)):
                        begin((name, h))
                        done(t.matmul(bank((name, h), QK, SPAN), w[:, h], conv[:, h], start=True, stop=True))
                for i in range(NCH):
                    begin(("kt", i))
                    for h in range(H):
                        last = t.matmul(bank(("kt", i))[:, h * QK:(h + 1) * QK], conv[:, h, i * P:(i + 1) * P], wk[:, h],
                                        start=True, stop=True)
                    done(last)
                    begin(("vm", i))
                    for h in range(H):
                        last = t.matmul(bank(("vm", i))[:, h * P:(h + 1) * P], mmT[:, h, 3 + i * P:3 + (i + 1) * P],
                                        wv[:, h], start=True, stop=True)
                    done(last)
                pe.wait_ge(ev("row_exps"), 1)
                begin("cols")
                for c in range(NCH):
                    for n, r in enumerate((rc, ra, rb, rd)):
                        o = (c * 4 + n) * H
                        last = t.transpose(bank("cols")[:, o:o + H], r[:, c * CH:(c + 1) * CH], ident[0:H, 0:H])
                done(last)
                begin("wp")
                pe.wait_ge(ev("dwp"), 1)
                done(t.matmul(bank("wp", QK, NCH * H), ones4[:], dwp[:].rearrange("p c h -> p (c h)"),
                              start=True, stop=True))
                pe.wait_ge(ev("kout"), 1)
                pe.wait_ge(ev("qin"), 1)
                pe.wait_ge(ev("vh"), 2 * NCH)
                pe.wait_ge(ev("qkm"), H)
                pe.wait_ge(ev("vm"), NCH)
                for c in range(NCH):
                    cs = slice(c * CH, (c + 1) * CH)
                    begin(("ko", c))
                    for h in range(H):
                        last = t.transpose(bank(("ko", c))[:, h * P:(h + 1) * P], kout[:, h, cs], ident[:])
                    done(last)
                    begin(("mb", c))
                    for h in range(H):
                        last = t.matmul(bank(("mb", c))[:, h * P:(h + 1) * P], sel[:, h], rm[:, cs], start=True, stop=True)
                    done(last)
                    begin(("sc", c))
                    pe.wait_ge(ev("kdec"), c + 1)
                    for h in range(H):
                        for i in range(NSUB):
                            last = t.matmul(bank(("sc", c))[:, h * P + i * SUB:h * P + (i + 1) * SUB], kdec[:, h, i],
                                            qdec[:, h, c * CH + i * SUB:c * CH + (i + 1) * SUB], start=True, stop=True)
                    done(last)
                    begin(("qk", c))
                    for h in range(H):
                        last = t.matmul(bank(("qk", c))[:, h * P:(h + 1) * P], km[:, h, cs], qm[:, h, cs],
                                        start=True, stop=True)
                    done(last)
                    begin(("oh", c))
                    if c:
                        pe.wait_ge(ev("sh_new"), c)
                    pe.wait_ge(ev("sct"), c + 1)
                    for h in range(H):
                        hv = slice(h * P, (h + 1) * P)
                        t.matmul(bank(("oh", c))[:, hv], qin[:, h, cs], sh[:, h], start=True, stop=False)
                        last = t.matmul(bank(("oh", c))[:, hv], sct[:, h], vh[:, c, hv], start=False, stop=True)
                    done(last)
                    begin(("ds", c))
                    pe.wait_ge(ev("ktok"), c + 1)
                    for h in range(H):
                        hv = slice(h * P, (h + 1) * P)
                        last = t.matmul(bank(("ds", c))[:, hv], ktok[:, h], vh[:, c, hv], start=True, stop=True)
                    done(last)
                    begin(("inter", c))
                    if c:
                        pe.wait_ge(ev("sm_new"), c)
                    for h in range(H):
                        last = t.matmul(two(("inter", c))[:, h // 2, h % 2], qm[:, h, cs], sm[:, h, 0:P + 1],
                                        start=True, stop=True)
                    done(last)
                    begin(("intra", c))
                    pe.wait_ge(ev("wgt"), c + 1)
                    for h in range(H):
                        last = t.matmul(two(("intra", c))[:, h // 2, h % 2], wgt[:, h], va[:, c, h, 0:P + 1],
                                        start=True, stop=True)
                    done(last)
                    begin(("dm", c))
                    pe.wait_ge(ev("kw"), c + 1)
                    for h in range(H):
                        last = t.matmul(two(("dm", c), QK)[:, h // 2, h % 2], kw[:, h], va[:, c, h, 0:P + 1],
                                        start=True, stop=True)
                    done(last)
                    begin(("yh", c))
                    pe.wait_ge(ev("oh_n"), c + 1)
                    for h in range(H):
                        last = t.transpose(bank(("yh", c))[:, h * P:(h + 1) * P], oh[:, h], ident[:])
                    done(last)
                    begin(("ym", c))
                    pe.wait_ge(ev("om_n"), c + 1)
                    for h in range(H):
                        last = t.transpose(bank(("ym", c))[:, h * P:(h + 1) * P], om[:, h], ident[:])
                    done(last)
                pe.wait_ge(ev("y_ready"), NCH)
                for m in range(4):
                    project("g0", m, [("g0", m, j) for j in range(2)], KD, xT)
                    project("b0", m, [("b0", m, j) for j in range(2)], H, sgh)
                    project("g1", m, [("g1", m, j) for j in range(2)], KD, xT)
                    project("b1", m, [("b1", m, j) for j in range(2)], H, smo)
                pe.wait_ge(ev("merged"), 8)
                for u in range(4):
                    rows("wo", u, [("wo", u, i) for i in range(NCH)], merged)
                pe.wait_ge(ev("xn_ready"), NCH)
                for k in range(KD):
                    begin(("nT", k))
                    for i in range(NCH):
                        last = t.transpose(bank(("nT", k))[:, i * P:(i + 1) * P], xrow[:, i, k * P:(k + 1) * P], ident[:])
                    done(last)
                pe.wait_ge(ev("nT"), KD)
                for i in range(NCH):
                    begin(("lg", i))
                    for k in range(KD):
                        last = t.matmul(bank(("lg", i), P, E), xT[:, k, i * P:(i + 1) * P], rw[:, k],
                                        start=k == 0, stop=k == KD - 1)
                    done(last)
                span_end(pe, s)

        @block.sync
        def _(sp):
            for dst, src in small:
                sp.dma_start(dst, src, allow_slow_non_contiguous=True).then_inc(ev("smallw"), 16)
            setup = {"const", "smallw", "lbs", "lbd", "oml", "pool_const", "span_ended", "span_cleared", "span_clearing"}
            with sp.Fori(0, NSPAN) as s:
                sp.dma_start(xrow[:], xin[:, bass.ds(s * NCH, NCH), :]).then_inc(ev("x_loaded"), 16)
                for n, (name, u, c0) in enumerate(L):
                    src = {"b0": wbh, "b1": wbm, "wo": w_out}.get(name, w_in)
                    kt_ = H if name in ("b0", "b1") else KD
                    if n >= NRING:
                        sp.wait_ge(ev("ps_ready"), J.ready(last_use(*L[n - NRING][0:2])))
                    sp.dma_start(ring[:, n % NRING, 0:kt_, :], src[:, :, c0:c0 + WC]).then_inc(ev(f"w_loaded{n % NRING}"), 16)
                sp.wait_ge(ev("h_ready"), 1)
                sp.dma_start(hrows[:, bass.ds(s * NCH, NCH), :], xs).then_inc(ev("rows_stored"), 16)
                sp.wait_ge(ev("xn_ready"), NCH)
                sp.dma_start(nrows[:, bass.ds(s * NCH, NCH), :], xrow[:]).then_inc(ev("rows_stored"), 16)
                sp.wait_ge(ev("rows_stored"), 32)
                sp.nop().then_inc(ev("span_ended"), 1)
                sp.wait_ge(ev("span_ended"), ENGINES * (s + 1))
                sp.nop().then_inc(ev("span_clearing"), 1)
                for name in [m for m in ev.made if m not in setup]:
                    sp.sem_clear(ev(name))
                sp.nop().then_inc(ev("span_cleared"), 1)


def from_routing(nc, ins, d, lg, ident, ev, out):
    with ExitStack() as ctx:
        def sb(name, shape, dt=F32):
            return ctx.enter_context(nc.sbuf_tensor(name, shape, dt))

        dest = sb("dest", [P, TOPK, NT], I32)
        gw = sb("gw", [P, NT, TOPK])
        ntail = sb("ntail", [1, E], I32)
        biasT = sb("biasT", [P, 24, E])
        eps2 = sb("eps2", [P, 1])
        routing(nc, ins, d, lg, ident, ev, dest, gw, ntail, biasT, eps2)
        experts(nc, ins, d, ident, ev, ntail, biasT)
        combine(nc, ins, d, ev, dest, gw, eps2, out)


def routing(nc, ins, d, lg, ident, ev, dest, gw, ntail, biasT, eps2):
    with ExitStack() as ctx:
        def sb(name, shape, dt=F32):
            return ctx.enter_context(nc.sbuf_tensor(name, shape, dt))

        top, topi, topf = sb("top", [P, NT, 8]), sb("topi", [P, NT, 8], U32), sb("topf", [P, NT, 8])
        iota_i, iota = sb("iota_i", [P, E], I32), sb("iota", [P, E])
        ebase = sb("ebase", [P, E])
        hot = sb("hot", [P, TOPK, NT, E])
        chosen = sb("chosen", [P, NT, E])
        before = sb("before", [P, NT + 1, E])
        prod = sb("prod", [P, NT, E])
        destf = sb("destf", [P, TOPK, NT])
        wsum = sb("wsum", [P, NT, 1])
        tri, ones = sb("tri", [P, P]), sb("ones", [P, P])
        rowid = sb("rowid", [P, TOPK, NT, 2], I32)
        blank = sb("blank", [P, TAB // P, 2], I32)
        cntf = sb("cntf", [1, 2, E])
        bgu, bdn = sb("bgu", [E, 2 * FF]), sb("bdn", [E, D])
        ps = ctx.enter_context(nc.psum_tensor("rps", [P, 4, 512], F32))
        block = ctx.enter_context(nc.Block())

        @block.sync
        def _(sp):
            sp.dma_start(bgu[:], ins["exp_b_gu"].rearrange("l e n -> (l e) n")).then_inc(ev("biases"), 16)
            sp.dma_start(bdn[:], ins["exp_b_down"].rearrange("l e n -> (l e) n")).then_inc(ev("biases"), 16)
            sp.wait_ge(ev("r_blank"), 2)
            sp.dma_start(d["table"].rearrange("(p n) o -> p (n o)", p=P),
                         blank[:].rearrange("p n o -> p (n o)")).then_inc(ev("table_blank"), 16)

        @block.gpsimd
        def _(pool):
            g = nc.gpsimd
            g.memset(blank[:, :, 0:1], 0).then_inc(ev("r_blank"), 1)
            g.memset(blank[:, :, 1:2], NOROW).then_inc(ev("r_blank"), 1)
            g.iota(iota_i[:], pattern=[[1, E]], base=0, channel_multiplier=0).then_inc(ev("r_iota"), 1)
            for k in range(TOPK):
                g.iota(rowid[:, k, :, 0:1], pattern=[[P, NT], [0, 1]], base=LEAD, channel_multiplier=1)\
                    .then_inc(ev("rowid"), 1)
                g.iota(rowid[:, k, :, 1:2], pattern=[[P, NT], [0, 1]], base=k * SEQ, channel_multiplier=1)\
                    .then_inc(ev("rowid"), 1)
            g.memset(eps2[:], EPS)
            g.memset(ones[:], 1.0).then_inc(ev("r_const"), 1)
            g.memset(tri[:], 1.0).then_inc(ev("r_const"), 1)
            pool.wait_ge(ev("r_const"), 2)
            g.affine_select(out=tri[:], in_=tri[:], compare_op=ALU.is_gt, fill=0.0, base=0,
                            pattern=[[1, P]], channel_multiplier=-1).then_inc(ev("r_const"), 1)
            pool.wait_ge(ev("table_blank"), 16)
            pool.wait_ge(ev("dest"), 1)
            pool.wait_ge(ev("rowid"), 2 * TOPK)
            for k in range(TOPK):
                for i in range(NT):
                    g.indirect_dma_start(out=d["table"], out_offset=bass.IndirectOffsetOnAxis(ap=dest[:, k, i:i + 1], axis=0),
                                         in_=rowid[:, k, i], in_offset=None).then_inc(ev("table"), 16)
            pool.wait_ge(ev("table"), 16 * TOPK * NT)

        @block.vector
        def _(dve):
            v = nc.vector
            n = [0]

            def link(ins_):
                n[0] += 1
                ins_.then_inc(ev("r_step"), 1)
                dve.wait_ge(ev("r_step"), n[0])

            for i in range(NT):
                link(v.max(top[:, i], lg[:, NSPAN * NCH - NT + i]))
                link(v.max_index(topi[:, i], top[:, i], lg[:, NSPAN * NCH - NT + i]))
            link(v.tensor_copy(topf[:], topi[:]))
            dve.wait_ge(ev("r_iota"), 1)
            link(v.tensor_copy(iota[:], iota_i[:]))
            link(v.tensor_scalar(ebase[:], iota[:], float(CAP), None, ALU.mult))
            every = iota[:].rearrange("p (o e) -> p o e", o=1).broadcast_to([P, NT, E])
            for k in range(TOPK):
                link(v.tensor_tensor(hot[:, k], every, topf[:, :, k:k + 1].broadcast_to([P, NT, E]), ALU.is_equal))
            link(v.tensor_tensor(chosen[:], hot[:, 0], hot[:, 1], ALU.add))
            for k in range(2, TOPK):
                link(v.tensor_tensor(chosen[:], chosen[:], hot[:, k], ALU.add))
            link(v.memset(before[:, 0], 0.0))
            for i in range(NT):
                link(v.tensor_tensor(before[:, i + 1], before[:, i], chosen[:, i], ALU.add))
            dve.sem_inc(ev("chosen"), 1)
            link(v.tensor_tensor(gw[:], top[:, :, 0:TOPK], top[:, :, 0:1].broadcast_to([P, NT, TOPK]), ALU.subtract))
            dve.sem_inc(ev("gw_arg"), 1)
            dve.wait_ge(ev("gw_exp"), 1)
            link(v.tensor_reduce(wsum[:].rearrange("p t o -> p (t o)"), gw[:], AX.X, ALU.add))
            link(v.reciprocal(wsum[:], wsum[:]))
            link(v.tensor_tensor(gw[:], gw[:], wsum[:].broadcast_to([P, NT, TOPK]), ALU.mult))
            dve.wait_ge(ev("ranks"), 1)
            rank = ps[:, 0, 0:NT * E].rearrange("p (t e) -> p t e", e=E)
            link(v.tensor_tensor(before[:, 0:NT], rank, ebase[:].rearrange("p (o e) -> p o e", o=1)
                                 .broadcast_to([P, NT, E]), ALU.add))
            for k in range(TOPK):
                link(v.tensor_tensor(prod[:], hot[:, k], before[:, 0:NT], ALU.mult))
                link(v.tensor_reduce(destf[:, k], prod[:], AX.X, ALU.add))
            link(v.tensor_copy(dest[:], destf[:]))
            dve.sem_inc(ev("dest"), 1)
            link(v.tensor_copy(cntf[:, 0], ps[0:1, 1, 0:E]))
            link(v.memset(cntf[:, 1], 0.0))
            for m in range(-(-(CAP - MAIN) // TAIL)):
                link(v.scalar_tensor_tensor(cntf[:, 1], cntf[:, 0], float(MAIN + m * TAIL), cntf[:, 1],
                                            ALU.is_gt, ALU.add))
            link(v.tensor_copy(ntail[:], cntf[:, 1]))
            dve.wait_ge(ev("bias_cols"), 1)
            link(v.tensor_copy(biasT[:, 0:12].rearrange("p a e -> p (a e)"), ps[:, 2, 0:12 * E]))
            link(v.tensor_copy(biasT[:, 12:24].rearrange("p a e -> p (a e)"), ps[:, 3, 0:12 * E]))

        @block.scalar
        def _(act):
            act.wait_ge(ev("gw_arg"), 1)
            nc.scalar.activation(gw[:], gw[:], ACT.Exp).then_inc(ev("gw_exp"), 1)

        @block.tensor
        def _(pe):
            t = nc.tensor
            pe.wait_ge(ev("biases"), 32)
            gu = bgu[:].rearrange("e (j p two) -> e two j p", two=2, p=P)
            for n in range(24):
                src = gu[:, n // 8, n % 8] if n < 16 else bdn[:, (n - 16) * P:(n - 15) * P]
                last = t.transpose(ps[:, 2 + n // 12, (n % 12) * E:(n % 12 + 1) * E], src, ident[0:E, 0:E])
            last.then_inc(ev("bias_cols"), 1)
            pe.wait_ge(ev("chosen"), 1)
            pe.wait_ge(ev("r_const"), 3)
            for i in range(NT):
                o = ps[:, 0, i * E:(i + 1) * E]
                t.matmul(o, tri[:], chosen[:, i], start=True, stop=False)
                t.matmul(o, ones[:], before[:, i], start=False, stop=True)
            t.matmul(ps[:, 1, 0:E], ones[:], before[:, NT], start=True, stop=True).then_inc(ev("ranks"), 1)


def experts(nc, ins, d, ident, ev, ntail, biasT):
    with ExitStack() as ctx:
        def sb(name, shape, dt=F32):
            return ctx.enter_context(nc.sbuf_tensor(name, shape, dt))

        NGP, NDP, PC = 4, 2, 512
        wgu = sb("wgu", [P, NGP, KD, PC])
        wdn = sb("wdn", [P, NDP, KD, PC])
        REST = MAIN - P
        ids1, ids2 = sb("ids1", [P, 2], I32), sb("ids2", [REST, 2], I32)
        to1, to2 = sb("to1", [P, 1], I32), sb("to2", [REST, 1], I32)
        xg1, xg2 = sb("xg1", [P, D]), sb("xg2", [REST, D])
        xT = sb("exT", [P, KD, MAIN])
        gt, ut = sb("gt", [P, 2, MAIN]), sb("ut", [P, 2, MAIN])
        sg = sb("sg", [P, 2, MAIN])
        actT = sb("actT", [P, KD, MAIN])
        yT = sb("yT", [P, KD, MAIN])
        yr1, yr2 = sb("yr1", [P, D]), sb("yr2", [REST, D])
        bcol = sb("bcol", [P, 24])
        ps = ctx.enter_context(nc.psum_tensor("eps", [P, 8, 512], F32))
        BANKS = {"x": (0, 1), "gu": (2, 3, 4, 5), "dn": (6, 7), "yr": (1, 0)}
        PIECES = NGP + NDP

        def parts(n):
            return (P, n - P) if n > P else (n // 2, n // 2)

        def bank(kind, k):
            b = BANKS[kind]
            return b[k % len(b)]

        wgu_v = ins["exp_w_gu"].rearrange("l e (k p) n -> p (l e) k n", p=P)
        wdn_v = ins["exp_w_down"].rearrange("l e (k p) n -> p (l e) k n", p=P)

        def over_blocks(eng, name, body, each=None):
            reg = eng.alloc_register(name)
            eng.reg_mov(reg, 0)
            with eng.Fori(0, E) as e:
                if each:
                    each(e)
                more = eng.value_load(ntail[0:1, bass.ds(e, 1)], min_val=0, max_val=-(-(CAP - MAIN) // TAIL))
                with eng.If(more > 0):
                    with eng.Fori(0, more) as i:
                        body(e, TAIL, eng.snap(reg, min_val=0, max_val=512), e * CAP + MAIN + i * TAIL)
                        eng.reg_add(reg, reg, 1)
                with eng.Else():
                    eng.nop()
                body(e, MAIN, eng.snap(reg, min_val=0, max_val=512), e * CAP)
                eng.reg_add(reg, reg, 1)
            return eng.snap(reg, min_val=0, max_val=512)

        block = ctx.enter_context(nc.Block())

        @block.sync
        def _(sp):
            sp.nop().then_inc(ev("pieces_free"), PIECES)
            with sp.Fori(0, E) as e:
                for p in range(PIECES):
                    sp.wait_ge(ev("pieces_free"), e * PIECES + p + 1)
                    if p < NGP:
                        dst, src = wgu[:, p], wgu_v[:, bass.ds(e, 1), :, p * PC:(p + 1) * PC]
                    else:
                        q = p - NGP
                        dst, src = wdn[:, q], wdn_v[:, bass.ds(e, 1), :, q * PC:(q + 1) * PC]
                    sp.nop()
                    sp.dma_start(dst, src.rearrange("p o k n -> p (o k) n")).then_inc(ev(f"piece{p}"), 16)

        @block.gpsimd
        def _(pool):
            g = nc.gpsimd

            def store_rows():
                for src, to in ((yr1, to1), (yr2, to2)):
                    g.indirect_dma_start(out=d["y"], out_offset=bass.IndirectOffsetOnAxis(ap=to[:], axis=0),
                                         in_=src[:], in_offset=None, bounds_check=TOPK * SEQ - 1,
                                         oob_is_err=False).then_inc(ev("y_stored"), 16)

            def body(e, n, blk, row0):
                n1, n2 = parts(n)
                g.dma_start(ids1[0:n1], d["table"][bass.ds(row0, n1), :]).then_inc(ev("ids"), 16)
                g.dma_start(ids2[0:n2], d["table"][bass.ds(row0 + n1, n2), :]).then_inc(ev("ids"), 16)
                pool.wait_ge(ev("ids"), blk * 32 + 32)
                pool.wait_ge(ev("x_banks"), blk * 3 + 3)
                pool.nop().then_inc(ev("pool_turn"), 1)
                for xg, ids, m in ((xg1, ids1, n1), (xg2, ids2, n2)):
                    g.indirect_dma_start(out=xg[0:m], out_offset=None, in_=d["xn"],
                                         in_offset=bass.IndirectOffsetOnAxis(ap=ids[0:m, 0:1], axis=0))\
                        .then_inc(ev("gathered"), 16)
                pool.wait_ge(ev("y_rows"), blk * 4 + 4)
                pool.nop().then_inc(ev("pool_turn"), 1)
                store_rows()
                pool.wait_ge(ev("y_stored"), blk * 32 + 32)
                pool.nop().then_inc(ev("pool_turn"), 1)
                for to, ids, m, whole in ((to1, ids1, n1, P), (to2, ids2, n2, REST)):
                    if m < whole:
                        g.memset(to[:], NOROW).then_inc(ev("to_cleared"), 1)
                        g.drain()
                    g.tensor_copy(to[0:m], ids[0:m, 1:2]).then_inc(ev("to_set"), 1)
                pool.wait_ge(ev("to_set"), blk * 2 + 4)
                pool.wait_ge(ev("gathered"), blk * 32 + 32)
                pool.nop().then_inc(ev("pool_turn"), 1)

            for buf, value in ((to1, NOROW), (to2, NOROW)):
                g.memset(buf[:], value).then_inc(ev("to_set"), 1)
            for buf in (yr1, yr2):
                g.memset(buf[:], 0.0).then_inc(ev("yr_blank"), 1)
            pool.wait_ge(ev("to_set"), 2)
            pool.wait_ge(ev("yr_blank"), 2)
            total = over_blocks(pool, "pool_blk", body)
            pool.wait_ge(ev("y_rows"), total * 4 + 4)
            pool.nop().then_inc(ev("pool_turn"), 1)
            store_rows()
            pool.wait_ge(ev("y_stored"), total * 32 + 32)
            pool.nop().then_inc(ev("pool_turn"), 1)

        @block.tensor
        def _(pe):
            t = nc.tensor

            def body(e, n, blk, row0):
                n1, n2 = parts(n)

                def piece_done(name, value):
                    if n == MAIN:
                        pe.wait_ge(ev(name), value)
                        pe.sem_inc(ev("pieces_free"), 1)

                pe.wait_ge(ev("gathered"), blk * 32 + 32)
                for m in range(3):
                    if m == 0:
                        pe.wait_ge(ev("y_rows"), blk * 4 + 4)
                        pe.nop().then_inc(ev("pe_turn"), 1)
                    if m == 2:
                        pe.wait_ge(ev("xT_made"), blk * 3 + 1)
                        pe.nop().then_inc(ev("pe_turn"), 1)
                    for k in range(3 * m, min(3 * m + 3, KD)):
                        o = ps[:, bank("x", m), (k % 3) * MAIN:(k % 3) * MAIN + n]
                        t.transpose(o[:, 0:n1], xg1[0:n1, k * P:(k + 1) * P], ident[0:n1, 0:n1])
                        last = t.transpose(o[:, n1:n], xg2[0:n2, k * P:(k + 1) * P], ident[0:n2, 0:n2])
                    last.then_inc(ev("x_banks"), 1)
                for jj in range(8):
                    if jj == 0:
                        pe.wait_ge(ev("xT_made"), blk * 3 + 3)
                    pe.wait_ge(ev("gu_read"), blk * 8 + jj + 1)
                    if jj % 2 == 0:
                        pe.wait_ge(ev(f"piece{jj // 2}"), e * 16 + 16)
                    for two in range(2):
                        o = ps[:, bank("gu", jj), two * 256:two * 256 + n]
                        for k in range(KD):
                            c = (jj % 2) * 256 + two
                            last = t.matmul(o, wgu[:, jj // 2, k, c:c + 255:2], xT[:, k, 0:n],
                                            start=k == 0, stop=k == KD - 1)
                    last.then_inc(ev("gu_banks"), 1)
                    if jj and jj % 2 == 0:
                        piece_done("gu_banks", blk * 8 + jj)
                for m in range(3):
                    if m == 0:
                        pe.wait_ge(ev("act_made"), blk * 8 + 16)
                    if m == 2:
                        pe.wait_ge(ev("yT_made"), blk * 3 + 1)
                    for j in range(3 * m, min(3 * m + 3, KD)):
                        if j % 4 == 0:
                            pe.wait_ge(ev(f"piece{NGP + j // 4}"), e * 16 + 16)
                        o = ps[:, bank("dn", m), (j % 3) * MAIN:(j % 3) * MAIN + n]
                        for k in range(KD):
                            last = t.matmul(o, wdn[:, j // 4, k, (j % 4) * P:(j % 4 + 1) * P], actT[:, k, 0:n],
                                            start=k == 0, stop=k == KD - 1)
                    last.then_inc(ev("dn_banks"), 1)
                    if m == 0:
                        piece_done("gu_banks", blk * 8 + 8)
                for q in range(4):
                    half, rest = q % 2, q // 2
                    if q == 0:
                        pe.wait_ge(ev("yT_made"), blk * 3 + 2)
                    if q == 1:
                        pe.wait_ge(ev("yT_made"), blk * 3 + 3)
                    if q >= 2:
                        pe.wait_ge(ev("y_rows"), blk * 4 + q - 1 + 4)
                    pe.nop().then_inc(ev("pe_turn"), 1)
                    a, z = (0, n1) if rest == 0 else (n1, n)
                    for j in range(4):
                        last = t.transpose(ps[0:z - a, bank("yr", q), j * P:(j + 1) * P],
                                           yT[:, half * 4 + j, a:z], ident[:])
                    last.then_inc(ev("yr_banks"), 1)
                    if q == 0:
                        piece_done("dn_banks", blk * 3 + 2)
                        piece_done("dn_banks", blk * 3 + 3)

            pe.sem_inc(ev("x_banks"), 3)
            over_blocks(pe, "pe_blk", body)

        @block.vector
        def _(dve):
            v = nc.vector

            def each(e):
                v.tensor_copy(bcol[:], biasT[:, :, bass.ds(e, 1)].rearrange("p a o -> p (a o)")).then_inc(ev("bcol"), 1)
                dve.wait_ge(ev("bcol"), e + 1)
                dve.nop()

            def body(e, n, blk, row0):
                n1, n2 = parts(n)

                def finish(jj):
                    s = jj % 2
                    dve.wait_ge(ev("sg_made"), blk * 8 + jj + 1)
                    v.tensor_tensor(actT[:, jj, 0:n], ut[:, s, 0:n], sg[:, s, 0:n], ALU.mult).then_inc(ev("act_made"), 1)

                for jj in range(8):
                    s = jj % 2
                    dve.wait_ge(ev("gu_banks"), blk * 8 + jj + 1)
                    if jj != 1:
                        dve.wait_ge(ev("act_made"), blk * 8 + max(jj - 1, 0) + 8)
                    b = ps[:, bank("gu", jj)]
                    v.tensor_scalar(gt[:, s, 0:n], b[:, 0:n], bcol[:, jj:jj + 1], LIMIT, ALU.add, ALU.min)\
                        .then_inc(ev("g_made"), 1)
                    v.tensor_scalar(ut[:, s, 0:n], b[:, 256:256 + n], bcol[:, 8 + jj:9 + jj], LIMIT, ALU.add, ALU.min)\
                        .then_inc(ev("gu_read"), 1)
                    dve.wait_ge(ev("gu_read"), blk * 8 + jj + 1 + 4)
                    v.tensor_scalar(ut[:, s, 0:n], ut[:, s, 0:n], -LIMIT, 1.0, ALU.max, ALU.add)\
                        .then_inc(ev("u_made"), 1)
                    dve.wait_ge(ev("u_made"), blk * 8 + jj + 1)
                    v.tensor_tensor(ut[:, s, 0:n], ut[:, s, 0:n], gt[:, s, 0:n], ALU.mult).then_inc(ev("ug_made"), 1)
                    dve.wait_ge(ev("ug_made"), blk * 8 + jj + 1)
                    if jj:
                        finish(jj - 1)
                finish(7)
                for q in range(4):
                    half, rest = q % 2, q // 2
                    dve.wait_ge(ev("yr_banks"), blk * 4 + q + 1)
                    if q == 0:
                        dve.wait_ge(ev("y_stored"), blk * 32 + 32)
                    dst = (yr1, yr2)[rest]
                    m = (n1, n2)[rest]
                    v.tensor_copy(dst[0:m, half * 512:(half + 1) * 512], ps[0:m, bank("yr", q)]).then_inc(ev("y_rows"), 1)

            dve.sem_inc(ev("y_rows"), 4)
            dve.sem_inc(ev("act_made"), 8)
            dve.nop().then_inc(ev("gu_read"), 4)
            over_blocks(dve, "dve_blk", body, each)

        @block.scalar
        def _(act):
            a = nc.scalar

            def body(e, n, blk, row0):
                n1, n2 = parts(n)
                for m in range(3):
                    act.wait_ge(ev("x_banks"), blk * 3 + m + 1 + 3)
                    w = min(3, KD - 3 * m)
                    src = ps[:, bank("x", m), 0:w * MAIN].rearrange("p (k n) -> p k n", k=w)[:, :, 0:n]
                    a.copy(xT[:, 3 * m:3 * m + w, 0:n], src).then_inc(ev("xT_made"), 1)
                for jj in range(8):
                    s = jj % 2
                    act.wait_ge(ev("g_made"), blk * 8 + jj + 1)
                    if jj >= 2:
                        act.wait_ge(ev("act_made"), blk * 8 + jj - 1 + 8)
                    a.activation(sg[:, s, 0:n], gt[:, s, 0:n], ACT.Sigmoid, scale=ALPHA).then_inc(ev("sg_made"), 1)
                for m in range(3):
                    act.wait_ge(ev("dn_banks"), blk * 3 + m + 1)
                    for j in range(3 * m, min(3 * m + 3, KD)):
                        last = a.activation(yT[:, j, 0:n], ps[:, bank("dn", m), (j % 3) * MAIN:(j % 3) * MAIN + n],
                                            ACT.Identity, bias=bcol[:, 16 + j:17 + j])
                    last.then_inc(ev("yT_made"), 1)

            over_blocks(act, "act_blk", body)


def combine(nc, ins, d, ev, dest, gw, eps2, out):
    with ExitStack() as ctx:
        def sb(name, shape, dt=F32):
            return ctx.enter_context(nc.sbuf_tensor(name, shape, dt))

        NBUF = 4
        yg = sb("yg", [P, NBUF, TOPK, D])
        acc = sb("acc", [P, NBUF, D])
        sq = sb("sq", [P, D])
        nfin = sb("nfin", [P, D])
        s2 = sb("s2", [P, NT, 2])
        block = ctx.enter_context(nc.Block())
        hrows = d["h"][LEAD:ROWS].rearrange("(i p) n -> i p n", p=P)
        yrows = d["y"].rearrange("(k i p) n -> i p k n", k=TOPK, p=P)
        orows = out.rearrange("(i p) n -> i p n", p=P)

        @block.sync
        def _(sp):
            sp.dma_start(nfin[:], ins["norm_final"].rearrange("(o n) -> o n", o=1).broadcast_to([P, D])).then_inc(ev("nfin"), 16)
            for i in range(NT):
                if i >= NBUF:
                    sp.wait_ge(ev(f"out_stored{i % NBUF}"), 16 * (i // NBUF))
                sp.dma_start(acc[:, i % NBUF], hrows[i]).then_inc(ev(f"hl{i % NBUF}"), 16)
                sp.dma_start(yg[:, i % NBUF], yrows[i]).then_inc(ev(f"yg{i % NBUF}"), 16)
                if i >= 1:
                    sp.wait_ge(ev("final"), i)
                    sp.dma_start(orows[i - 1], acc[:, (i - 1) % NBUF]).then_inc(ev(f"out_stored{(i - 1) % NBUF}"), 16)
            sp.wait_ge(ev("final"), NT)
            sp.dma_start(orows[NT - 1], acc[:, (NT - 1) % NBUF]).then_inc(ev(f"out_stored{(NT - 1) % NBUF}"), 16)
            for b in range(NBUF):
                sp.wait_ge(ev(f"out_stored{b}"), 16 * (NT // NBUF))

        @block.vector
        def _(dve):
            v = nc.vector
            n = [0]

            def link(ins_):
                n[0] += 1
                ins_.then_inc(ev("c_step"), 1)
                dve.wait_ge(ev("c_step"), n[0])

            dve.wait_ge(ev("nfin"), 16)
            for i in range(NT):
                b = i % NBUF
                dve.wait_ge(ev(f"hl{b}"), 16 * (i // NBUF + 1))
                dve.wait_ge(ev(f"yg{b}"), 16 * (i // NBUF + 1))
                for k in range(TOPK):
                    link(v.scalar_tensor_tensor(acc[:, b], yg[:, b, k], gw[:, i, k:k + 1], acc[:, b], ALU.mult, ALU.add))
                dve.sem_inc(ev("summed"), 1)
                dve.wait_ge(ev("c_rms"), i + 1)
                link(v.reciprocal(s2[:, i, 1:2], s2[:, i, 0:1]))
                link(v.scalar_tensor_tensor(acc[:, b], acc[:, b], s2[:, i, 1:2], nfin[:], ALU.mult, ALU.mult))
                dve.sem_inc(ev("final"), 1)

        @block.scalar
        def _(act):
            a = nc.scalar
            for i in range(NT):
                act.wait_ge(ev("summed"), i + 1)
                a.activation(sq[:], acc[:, i % NBUF], ACT.Square, accum_out=s2[:, i, 0:1]).then_inc(ev("c_sq"), 1)
                act.wait_ge(ev("c_sq"), i + 1)
                a.activation(s2[:, i, 0:1], s2[:, i, 0:1], ACT.Sqrt, scale=1.0 / D, bias=eps2[:, 0:1]).then_inc(ev("c_rms"), 1)


_SMALL = ["hg_lb_logits", "norm_mix", "w_in", "hg_norm", "ml_conv_w", "ml_conv_b", "ml_wq", "ml_wk", "ml_wv",
          "ml_gate_b", "ml_norm", "ml_skip", "w_branch_hg", "w_branch_ml", "w_out", "norm_ffn", "router_w",
          "router_b", "exp_w_gu", "exp_b_gu", "exp_w_down", "exp_b_down", "norm_final"]


def kernel(**inputs):
    import concourse.bacc as bacc
    from concourse.bass_utils import run_bass_kernel_spmd

    nc = bacc.Bacc("TRN2", target_bir_lowering=False, num_devices=1)
    arrays = {n: np.ascontiguousarray(inputs[n]) for n in _SMALL}
    x, meta = np.asarray(inputs["x"]), np.asarray(inputs["meta_tokens"])
    arrays["rows"] = np.concatenate([np.zeros((PAD, D), x.dtype), meta, x[0]], axis=0)
    ins = {n: nc.dram_tensor(n, a.shape, mybir.dt.from_np(a.dtype), kind="ExternalInput").ap() for n, a in arrays.items()}
    out = nc.dram_tensor("out", [SEQ, D], F32, kind="ExternalOutput").ap()
    build(nc, ins, out)
    r = run_bass_kernel_spmd(nc, [arrays], core_ids=[0])
    return r.results[0]["out"].reshape(1, SEQ, D)
```

```python
import numpy as np
import concourse.bass as bass
from concourse import mybir
from contextlib import ExitStack

F32 = mybir.dt.float32
R32 = mybir.dt.float32r
I32 = mybir.dt.int32
U32 = mybir.dt.uint32
ALU = mybir.AluOpType
ACT = mybir.ActivationFunctionType
AX = mybir.AxisListType

P = 128
D = 1024
KD = D // P
META, SEQ = 16, 1024
CH = 128
NCH = 3
SPAN = NCH * CH
NSPAN = 3
ROWS = NSPAN * SPAN
LEAD = ROWS - SEQ
PAD = LEAD - META
H = 4
W = 512
QK = 64
SUB = 16
NSUB = CH // SUB
EPS = 1e-6
NEG = -1e30
BIG = 1e34

E = 32
TOPK = 4
FF = 1024
CAP = 1024
NT = SEQ // P
NPASS = CAP // (2 * P)
TAB = E * CAP + 256
LIMIT, ALPHA = 7.0, 1.702
NOROW = 1 << 20

WC = 256
NRING = 4
C_HQ, C_HF, C_HI, C_HG, C_MM, C_MO, C_IF, C_G0 = 0, 512, 1024, 1536, 2048, 2560, 3072, 3080
C_G1 = C_G0 + D


class Events:

    def __init__(self, nc, ctx):
        self.nc, self.ctx, self.made = nc, ctx, {}

    def __call__(self, name):
        if name not in self.made:
            self.made[name] = self.ctx.enter_context(self.nc.semaphore(name))
        return self.made[name]


class Banks:

    def __init__(self, nbanks):
        self.n, self.at, self.jobs, self.count, self.owner = nbanks, 0, {}, {"A": 0, "D": 0}, {}
        self.total = 0

    def add(self, name, engine, width=1):
        at = self.at if self.at + width <= self.n else 0
        before = [self.owner[b] for b in range(at, at + width) if b in self.owner]
        waits = {}
        for e, c in before:
            waits[e] = max(waits.get(e, 0), c)
        self.count[engine] += 1
        self.total += 1
        for b in range(at, at + width):
            self.owner[b] = (engine, self.count[engine])
        self.at = at + width
        self.jobs[name] = (at, self.total, waits, engine)

    def bank(self, name):
        return self.jobs[name][0]

    def ready(self, name):
        return self.jobs[name][1]


def span_jobs():
    b = Banks(8)
    for k in range(KD):
        b.add(("xT", k), "A")
    b.add("gi", "D")
    b.add("gf", "D")
    for j in range(H):
        b.add(("mm", j), "D")
    for j in range(H):
        b.add(("hf", j), "A")
    for u in range(2):
        for i in range(NCH):
            b.add(("hi", u, i), "A")
    for j in range(H):
        b.add(("hq", j), "D")
    for j in range(H):
        b.add(("hg", j), "D")
    for j in range(H):
        b.add(("mo", j), "A")
    for j in range(H):
        b.add(("qm", j), "A")
        b.add(("km", j), "A")
    for i in range(NCH):
        b.add(("kt", i), "A")
        b.add(("vm", i), "D")
    b.add("cols", "D")
    b.add("wp", "D")
    for c in range(NCH):
        b.add(("ko", c), "A")
        b.add(("mb", c), "D")
        b.add(("sc", c), "D")
        b.add(("qk", c), "D")
        b.add(("oh", c), "A")
        b.add(("ds", c), "D")
        b.add(("inter", c), "A", 2)
        b.add(("intra", c), "D", 2)
        b.add(("dm", c), "D", 2)
        b.add(("yh", c), "D")
        b.add(("ym", c), "D")
    for m in range(4):
        for j in range(2):
            b.add(("g0", m, j), "A")
        for j in range(2):
            b.add(("b0", m, j), "D")
        for j in range(2):
            b.add(("g1", m, j), "A")
        for j in range(2):
            b.add(("b1", m, j), "D")
    for u in range(4):
        for i in range(NCH):
            b.add(("wo", u, i), "D")
    for k in range(KD):
        b.add(("nT", k), "A")
    for i in range(NCH):
        b.add(("lg", i), "D")
    return b


def weight_chunks():
    out = []
    for name, c0 in (("mm", C_MM), ("hf", C_HF), ("hi", C_HI), ("hq", C_HQ), ("hg", C_HG), ("mo", C_MO)):
        for u in range(2):
            out.append((name, u, c0 + u * WC))
    for m in range(4):
        out += [("g0", m, C_G0 + m * WC), ("b0", m, m * WC), ("g1", m, C_G1 + m * WC), ("b1", m, m * WC)]
    for u in range(4):
        out.append(("wo", u, u * WC))
    return out


def build(nc, ins, out, dbg=None):
    with ExitStack() as top:
        ev = Events(nc, top)

        def dram(name, shape, dt=F32):
            return nc.dram_tensor(name, shape, dt, kind="ExternalOutput" if dbg else "Internal").ap()

        d = {
            "h": dram("h_rows", [ROWS, D]),
            "hb": dram("hb_rows", [SEQ, D]),
            "xn": dram("xn_rows", [ROWS, D]),
            "table": dram("row_table", [TAB, 2], I32),
            "y": dram("y_rows", [TOPK * SEQ, D]),
        }
        lg = top.enter_context(nc.sbuf_tensor("lg", [P, NSPAN * NCH, E], F32))
        ident = top.enter_context(nc.sbuf_tensor("ident", [P, P], F32))
        mixer(nc, ins, d, lg, ident, ev)
        if dbg != "mixer":
            from_routing(nc, ins, d, lg, ident, ev, out)


def mixer(nc, ins, d, lg, ident, ev):
    with ExitStack() as ctx:
        def sb(name, shape, dt=F32):
            return ctx.enter_context(nc.sbuf_tensor(name, shape, dt))

        xrow = sb("xrow", [P, NCH, D])
        region = sb("region", [P, H * NSUB * CH])
        xs = region[:, 0:NCH * D].rearrange("p (i n) -> p i n", i=NCH)
        kdec = region[:, :].rearrange("p (h i s) -> p h i s", h=H, i=NSUB)
        xT = sb("xT", [P, KD, SPAN])
        tmp = sb("tmp", [P, 2, H, SPAN])
        tmp1, kout = tmp[:, 0], tmp[:, 1]
        merged = tmp[:, :, :, :].rearrange("p a h s -> p (a h) s")
        qin, qdec, kh, bh = (sb(n, [P, H, SPAN]) for n in ("qin", "qdec", "kh", "bh"))
        sgh, conv, smo = (sb(n, [P, H, SPAN]) for n in ("sgh", "conv", "smo"))
        mmT = sb("mmT", [P, H, 3 + SPAN])
        qm, km = sb("qm", [QK, H, SPAN]), sb("km", [QK, H, SPAN])
        kt = sb("kt", [P, NCH, H, QK])
        VA = P + 2
        va = sb("va", [P, NCH, H, VA])
        vh = sb("vh", [P, NCH, W])
        sct, wgt, ktok = sb("sct", [P, H, CH]), sb("wgt", [P, H, CH]), sb("ktok", [P, H, CH])
        kw = sb("kw", [P, H, QK])
        nd = sb("nd", [P, H, VA])
        oh, om = sb("oh", [P, H, CH]), sb("om", [P, H, CH])
        ring = sb("ring", [P, NRING, KD, WC])
        sh, sm = sb("sh", [P, H, P]), sb("sm", [QK, H, VA])
        mst = sb("mst", [H, NCH + 1])
        ra, rb, rc, rm, rd = (sb(n, [H, SPAN]) for n in ("ra", "rb", "rc", "rm", "rd"))
        padneg, keep4 = sb("padneg", [H, SPAN]), sb("keep4", [H, SPAN])
        mneg = sb("mneg", [H, NCH])
        dwp = sb("dwp", [H, NCH, H])
        cols, wpb, ebl = sb("cols", [P, NCH, 4, H]), sb("wpb", [QK, NCH, H]), sb("ebl", [P, H, NCH])
        ss = sb("ss", [P, NCH, 4])
        hs = sb("hs", [P, 6, H])
        keep = sb("keep", [P, CH])
        mge = sb("mge", [P, CH])
        mask = sb("mask", [P, CH], I32)
        sel = sb("sel", [H, H, P])
        ones4 = sb("ones4", [H, QK])
        epsc = sb("epsc", [P, 1])
        wif = sb("wif", [P, KD, 2 * H])
        wq, wk, wv = sb("wq", [P, H, QK]), sb("wk", [P, H, QK]), sb("wv", [P, H, P])
        rw, rbias = sb("rw", [P, KD, E]), sb("rbias", [P, E])
        nmix, nffn = sb("nmix", [P, KD]), sb("nffn", [P, D])
        cw, cb = sb("cw", [P, 4, H]), sb("cb", [P, H])
        hgn, mln, skp = sb("hgn", [P, H]), sb("mln", [P, H]), sb("skp", [P, H])
        lb, oml, lgt = sb("lb", [P, H]), sb("oml", [P, H]), sb("lgt", [P, 2, H])
        gbi, gbf = sb("gbi", [H, 1]), sb("gbf", [H, 1])
        ps = ctx.enter_context(nc.psum_tensor("ps", [P, 8, 512], F32))

        gate0, gate1 = kh, bh

        def ml_gated(m):
            return (qin, qdec)[m // 4][:, m % 4]

        J = span_jobs()
        L = weight_chunks()
        at = {(n, u): i for i, (n, u, _) in enumerate(L)}

        def last_use(name, u):
            if name in ("hi", "wo"):
                return name, u, NCH - 1
            return (name, u, 1) if name in ("g0", "b0", "g1", "b1") else (name, 2 * u + 1)

        def slot(n, u):
            return ring[:, at[n, u] % NRING]

        def bank(name, parts=P, w=512):
            return ps[0:parts, J.bank(name), 0:w]

        def two(name, parts=P):
            b = J.bank(name)
            return ps[0:parts, b:b + 2, :].rearrange("p b (a v) -> p b a v", a=2)[:, :, :, 0:P + 1]

        SETUP = ("const", "smallw", "lbs")
        small = [
            (wif[:, :, :], ins["w_in"][:, :, C_IF:C_IF + 2 * H].rearrange("l (k p) n -> p (l k) n", p=P)),
            (wq[:, :, :], ins["ml_wq"].rearrange("l h c d -> c (l h) d")),
            (wk[:, :, :], ins["ml_wk"].rearrange("l h c d -> c (l h) d")),
            (wv[:, :, :], ins["ml_wv"].rearrange("l h c d -> c (l h) d")),
            (rw[:, :, :], ins["router_w"].rearrange("l (k p) e -> p (l k) e", p=P)),
            (rbias[:, :], ins["router_b"].broadcast_to([P, E])),
            (nffn[:, :], ins["norm_ffn"].broadcast_to([P, D])),
            (nmix[:, :], ins["norm_mix"].rearrange("l (k p) -> p (l k)", p=P)),
            (cb[:, :], ins["ml_conv_b"].rearrange("l (h p) -> p (l h)", p=P)),
            (hgn[:, :], ins["hg_norm"].rearrange("l (h p) -> p (l h)", p=P)),
            (mln[:, :], ins["ml_norm"].rearrange("l (h p) -> p (l h)", p=P)),
            (skp[:, :], ins["ml_skip"].rearrange("l (h p) -> p (l h)", p=P)),
            (gbi[:, :], ins["ml_gate_b"][0:1, 0:H].rearrange("l h -> h l")),
            (gbf[:, :], ins["ml_gate_b"][0:1, H:2 * H].rearrange("l h -> h l")),
        ] + [(cw[:, w], ins["ml_conv_w"][0, w].rearrange("(h p) -> p h", p=P)) for w in range(4)] \
          + [(lgt[:, r], ins["hg_lb_logits"][r].rearrange("(h p) -> p h", p=P)) for r in range(2)]

        ENGINES = 5

        def span_end(eng, s):
            eng.nop().then_inc(ev("span_ended"), 1)
            eng.wait_ge(ev("span_cleared"), s + 1)
            eng.nop()

        w_in = ins["w_in"].rearrange("l (k p) n -> p (l k) n", p=P)
        wbh = ins["w_branch_hg"].rearrange("l (k p) n -> p (l k) n", p=P)
        wbm = ins["w_branch_ml"].rearrange("l (k p) n -> p (l k) n", p=P)
        w_out = ins["w_out"].rearrange("l (k p) n -> p (l k) n", p=P)
        xin = ins["rows"].rearrange("(i p) n -> p i n", p=P)
        hrows = d["h"].rearrange("(i p) n -> p i n", p=P)
        nrows = d["xn"].rearrange("(i p) n -> p i n", p=P)

        block = ctx.enter_context(nc.Block())

        @block.gpsimd
        def _(pool):
            g = nc.gpsimd
            n = [0]

            def link(ins_):
                n[0] += 1
                ins_.then_inc(ev("pool_const"), 1)
                pool.wait_ge(ev("pool_const"), n[0])

            link(g.memset(ident[:], 0.0))
            link(g.affine_select(out=ident[:], in_=ident[:], compare_op=ALU.not_equal, fill=1.0, base=0,
                                 pattern=[[-1, P]], channel_multiplier=1))
            link(g.memset(mge[:], 0.0))
            link(g.affine_select(out=mge[:], in_=mge[:], compare_op=ALU.is_ge, fill=NEG, base=0,
                                 pattern=[[1, CH]], channel_multiplier=-1))
            link(g.memset(mask[:], 1))
            link(g.affine_select(out=mask[:], in_=mask[:], compare_op=ALU.is_ge, fill=0.0, base=0,
                                 pattern=[[1, CH]], channel_multiplier=-1))
            link(g.memset(keep[:], 1.0))
            link(g.memset(keep[:, 0:1], 0.0))
            link(g.memset(keep4[:], 1.0))
            for c in range(NCH):
                link(g.memset(keep4[:, c * CH:c * CH + 1], 0.0))
            link(g.memset(padneg[:], 0.0))
            link(g.memset(padneg[:, 0:PAD], NEG))
            link(g.memset(sel[:], 0.0))
            link(g.affine_select(out=sel[:], in_=sel[:], compare_op=ALU.not_equal, fill=-1.0, base=0,
                                 pattern=[[-1, H], [0, P]], channel_multiplier=1))
            link(g.memset(ones4[:], 1.0))
            link(g.memset(epsc[:], EPS))
            link(g.memset(sh[:], 0.0))
            link(g.memset(sm[:], 0.0))
            link(g.memset(mst[:], 0.0))
            link(g.memset(mmT[:], 0.0))
            link(g.memset(va[:], 1.0))
            g.memset(sct[:], 0.0).then_inc(ev("const"), 1)
            with pool.Fori(0, NSPAN) as s:
                pool.wait_ge(ev("ps_ready"), J.ready(("xT", KD - 1)))
                pool.wait_ge(ev("bh_ready"), 1)
                g.memset(region[:], 0.0).then_inc(ev("kdec_zero"), 1)
                pool.wait_ge(ev("kdec_zero"), 1)
                for c in range(NCH):
                    if c:
                        pool.wait_ge(ev("ps_ready"), J.ready(("sc", c - 1)))
                    for i in range(NSUB):
                        n_s = (i + 1) * SUB
                        ref = bh[:, :, c * CH + i * SUB + SUB // 2 - 1:c * CH + i * SUB + SUB // 2]
                        g.tensor_tensor(kdec[:, :, i, 0:n_s], ref.broadcast_to([P, H, n_s]),
                                        bh[:, :, c * CH:c * CH + n_s], ALU.subtract).then_inc(ev("kexp_arg"), 1)
                for m in range(8):
                    pool.wait_ge(ev("branches"), m + 1)
                    g.tensor_tensor(merged[:, m], merged[:, m], ml_gated(m), ALU.add).then_inc(ev("merged"), 1)
                span_end(pool, s)

        @block.vector
        def _(dve):
            v = nc.vector
            seq = [0]

            def link(ins_, *also):
                seq[0] += 1
                ins_.then_inc(ev("dve_step"), 1)
                dve.wait_ge(ev("dve_step"), seq[0])
                for name in also:
                    dve.sem_inc(ev(name), 1)

            def freed(name):
                assert J.jobs[name][3] == "D"
                dve.sem_inc(ev("D_freed"), 1)

            def ready(name):
                dve.wait_ge(ev("ps_ready"), J.ready(name))

            dve.wait_ge(ev("const"), 1)
            dve.wait_ge(ev("smallw"), 16 * len(small))
            v.tensor_tensor(lb[:], lgt[:, 1], lgt[:, 0], ALU.subtract).then_inc(ev("lbd"), 1)
            dve.wait_ge(ev("lbs"), 1)
            v.tensor_scalar(oml[:], lb[:], -1.0, 1.0, ALU.mult, ALU.add).then_inc(ev("oml"), 1)
            dve.wait_ge(ev("oml"), 1)
            with dve.Fori(0, NSPAN) as s:
                for i in range(NCH):
                    dve.wait_ge(ev("ss1"), i + 1)
                    link(v.reciprocal(ss[:, i, 1:2], ss[:, i, 0:1]))
                    link(v.tensor_scalar(xs[:, i], xrow[:, i], ss[:, i, 1:2], None, ALU.mult), "xs")
                ready("gi")
                link(v.scalar_tensor_tensor(rc[:], bank("gi", H, SPAN), gbi[:, 0:1], padneg[:], ALU.add, ALU.add))
                freed("gi")
                ready("gf")
                link(v.tensor_scalar(ra[:], bank("gf", H, SPAN), gbf[:, 0:1], None, ALU.add), "gf_sum")
                freed("gf")
                link(v.tensor_copy(mmT[:, :, 0:3], mmT[:, :, SPAN:SPAN + 3]))
                for j in range(H):
                    ready(("mm", j))
                    link(v.tensor_copy(mmT[:, j, 3:3 + SPAN], bank(("mm", j), P, SPAN)), "mmT")
                    freed(("mm", j))
                for j in range(H):
                    link(v.tensor_scalar(conv[:, j], mmT[:, j, 0:SPAN], cw[:, 0, j:j + 1], cb[:, j:j + 1],
                                         ALU.mult, ALU.add))
                    for w in range(1, 4):
                        link(v.scalar_tensor_tensor(conv[:, j], mmT[:, j, w:w + SPAN], cw[:, w, j:j + 1],
                                                    conv[:, j], ALU.mult, ALU.add))
                    dve.sem_inc(ev("conv_lin"), 1)
                for j in range(H):
                    dve.wait_ge(ev("hf_sig"), j + 1)
                    link(v.tensor_scalar(tmp1[:, j], tmp1[:, j], oml[:, j:j + 1], lb[:, j:j + 1], ALU.mult, ALU.add))
                dve.sem_inc(ev("f_ready"), 1)
                link(v.tensor_scalar(kh[:], tmp1, -1.0, 1.0, ALU.mult, ALU.add))
                for j in range(H):
                    dve.wait_ge(ev("conv_sig"), j + 1)
                    link(v.tensor_tensor(conv[:, j], conv[:, j], smo[:, j], ALU.mult), "conv_ready")
                for j in range(H):
                    dve.wait_ge(ev("hq_sig"), j + 1)
                    link(v.tensor_tensor(qin[:, j], bank(("hq", j), P, SPAN), qin[:, j], ALU.mult))
                    freed(("hq", j))
                for j in range(H):
                    dve.wait_ge(ev("hg_sig"), j + 1)
                    link(v.tensor_tensor(sgh[:, j], bank(("hg", j), P, SPAN), sgh[:, j], ALU.mult))
                    freed(("hg", j))
                dve.wait_ge(ev("logf"), 1)
                for j in range(H):
                    for c in range(NCH):
                        cs = slice(c * CH, (c + 1) * CH)
                        last = v.tensor_tensor_scan(bh[:, j, cs], keep[:], kout[:, j, cs], 0.0, ALU.mult, ALU.add)
                link(last, "bh_ready")
                b4 = bh[:].rearrange("p h (n s) -> p (h n) s", s=SUB)
                t4 = tmp1.rearrange("p h (n s) -> p (h n) s", s=SUB)
                mid = b4[:, :, SUB // 2 - 1:SUB // 2].broadcast_to([P, H * NCH * NSUB, SUB])
                link(v.tensor_tensor(t4, b4, mid, ALU.subtract), "qexp_arg")
                b3 = bh[:].rearrange("p h (n s) -> p (h n) s", s=CH)
                k3 = kout.rearrange("p h (n s) -> p (h n) s", s=CH)
                lastb = b3[:, :, CH - 1:CH].broadcast_to([P, H * NCH, CH])
                link(v.tensor_tensor(k3, lastb, b3, ALU.subtract), "kout_arg")
                dve.wait_ge(ev("qexp"), 1)
                link(v.scalar_tensor_tensor(qdec[:], tmp1, BIG, qin[:], ALU.min, ALU.mult), "qdec")
                dve.wait_ge(ev("qin_exp"), 1)
                link(v.tensor_tensor(qin[:], qin[:], tmp1, ALU.mult), "qin")
                dve.wait_ge(ev("kout_exp"), 1)
                link(v.tensor_tensor(kout, kout, kh[:], ALU.mult), "kout")
                dve.wait_ge(ev("lf_log"), 1)
                link(v.scalar_tensor_tensor(ra[:], ra[:], 0.0, rb[:], ALU.min, ALU.subtract))
                link(v.tensor_tensor_scan(rb[:], keep4[:], ra[:], 0.0, ALU.mult, ALU.add))
                link(v.tensor_tensor(rc[:], rc[:], rb[:], ALU.subtract))
                link(v.tensor_copy(mst[:, 0:1], mst[:, NCH:NCH + 1]))
                for c in range(NCH):
                    cs = slice(c * CH, (c + 1) * CH)
                    end = slice((c + 1) * CH - 1, (c + 1) * CH)
                    link(v.tensor_tensor_scan(rm[:, cs], rc[:, cs], rc[:, cs], mst[:, c:c + 1], ALU.max, ALU.max))
                    link(v.tensor_tensor(mst[:, c + 1:c + 2], rb[:, end], rm[:, end], ALU.add))
                    link(v.tensor_scalar(mneg[:, c:c + 1], rm[:, end], -1.0, None, ALU.mult))
                link(v.tensor_tensor(rb[:], rb[:], rm[:], ALU.add), "rows")
                link(v.memset(padneg[:], 0.0))
                dve.wait_ge(ev("row_exps"), 1)
                for c in range(NCH):
                    end = slice((c + 1) * CH - 1, (c + 1) * CH)
                    link(v.tensor_scalar(dwp[:, c], ident[0:H, 0:H], ra[:, end], None, ALU.mult))
                dve.sem_inc(ev("dwp"), 1)
                for i in range(NCH):
                    ready(("vm", i))
                    link(v.tensor_copy(va[:, i, :, 0:P], bank(("vm", i)).rearrange("p (h v) -> p h v", h=H)), "vm")
                    freed(("vm", i))
                ready("cols")
                link(v.tensor_copy(cols[:].rearrange("p c k h -> p (c k h)"), bank("cols", P, NCH * 16)), "cols")
                freed("cols")
                ready("wp")
                link(v.tensor_copy(wpb[:].rearrange("p c h -> p (c h)"), bank("wp", QK, NCH * H)))
                freed("wp")
                for j in range(H):
                    link(v.tensor_scalar(conv[:, j], conv[:, j], skp[:, j:j + 1], None, ALU.mult))

                for c in range(NCH):
                    cs = slice(c * CH, (c + 1) * CH)
                    for i in range(NSUB):
                        n_s = (i + 1) * SUB
                        dve.wait_ge(ev("kexp"), c * NSUB + i + 1)
                        link(v.scalar_tensor_tensor(kdec[:, :, i, 0:n_s], kdec[:, :, i, 0:n_s], BIG,
                                                    kh[:, :, c * CH:c * CH + n_s], ALU.min, ALU.mult))
                    dve.sem_inc(ev("kdec"), 1)
                    ready(("mb", c))
                    if c:
                        dve.wait_ge(ev("ps_ready"), J.ready(("intra", c - 1)))
                    for h in range(H):
                        link(v.scalar_tensor_tensor(wgt[:, h], bank(("mb", c)).rearrange("p (h t) -> p h t", h=H)[:, h],
                                                    cols[:, c, 0, h:h + 1], mge[:], ALU.add, ALU.min))
                    dve.sem_inc(ev("wexp_arg"), 1)
                    freed(("mb", c))
                    link(v.tensor_tensor(kw[:], kt[:, c], cols[:, c, 3].rearrange("p (h o) -> p h o", o=1)
                                         .broadcast_to([P, H, QK]), ALU.mult), "kw")
                    ready(("sc", c))
                    link(v.copy_predicated(sct[:], mask[:].rearrange("p (o t) -> p o t", o=1).broadcast_to([P, H, CH]),
                                           bank(("sc", c)).rearrange("p (h t) -> p h t", h=H)), "sct")
                    freed(("sc", c))
                    ready(("qk", c))
                    dve.wait_ge(ev("wexp"), c + 1)
                    link(v.tensor_tensor(wgt[:], wgt[:], bank(("qk", c)).rearrange("p (h t) -> p h t", h=H), ALU.mult),
                         "wgt")
                    freed(("qk", c))
                    ready(("ds", c))
                    for h in range(H):
                        link(v.scalar_tensor_tensor(sh[:, h], sh[:, h], ebl[:, h, c:c + 1],
                                                    bank(("ds", c)).rearrange("p (h t) -> p h t", h=H)[:, h],
                                                    ALU.mult, ALU.add))
                    dve.sem_inc(ev("sh_new"), 1)
                    freed(("ds", c))
                    dve.wait_ge(ev("inter_sc"), c + 1)
                    ready(("intra", c))
                    nd4 = nd[:].rearrange("p (b a) v -> p b a v", a=2)[:, :, :, 0:P + 1]
                    for b2 in range(2):
                        link(v.tensor_tensor(nd4[:, b2], nd4[:, b2], two(("intra", c))[:, b2], ALU.add))
                    freed(("intra", c))
                    ready(("dm", c))
                    for h in range(H):
                        link(v.scalar_tensor_tensor(sm[:, h, 0:P + 1], sm[:, h, 0:P + 1], wpb[:, c, h:h + 1],
                                                    two(("dm", c), QK)[:, h // 2, h % 2], ALU.mult, ALU.add))
                    dve.sem_inc(ev("sm_new"), 1)
                    freed(("dm", c))
                    den = nd[:, :, P:P + 1].rearrange("p h o -> p (h o)")
                    link(v.scalar_tensor_tensor(hs[:, 0], den, -1.0, den, ALU.mult, ALU.max))
                    link(v.tensor_tensor(hs[:, 0], hs[:, 0], cols[:, c, 2], ALU.max))
                    link(v.reciprocal(hs[:, 0], hs[:, 0]))
                    if c:
                        dve.wait_ge(ev("ps_ready"), J.ready(("ym", c - 1)))
                    link(v.tensor_tensor(om[:], nd[:, :, 0:P], hs[:, 0].rearrange("p (h o) -> p h o", o=1)
                                         .broadcast_to([P, H, P]), ALU.mult), "om")
                    dve.wait_ge(ev("o_rms"), 2 * c + 1)
                    link(v.tensor_tensor(oh[:], oh[:], hs[:, 2].rearrange("p (h o) -> p h o", o=1)
                                         .broadcast_to([P, H, P]), ALU.mult), "oh_n")
                    dve.wait_ge(ev("o_rms"), 2 * c + 2)
                    link(v.tensor_tensor(om[:], om[:], hs[:, 4].rearrange("p (h o) -> p h o", o=1)
                                         .broadcast_to([P, H, P]), ALU.mult), "om_n")
                    ready(("yh", c))
                    for h in range(H):
                        link(v.scalar_tensor_tensor(sgh[:, h, cs], bank(("yh", c))[:, h * P:(h + 1) * P],
                                                    hgn[:, h:h + 1], sgh[:, h, cs], ALU.mult, ALU.mult))
                    freed(("yh", c))
                    ready(("ym", c))
                    for h in range(H):
                        link(v.scalar_tensor_tensor(conv[:, h, cs], bank(("ym", c))[:, h * P:(h + 1) * P],
                                                    mln[:, h:h + 1], conv[:, h, cs], ALU.mult, ALU.add))
                    freed(("ym", c))
                    link(v.tensor_tensor(smo[:, :, cs], conv[:, :, cs], smo[:, :, cs], ALU.mult), "y_ready")

                for m in range(4):
                    for j in range(2):
                        t = 2 * m + j
                        ready(("b0", m, j))
                        dve.wait_ge(ev("gates"), 4 * m + j + 1)
                        link(v.tensor_tensor(merged[:, t], bank(("b0", m, j), P, SPAN), gate0[:, t % 4], ALU.mult))
                        freed(("b0", m, j))
                    for j in range(2):
                        t = 2 * m + j
                        ready(("b1", m, j))
                        dve.wait_ge(ev("gates"), 4 * m + 2 + j + 1)
                        link(v.tensor_tensor(ml_gated(t), bank(("b1", m, j), P, SPAN), gate1[:, t % 4], ALU.mult),
                             "branches")
                        freed(("b1", m, j))
                for u in range(4):
                    for i in range(NCH):
                        us = slice(u * WC, (u + 1) * WC)
                        ready(("wo", u, i))
                        link(v.tensor_tensor(xs[:, i, us], bank(("wo", u, i), P, WC), xrow[:, i, us], ALU.add))
                        freed(("wo", u, i))
                dve.sem_inc(ev("h_ready"), 1)
                for i in range(NCH):
                    dve.wait_ge(ev("ss2"), i + 1)
                    link(v.reciprocal(ss[:, i, 3:4], ss[:, i, 2:3]))
                    link(v.scalar_tensor_tensor(xrow[:, i], xs[:, i], ss[:, i, 3:4], nffn[:], ALU.mult, ALU.mult),
                         "xn_ready")
                for i in range(NCH):
                    ready(("lg", i))
                    link(v.tensor_tensor(lg[:, bass.ds(s * NCH + i, 1), :].rearrange("p o e -> p (o e)"),
                                         bank(("lg", i), P, E), rbias[:], ALU.add))
                    freed(("lg", i))
                span_end(dve, s)

        @block.scalar
        def _(act):
            a = nc.scalar
            seq = [0]

            def link(ins_, *also):
                seq[0] += 1
                ins_.then_inc(ev("act_step"), 1)
                act.wait_ge(ev("act_step"), seq[0])
                for name in also:
                    act.sem_inc(ev(name), 1)

            def freed(name):
                assert J.jobs[name][3] == "A"
                act.sem_inc(ev("A_freed"), 1)

            def ready(name):
                act.wait_ge(ev("ps_ready"), J.ready(name))

            act.wait_ge(ev("lbd"), 1)
            a.activation(lb[:], lb[:], ACT.Sigmoid, scale=-1.0).then_inc(ev("lbs"), 1)
            with act.Fori(0, NSPAN) as s:
                act.wait_ge(ev("x_loaded"), 16)
                for i in range(NCH):
                    link(a.activation(xs[:, i], xrow[:, i], ACT.Square, accum_out=ss[:, i, 0:1]))
                for i in range(NCH):
                    link(a.activation(ss[:, i, 0:1], ss[:, i, 0:1], ACT.Sqrt, scale=1.0 / D, bias=epsc[:, 0:1]), "ss1")
                for k in range(KD):
                    ready(("xT", k))
                    link(a.activation(xT[:, k], bank(("xT", k), P, SPAN), ACT.Copy, scale=nmix[:, k:k + 1]), "xT")
                    freed(("xT", k))
                for j in range(H):
                    ready(("hf", j))
                    link(a.activation(tmp1[:, j], bank(("hf", j), P, SPAN), ACT.Sigmoid), "hf_sig")
                    freed(("hf", j))
                for j in range(H):
                    act.wait_ge(ev("conv_lin"), j + 1)
                    link(a.activation(smo[:, j], conv[:, j], ACT.Sigmoid), "conv_sig")
                for u in range(2):
                    for i in range(NCH):
                        ready(("hi", u, i))
                        link(a.copy(vh[:, i, u * WC:(u + 1) * WC], bank(("hi", u, i), P, WC)), "vh")
                        freed(("hi", u, i))
                for j in range(H):
                    ready(("hq", j))
                    link(a.activation(qin[:, j], bank(("hq", j), P, SPAN), ACT.Sigmoid), "hq_sig")
                for j in range(H):
                    ready(("hg", j))
                    link(a.activation(sgh[:, j], bank(("hg", j), P, SPAN), ACT.Sigmoid), "hg_sig")
                act.wait_ge(ev("conv_ready"), H)
                for j in range(H):
                    ready(("mo", j))
                    link(a.activation(smo[:, j], bank(("mo", j), P, SPAN), ACT.Sigmoid))
                    freed(("mo", j))
                act.wait_ge(ev("f_ready"), 1)
                link(a.activation(kout, tmp1, ACT.Ln), "logf")
                act.wait_ge(ev("gf_sum"), 1)
                link(a.activation(rb[:], ra[:], ACT.Abs))
                link(a.activation(rb[:], rb[:], ACT.Exp, scale=-1.0))
                link(a.activation(rb[:], rb[:], ACT.Ln, bias=1.0), "lf_log")
                for j in range(H):
                    ready(("qm", j))
                    link(a.mul(qm[:, j], bank(("qm", j), QK, SPAN), QK ** -0.5))
                    freed(("qm", j))
                    ready(("km", j))
                    link(a.copy(km[:, j], bank(("km", j), QK, SPAN)), "qkm")
                    freed(("km", j))
                act.wait_ge(ev("qexp_arg"), 1)
                link(a.activation(tmp1, tmp1, ACT.Exp), "qexp")
                act.wait_ge(ev("kout_arg"), 1)
                link(a.activation(kout, kout, ACT.Exp), "kout_exp")
                act.wait_ge(ev("qdec"), 1)
                link(a.activation(tmp1, bh[:], ACT.Exp), "qin_exp")
                link(a.activation(ebl[:].rearrange("p h c -> p (h c)"),
                                  bh[:].rearrange("p h (n s) -> p (h n) s", s=CH)[:, :, CH - 1:CH]
                                  .rearrange("p n o -> p (n o)"), ACT.Exp))
                for i in range(NCH):
                    ready(("kt", i))
                    link(a.copy(kt[:, i].rearrange("p h d -> p (h d)"), bank(("kt", i), P, H * QK)), "kt")
                    freed(("kt", i))
                act.wait_ge(ev("rows"), 1)
                for c in range(NCH):
                    cs = slice(c * CH, (c + 1) * CH)
                    a.activation(ra[:, cs], rm[:, cs], ACT.Exp, scale=-1.0, bias=mst[:, c:c + 1])
                    a.activation(rd[:, cs], rc[:, cs], ACT.Exp, bias=mneg[:, c:c + 1])
                link(a.activation(rb[:], rb[:], ACT.Exp, scale=-1.0), "row_exps")

                for c in range(NCH):
                    for i in range(NSUB):
                        n_s = (i + 1) * SUB
                        act.wait_ge(ev("kexp_arg"), c * NSUB + i + 1)
                        link(a.activation(kdec[:, :, i, 0:n_s], kdec[:, :, i, 0:n_s], ACT.Exp), "kexp")
                    ready(("ko", c))
                    link(a.copy(ktok[:].rearrange("p h d -> p (h d)"), bank(("ko", c))), "ktok")
                    freed(("ko", c))
                    act.wait_ge(ev("wexp_arg"), c + 1)
                    link(a.activation(wgt[:], wgt[:], ACT.Exp), "wexp")
                    ready(("oh", c))
                    if c:
                        act.wait_ge(ev("ps_ready"), J.ready(("yh", c - 1)))
                    link(a.copy(oh[:].rearrange("p h d -> p (h d)"), bank(("oh", c))))
                    freed(("oh", c))
                    for h in range(H):
                        a.activation(tmp1[:, h, 0:CH], oh[:, h], ACT.Square, accum_out=hs[:, 1, h:h + 1])
                    link(a.activation(epsc[:, 0:1], epsc[:, 0:1], ACT.Copy))
                    link(a.activation(hs[:, 1], hs[:, 1], ACT.Ln, scale=1.0 / P, bias=epsc[:, 0:1]))
                    link(a.activation(hs[:, 2], hs[:, 1], ACT.Exp, scale=-0.5), "o_rms")
                    ready(("inter", c))
                    for h in range(H):
                        last = a.activation(nd[:, h, 0:P + 1], two(("inter", c))[:, h // 2, h % 2], ACT.Copy,
                                            scale=cols[:, c, 1, h:h + 1])
                    link(last, "inter_sc")
                    freed(("inter", c))
                    act.wait_ge(ev("om"), c + 1)
                    for h in range(H):
                        a.activation(tmp1[:, h, 0:CH], om[:, h], ACT.Square, accum_out=hs[:, 3, h:h + 1])
                    link(a.activation(epsc[:, 0:1], epsc[:, 0:1], ACT.Copy))
                    link(a.activation(hs[:, 3], hs[:, 3], ACT.Ln, scale=1.0 / P, bias=epsc[:, 0:1]))
                    link(a.activation(hs[:, 4], hs[:, 3], ACT.Exp, scale=-0.5), "o_rms")
                act.wait_ge(ev("y_ready"), NCH)
                for m in range(4):
                    if m >= 2:
                        act.wait_ge(ev("branches"), 2 * (m - 1))
                    for w, g in (("g0", gate0), ("g1", gate1)):
                        for j in range(2):
                            ready((w, m, j))
                            link(a.activation(g[:, (2 * m + j) % 4], bank((w, m, j), P, SPAN), ACT.Sigmoid), "gates")
                            freed((w, m, j))
                act.wait_ge(ev("h_ready"), 1)
                act.wait_ge(ev("merged"), 8)
                for i in range(NCH):
                    link(a.activation(merged[:, 0:8].rearrange("p m s -> p (m s)")[:, 0:D], xs[:, i], ACT.Square,
                                      accum_out=ss[:, i, 2:3]))
                for i in range(NCH):
                    link(a.activation(ss[:, i, 2:3], ss[:, i, 2:3], ACT.Sqrt, scale=1.0 / D, bias=epsc[:, 0:1]), "ss2")
                for k in range(KD):
                    ready(("nT", k))
                    link(a.copy(xT[:, k], bank(("nT", k), P, SPAN)), "nT")
                    freed(("nT", k))
                span_end(act, s)

        @block.tensor
        def _(pe):
            t = nc.tensor

            def begin(name):
                for e, c in J.jobs[name][2].items():
                    pe.wait_ge(ev(f"{e}_freed"), c)

            def done(last):
                last.then_inc(ev("ps_ready"), 1)

            def weights(name, u):
                n = at[name, u]
                pe.wait_ge(ev(f"w_loaded{n % NRING}"), 16 * (n // NRING + 1))

            pe.wait_ge(ev("const"), 1)
            pe.wait_ge(ev("smallw"), 16 * len(small))
            with pe.Fori(0, NSPAN) as s:
                pe.wait_ge(ev("xs"), NCH)
                for k in range(KD):
                    begin(("xT", k))
                    for i in range(NCH):
                        last = t.transpose(bank(("xT", k))[:, i * P:(i + 1) * P], xs[:, i, k * P:(k + 1) * P], ident[:])
                    done(last)
                pe.wait_ge(ev("xT"), KD)
                for name, o in (("gi", 0), ("gf", H)):
                    begin(name)
                    for k in range(KD):
                        last = t.matmul(bank(name, H, SPAN), wif[:, k, o:o + H], xT[:, k], start=k == 0, stop=k == KD - 1)
                    done(last)

                def project(name, u, jobs, kt_, rhs):
                    weights(name, u)
                    for j in range(2):
                        begin(jobs[j])
                        for k in range(kt_):
                            last = t.matmul(bank(jobs[j], P, SPAN), slot(name, u)[:, k, j * P:(j + 1) * P], rhs[:, k],
                                            start=k == 0, stop=k == kt_ - 1)
                        done(last)

                def rows(name, u, jobs, lhs):
                    weights(name, u)
                    for i in range(NCH):
                        begin(jobs[i])
                        for k in range(KD):
                            last = t.matmul(bank(jobs[i], P, WC), lhs[:, k, i * P:(i + 1) * P], slot(name, u)[:, k],
                                            start=k == 0, stop=k == KD - 1)
                        done(last)

                for name in ("mm", "hf", "hi", "hq", "hg", "mo"):
                    for u in range(2):
                        if name == "hi":
                            rows(name, u, [("hi", u, i) for i in range(NCH)], xT)
                        else:
                            project(name, u, [(name, 2 * u + j) for j in range(2)], KD, xT)
                pe.wait_ge(ev("conv_ready"), H)
                for h in range(H):
                    for name, w in (("qm", wq), ("km", wk)):
                        begin((name, h))
                        done(t.matmul(bank((name, h), QK, SPAN), w[:, h], conv[:, h], start=True, stop=True))
                for i in range(NCH):
                    begin(("kt", i))
                    for h in range(H):
                        last = t.matmul(bank(("kt", i))[:, h * QK:(h + 1) * QK], conv[:, h, i * P:(i + 1) * P], wk[:, h],
                                        start=True, stop=True)
                    done(last)
                    begin(("vm", i))
                    for h in range(H):
                        last = t.matmul(bank(("vm", i))[:, h * P:(h + 1) * P], mmT[:, h, 3 + i * P:3 + (i + 1) * P],
                                        wv[:, h], start=True, stop=True)
                    done(last)
                pe.wait_ge(ev("row_exps"), 1)
                begin("cols")
                for c in range(NCH):
                    for n, r in enumerate((rc, ra, rb, rd)):
                        o = (c * 4 + n) * H
                        last = t.transpose(bank("cols")[:, o:o + H], r[:, c * CH:(c + 1) * CH], ident[0:H, 0:H])
                done(last)
                begin("wp")
                pe.wait_ge(ev("dwp"), 1)
                done(t.matmul(bank("wp", QK, NCH * H), ones4[:], dwp[:].rearrange("p c h -> p (c h)"),
                              start=True, stop=True))
                pe.wait_ge(ev("kout"), 1)
                pe.wait_ge(ev("qin"), 1)
                pe.wait_ge(ev("vh"), 2 * NCH)
                pe.wait_ge(ev("qkm"), H)
                pe.wait_ge(ev("vm"), NCH)
                for c in range(NCH):
                    cs = slice(c * CH, (c + 1) * CH)
                    begin(("ko", c))
                    for h in range(H):
                        last = t.transpose(bank(("ko", c))[:, h * P:(h + 1) * P], kout[:, h, cs], ident[:])
                    done(last)
                    begin(("mb", c))
                    for h in range(H):
                        last = t.matmul(bank(("mb", c))[:, h * P:(h + 1) * P], sel[:, h], rm[:, cs], start=True, stop=True)
                    done(last)
                    begin(("sc", c))
                    pe.wait_ge(ev("kdec"), c + 1)
                    for h in range(H):
                        for i in range(NSUB):
                            last = t.matmul(bank(("sc", c))[:, h * P + i * SUB:h * P + (i + 1) * SUB], kdec[:, h, i],
                                            qdec[:, h, c * CH + i * SUB:c * CH + (i + 1) * SUB], start=True, stop=True)
                    done(last)
                    begin(("qk", c))
                    for h in range(H):
                        last = t.matmul(bank(("qk", c))[:, h * P:(h + 1) * P], km[:, h, cs], qm[:, h, cs],
                                        start=True, stop=True)
                    done(last)
                    begin(("oh", c))
                    if c:
                        pe.wait_ge(ev("sh_new"), c)
                    pe.wait_ge(ev("sct"), c + 1)
                    for h in range(H):
                        hv = slice(h * P, (h + 1) * P)
                        t.matmul(bank(("oh", c))[:, hv], qin[:, h, cs], sh[:, h], start=True, stop=False)
                        last = t.matmul(bank(("oh", c))[:, hv], sct[:, h], vh[:, c, hv], start=False, stop=True)
                    done(last)
                    begin(("ds", c))
                    pe.wait_ge(ev("ktok"), c + 1)
                    for h in range(H):
                        hv = slice(h * P, (h + 1) * P)
                        last = t.matmul(bank(("ds", c))[:, hv], ktok[:, h], vh[:, c, hv], start=True, stop=True)
                    done(last)
                    begin(("inter", c))
                    if c:
                        pe.wait_ge(ev("sm_new"), c)
                    for h in range(H):
                        last = t.matmul(two(("inter", c))[:, h // 2, h % 2], qm[:, h, cs], sm[:, h, 0:P + 1],
                                        start=True, stop=True)
                    done(last)
                    begin(("intra", c))
                    pe.wait_ge(ev("wgt"), c + 1)
                    for h in range(H):
                        last = t.matmul(two(("intra", c))[:, h // 2, h % 2], wgt[:, h], va[:, c, h, 0:P + 1],
                                        start=True, stop=True)
                    done(last)
                    begin(("dm", c))
                    pe.wait_ge(ev("kw"), c + 1)
                    for h in range(H):
                        last = t.matmul(two(("dm", c), QK)[:, h // 2, h % 2], kw[:, h], va[:, c, h, 0:P + 1],
                                        start=True, stop=True)
                    done(last)
                    begin(("yh", c))
                    pe.wait_ge(ev("oh_n"), c + 1)
                    for h in range(H):
                        last = t.transpose(bank(("yh", c))[:, h * P:(h + 1) * P], oh[:, h], ident[:])
                    done(last)
                    begin(("ym", c))
                    pe.wait_ge(ev("om_n"), c + 1)
                    for h in range(H):
                        last = t.transpose(bank(("ym", c))[:, h * P:(h + 1) * P], om[:, h], ident[:])
                    done(last)
                pe.wait_ge(ev("y_ready"), NCH)
                for m in range(4):
                    project("g0", m, [("g0", m, j) for j in range(2)], KD, xT)
                    project("b0", m, [("b0", m, j) for j in range(2)], H, sgh)
                    project("g1", m, [("g1", m, j) for j in range(2)], KD, xT)
                    project("b1", m, [("b1", m, j) for j in range(2)], H, smo)
                pe.wait_ge(ev("merged"), 8)
                for u in range(4):
                    rows("wo", u, [("wo", u, i) for i in range(NCH)], merged)
                pe.wait_ge(ev("xn_ready"), NCH)
                for k in range(KD):
                    begin(("nT", k))
                    for i in range(NCH):
                        last = t.transpose(bank(("nT", k))[:, i * P:(i + 1) * P], xrow[:, i, k * P:(k + 1) * P], ident[:])
                    done(last)
                pe.wait_ge(ev("nT"), KD)
                for i in range(NCH):
                    begin(("lg", i))
                    for k in range(KD):
                        last = t.matmul(bank(("lg", i), P, E), xT[:, k, i * P:(i + 1) * P], rw[:, k],
                                        start=k == 0, stop=k == KD - 1)
                    done(last)
                span_end(pe, s)

        @block.sync
        def _(sp):
            for dst, src in small:
                sp.dma_start(dst, src, allow_slow_non_contiguous=True).then_inc(ev("smallw"), 16)
            setup = {"const", "smallw", "lbs", "lbd", "oml", "pool_const", "span_ended", "span_cleared", "span_clearing"}
            with sp.Fori(0, NSPAN) as s:
                sp.dma_start(xrow[:], xin[:, bass.ds(s * NCH, NCH), :]).then_inc(ev("x_loaded"), 16)
                for n, (name, u, c0) in enumerate(L):
                    src = {"b0": wbh, "b1": wbm, "wo": w_out}.get(name, w_in)
                    kt_ = H if name in ("b0", "b1") else KD
                    if n >= NRING:
                        sp.wait_ge(ev("ps_ready"), J.ready(last_use(*L[n - NRING][0:2])))
                    sp.dma_start(ring[:, n % NRING, 0:kt_, :], src[:, :, c0:c0 + WC]).then_inc(ev(f"w_loaded{n % NRING}"), 16)
                sp.wait_ge(ev("h_ready"), 1)
                sp.dma_start(hrows[:, bass.ds(s * NCH, NCH), :], xs).then_inc(ev("rows_stored"), 16)
                sp.wait_ge(ev("xn_ready"), NCH)
                sp.dma_start(nrows[:, bass.ds(s * NCH, NCH), :], xrow[:]).then_inc(ev("rows_stored"), 16)
                sp.wait_ge(ev("rows_stored"), 32)
                sp.nop().then_inc(ev("span_ended"), 1)
                sp.wait_ge(ev("span_ended"), ENGINES * (s + 1))
                sp.nop().then_inc(ev("span_clearing"), 1)
                for name in [m for m in ev.made if m not in setup]:
                    sp.sem_clear(ev(name))
                sp.nop().then_inc(ev("span_cleared"), 1)


def from_routing(nc, ins, d, lg, ident, ev, out):
    with ExitStack() as ctx:
        def sb(name, shape, dt=F32):
            return ctx.enter_context(nc.sbuf_tensor(name, shape, dt))

        dest = sb("dest", [P, TOPK, NT], I32)
        gw = sb("gw", [P, NT, TOPK])
        npass = sb("npass", [1, 2, E], I32)
        bparts = sb("bparts", [2 * E, 2 * FF], R32)
        pickf = sb("pickf", [2 * E, E])
        eps2 = sb("eps2", [P, 1])
        routing(nc, ins, d, lg, ident, ev, dest, gw, npass, bparts, pickf, eps2)
        experts(nc, ins, d, ident, ev, npass, bparts, pickf)
        combine(nc, ins, d, ev, dest, gw, eps2, out)


def routing(nc, ins, d, lg, ident, ev, dest, gw, npass, bparts, pickf, eps2):
    with ExitStack() as ctx:
        def sb(name, shape, dt=F32):
            return ctx.enter_context(nc.sbuf_tensor(name, shape, dt))

        top, topi, topf = sb("top", [P, NT, 8]), sb("topi", [P, NT, 8], U32), sb("topf", [P, NT, 8])
        iota_i, iota = sb("iota_i", [P, E], I32), sb("iota", [P, E])
        ebase = sb("ebase", [P, E])
        hot = sb("hot", [P, TOPK, NT, E])
        chosen = sb("chosen", [P, NT, E])
        before = sb("before", [P, NT + 1, E])
        prod = sb("prod", [P, NT, E])
        destf = sb("destf", [P, TOPK, NT])
        wsum = sb("wsum", [P, NT, 1])
        tri, ones = sb("tri", [P, P]), sb("ones", [P, P])
        rowid = sb("rowid", [P, TOPK, NT, 2], I32)
        blank = sb("blank", [P, TAB // P, 2], I32)
        cntf = sb("cntf", [1, 3, E])
        hrow = sb("hrow", [P, NT, D])
        share = sb("share", [P, NT, E])
        shareT = sb("shareT", [E, NT, P])
        bgu, bdn = sb("bgu", [2 * E, 2 * FF]), sb("bdn", [E, D])
        ps = ctx.enter_context(nc.psum_tensor("rps", [P, 8, 512], F32))
        hrows = d["h"][LEAD:ROWS].rearrange("(i p) n -> p i n", p=P)
        hbrows = d["hb"].rearrange("(i p) n -> p i n", p=P)
        block = ctx.enter_context(nc.Block())

        @block.sync
        def _(sp):
            for r in range(2):
                sp.dma_start(bgu[r * E:(r + 1) * E, :], ins["exp_b_gu"].rearrange("l e n -> (l e) n"))\
                    .then_inc(ev("biases"), 16)
            sp.dma_start(bdn[:], ins["exp_b_down"].rearrange("l e n -> (l e) n")).then_inc(ev("biases"), 16)
            sp.dma_start(hrow[:], hrows).then_inc(ev("hrow"), 16)
            sp.wait_ge(ev("r_blank"), 2)
            sp.dma_start(d["table"].rearrange("(p n) o -> p (n o)", p=P),
                         blank[:].rearrange("p n o -> p (n o)")).then_inc(ev("table_blank"), 16)
            sp.wait_ge(ev("hb_made"), 2 * NT)
            sp.dma_start(hbrows, hrow[:]).then_inc(ev("hb_stored"), 16)
            sp.wait_ge(ev("hb_stored"), 16)

        @block.gpsimd
        def _(pool):
            g = nc.gpsimd
            g.memset(blank[:, :, 0:1], 0).then_inc(ev("r_blank"), 1)
            g.memset(blank[:, :, 1:2], NOROW).then_inc(ev("r_blank"), 1)
            g.iota(iota_i[:], pattern=[[1, E]], base=0, channel_multiplier=0).then_inc(ev("r_iota"), 1)
            for k in range(TOPK):
                g.iota(rowid[:, k, :, 0:1], pattern=[[P, NT], [0, 1]], base=LEAD, channel_multiplier=1)\
                    .then_inc(ev("rowid"), 1)
                g.iota(rowid[:, k, :, 1:2], pattern=[[P, NT], [0, 1]], base=k * SEQ, channel_multiplier=1)\
                    .then_inc(ev("rowid"), 1)
            g.memset(eps2[:], EPS)
            g.memset(ones[:], 1.0).then_inc(ev("r_const"), 1)
            g.memset(tri[:], 1.0).then_inc(ev("r_const"), 1)
            pool.wait_ge(ev("r_const"), 2)
            g.affine_select(out=tri[:], in_=tri[:], compare_op=ALU.is_gt, fill=0.0, base=0,
                            pattern=[[1, P]], channel_multiplier=-1).then_inc(ev("r_const"), 1)
            pool.wait_ge(ev("table_blank"), 16)
            pool.wait_ge(ev("dest"), 1)
            pool.wait_ge(ev("rowid"), 2 * TOPK)
            for k in range(TOPK):
                for i in range(NT):
                    g.indirect_dma_start(out=d["table"], out_offset=bass.IndirectOffsetOnAxis(ap=dest[:, k, i:i + 1], axis=0),
                                         in_=rowid[:, k, i], in_offset=None).then_inc(ev("table"), 16)
            pool.wait_ge(ev("table"), 16 * TOPK * NT)

        @block.vector
        def _(dve):
            v = nc.vector
            n = [0]

            def link(ins_):
                n[0] += 1
                ins_.then_inc(ev("r_step"), 1)
                dve.wait_ge(ev("r_step"), n[0])

            for i in range(NT):
                link(v.max(top[:, i], lg[:, NSPAN * NCH - NT + i]))
                link(v.max_index(topi[:, i], top[:, i], lg[:, NSPAN * NCH - NT + i]))
            link(v.tensor_copy(topf[:], topi[:]))
            dve.wait_ge(ev("r_iota"), 1)
            link(v.tensor_copy(iota[:], iota_i[:]))
            link(v.tensor_scalar(ebase[:], iota[:], float(CAP), None, ALU.mult))
            every = iota[:].rearrange("p (o e) -> p o e", o=1).broadcast_to([P, NT, E])
            for k in range(TOPK):
                link(v.tensor_tensor(hot[:, k], every, topf[:, :, k:k + 1].broadcast_to([P, NT, E]), ALU.is_equal))
            link(v.tensor_tensor(chosen[:], hot[:, 0], hot[:, 1], ALU.add))
            for k in range(2, TOPK):
                link(v.tensor_tensor(chosen[:], chosen[:], hot[:, k], ALU.add))
            link(v.memset(before[:, 0], 0.0))
            for i in range(NT):
                link(v.tensor_tensor(before[:, i + 1], before[:, i], chosen[:, i], ALU.add))
            dve.sem_inc(ev("chosen"), 1)
            link(v.tensor_tensor(gw[:], top[:, :, 0:TOPK], top[:, :, 0:1].broadcast_to([P, NT, TOPK]), ALU.subtract))
            dve.sem_inc(ev("gw_arg"), 1)
            dve.wait_ge(ev("gw_exp"), 1)
            link(v.tensor_reduce(wsum[:].rearrange("p t o -> p (t o)"), gw[:], AX.X, ALU.add))
            link(v.reciprocal(wsum[:], wsum[:]))
            link(v.tensor_tensor(gw[:], gw[:], wsum[:].broadcast_to([P, NT, TOPK]), ALU.mult))
            dve.wait_ge(ev("ranks"), 1)
            rank = ps[:, 0, 0:NT * E].rearrange("p (t e) -> p t e", e=E)
            link(v.tensor_tensor(before[:, 0:NT], rank, ebase[:].rearrange("p (o e) -> p o e", o=1)
                                 .broadcast_to([P, NT, E]), ALU.add))
            for k in range(TOPK):
                link(v.tensor_tensor(prod[:], hot[:, k], before[:, 0:NT], ALU.mult))
                link(v.tensor_reduce(destf[:, k], prod[:], AX.X, ALU.add))
            link(v.tensor_copy(dest[:], destf[:]))
            dve.sem_inc(ev("dest"), 1)
            link(v.tensor_copy(cntf[:, 0], ps[0:1, 1, 0:E]))
            link(v.memset(cntf[:, 1], 0.0))
            link(v.memset(cntf[:, 2], 1.0))
            for m in range(NPASS):
                link(v.scalar_tensor_tensor(cntf[:, 1], cntf[:, 0], float(P + m * 2 * P), cntf[:, 1],
                                            ALU.is_gt, ALU.add))
                if m:
                    link(v.scalar_tensor_tensor(cntf[:, 2], cntf[:, 0], float(m * 2 * P), cntf[:, 2],
                                                ALU.is_gt, ALU.add))
            link(v.tensor_tensor(cntf[:, 2], cntf[:, 2], cntf[:, 1], ALU.subtract))
            link(v.tensor_copy(npass[:], cntf[:, 1:3]))
            dve.wait_ge(ev("biases"), 48)
            link(v.tensor_scalar(bgu[:, 1:2 * FF:2], bgu[:, 1:2 * FF:2], 1.0, None, ALU.add))
            link(v.tensor_copy(bparts[:], bgu[:]))
            link(v.tensor_tensor(bparts[E:2 * E, :], bgu[E:2 * E, :], bparts[E:2 * E, :].bitcast(F32), ALU.subtract))
            for r in range(2):
                link(v.tensor_copy(pickf[r * E:(r + 1) * E, :], ident[0:E, 0:E]))
            for k in range(TOPK):
                dst = share if k == 0 else prod
                link(v.tensor_tensor(dst[:], hot[:, k], gw[:, :, k:k + 1].broadcast_to([P, NT, E]), ALU.mult))
                if k:
                    link(v.tensor_tensor(share[:], share[:], prod[:], ALU.add))
            dve.sem_inc(ev("share"), 1)
            dve.wait_ge(ev("shareT_ps"), 1)
            for q in range(2):
                link(v.tensor_copy(shareT[:, 4 * q:4 * q + 4].rearrange("e i p -> e (i p)"), ps[0:E, 4 + q]))
            dve.sem_inc(ev("shareT"), 1)
            dve.wait_ge(ev("hrow"), 16)
            for m in range(2 * NT):
                dve.wait_ge(ev("hb_ps"), m + 1)
                half = hrow[:, m // 2, (m % 2) * 512:(m % 2 + 1) * 512]
                link(v.tensor_tensor(half, half, ps[:, 6 + m % 2], ALU.add))
                dve.sem_inc(ev("hb_made"), 1)

        @block.scalar
        def _(act):
            act.wait_ge(ev("gw_arg"), 1)
            nc.scalar.activation(gw[:], gw[:], ACT.Exp).then_inc(ev("gw_exp"), 1)

        @block.tensor
        def _(pe):
            t = nc.tensor
            pe.wait_ge(ev("biases"), 48)
            pe.wait_ge(ev("chosen"), 1)
            pe.wait_ge(ev("r_const"), 3)
            for i in range(NT):
                o = ps[:, 0, i * E:(i + 1) * E]
                t.matmul(o, tri[:], chosen[:, i], start=True, stop=False)
                t.matmul(o, ones[:], before[:, i], start=False, stop=True)
            t.matmul(ps[:, 1, 0:E], ones[:], before[:, NT], start=True, stop=True).then_inc(ev("ranks"), 1)
            pe.wait_ge(ev("share"), 1)
            for i in range(NT):
                last = t.transpose(ps[0:E, 4 + i // 4, (i % 4) * P:(i % 4 + 1) * P], share[:, i], ident[:])
            last.then_inc(ev("shareT_ps"), 1)
            pe.wait_ge(ev("shareT"), 1)
            for n in range(2 * NT):
                if n >= 2:
                    pe.wait_ge(ev("hb_made"), n - 1)
                t.matmul(ps[:, 6 + n % 2], shareT[:, n // 2], bdn[:, (n % 2) * 512:(n % 2 + 1) * 512],
                         start=True, stop=True).then_inc(ev("hb_ps"), 1)


def experts(nc, ins, d, ident, ev, npass, bparts, pickf):
    with ExitStack() as ctx:
        def sb(name, shape, dt=F32):
            return ctx.enter_context(nc.sbuf_tensor(name, shape, dt))

        PC, KH = 512, KD // 2
        NPIECE = 4
        ITEMS = [(p, kh) for p in range(NPIECE) for kh in range(2)] + [(4, 0), (5, 0), (4, 1), (5, 1)]
        NI = len(ITEMS)
        NRAW, NHL, AHEAD = 4, 6, 5

        def turned(nb):
            return (2, 4, 6, 8)

        LIMU = LIMIT + 1.0

        raw = sb("raw", [P, NRAW, KH, PC])
        whi, wlo = sb("whi", [P, NHL, KH, PC], R32), sb("wlo", [P, NHL, KH, PC], R32)
        ids = [sb(f"ids{b}", [P, 2], I32) for b in "AB"]
        to = [sb(f"to{b}", [P, 1], I32) for b in "AB"]
        xg = [sb(f"xg{b}", [P, D]) for b in "AB"]
        xhi, xlo = ([sb(f"{n}{b}", [P, KD, P], R32) for b in "AB"] for n in ("xhi", "xlo"))
        sg, am = ([sb(f"{n}{b}", [P, 2, PC // 2]) for b in "AB"] for n in ("sg", "am"))
        u_ = [sb(f"u{b}", [P, PC // 2]) for b in "AB"]
        ahi, alo = ([sb(f"{n}{b}", [P, KD, P], R32) for b in "AB"] for n in ("ahi", "alo"))
        y_ = [sb(f"y{b}", [P, D]) for b in "AB"]
        pick = sb("pick", [2 * E, P], R32)
        ps = ctx.enter_context(nc.psum_tensor("eps", [P, 8, 512], F32))

        def mm_bank(piece, b):
            return ps[:, 2 * (piece % 3) + b]

        def t_bank(b):
            return ps[:, 6 + b]

        SMAX = float(1.0 / (1.0 + np.exp(-ALPHA * LIMIT)))

        def gu_bank(nb, p, b):
            return t_bank(b if nb == 2 else p % 2)

        wgu_v = ins["exp_w_gu"].rearrange("l e (k p) n -> p (l e) k n", p=P)
        wdn_v = ins["exp_w_down"].rearrange("l e (k p) n -> p (l e) k n", p=P)

        def over_passes(eng, name, body):
            reg = eng.alloc_register(name)
            eng.reg_mov(reg, 0)
            most = E * NPASS
            with eng.Fori(0, E) as e:
                two = eng.value_load(npass[0:1, 0, bass.ds(e, 1)], min_val=0, max_val=NPASS)
                one = eng.value_load(npass[0:1, 1, bass.ds(e, 1)], min_val=0, max_val=1)
                with eng.If(two > 0):
                    with eng.Fori(0, two) as i:
                        body(e, 2, eng.snap(reg, min_val=0, max_val=most), e * CAP + i * 2 * P)
                        eng.reg_add(reg, reg, 1)
                with eng.Else():
                    eng.nop()
                with eng.If(one > 0):
                    body(e, 1, eng.snap(reg, min_val=0, max_val=most), e * CAP + two * 2 * P)
                    eng.reg_add(reg, reg, 1)
                with eng.Else():
                    eng.nop()
            return eng.snap(reg, min_val=0, max_val=most)

        def step(ins_, name, b, nb, extra=1):
            ins_.then_inc(ev(name), 1 if nb == 2 else 1 + (extra if b == 0 else 0))

        block = ctx.enter_context(nc.Block())

        @block.sync
        def _(sp):
            def load(e, n):
                p, kh = ITEMS[n]
                ks = slice(kh * KH, (kh + 1) * KH)
                if p < NPIECE:
                    src = wgu_v[:, bass.ds(e, 1), ks, p * PC:(p + 1) * PC]
                else:
                    src = wdn_v[:, bass.ds(e, 1), ks, (p - NPIECE) * PC:(p - NPIECE + 1) * PC]
                sp.dma_start(raw[:, n % NRAW], src.rearrange("p o k n -> p (o k) n")).then_inc(ev(f"raw{n % NRAW}"), 16)

            def body(e, nb, ps_, row0):
                for n in range(NI):
                    sp.wait_ge(ev("lo_made"), ps_ * NI + n + 1)
                    sp.nop().then_inc(ev("sp_turn"), 1)
                    load(e, n)

            total = over_passes(sp, "sp_pass", body)
            for n in range(AHEAD):
                sp.wait_ge(ev("lo_made"), total * NI + n + 1)
                sp.nop().then_inc(ev("sp_turn"), 1)
                load(0, n)

        @block.gpsimd
        def _(pool):
            g = nc.gpsimd

            def turn():
                pool.nop().then_inc(ev("pool_turn"), 1)

            def gather():
                for b in range(2):
                    g.indirect_dma_start(out=xg[b][:], out_offset=None, in_=d["xn"],
                                         in_offset=bass.IndirectOffsetOnAxis(ap=ids[b][:, 0:1], axis=0))\
                        .then_inc(ev("gathered"), 16)

            def store_rows():
                for b in range(2):
                    g.indirect_dma_start(out=d["y"], out_offset=bass.IndirectOffsetOnAxis(ap=to[b][:], axis=0),
                                         in_=y_[b][:], in_offset=None, bounds_check=TOPK * SEQ - 1,
                                         oob_is_err=False).then_inc(ev("y_stored"), 16)

            def body(e, nb, ps_, row0):
                for b in range(2):
                    g.dma_start(ids[b][:], d["table"][bass.ds(row0 + b * P, P), :]).then_inc(ev("ids"), 16)
                pool.wait_ge(ev("ids"), ps_ * 32 + 32)
                pool.wait_ge(ev("x_trans"), ps_ * 4 + 4)
                turn()
                gather()
                pool.wait_ge(ev("y_made"), ps_ * 4 + 4)
                turn()
                store_rows()
                pool.wait_ge(ev("y_stored"), ps_ * 32 + 32)
                turn()
                for b in range(2):
                    if b < nb:
                        g.tensor_copy(to[b][:], ids[b][:, 1:2]).then_inc(ev("to_set"), 1)
                    else:
                        g.memset(to[b][:], NOROW).then_inc(ev("to_set"), 1)
                pool.wait_ge(ev("to_set"), ps_ * 2 + 4)
                pool.wait_ge(ev("gathered"), ps_ * 32 + 32)
                turn()

            for b in range(2):
                g.memset(to[b][:], NOROW).then_inc(ev("to_set"), 1)
                g.memset(y_[b][:], 0.0).then_inc(ev("y_blank"), 1)
            pool.wait_ge(ev("to_set"), 2)
            pool.wait_ge(ev("y_blank"), 2)
            total = over_passes(pool, "pool_pass", body)
            pool.wait_ge(ev("x_trans"), total * 4 + 4)
            turn()
            gather()
            pool.wait_ge(ev("y_made"), total * 4 + 4)
            turn()
            store_rows()
            pool.wait_ge(ev("y_stored"), total * 32 + 32)
            pool.wait_ge(ev("gathered"), total * 32 + 32)
            turn()

        @block.tensor
        def _(pe):
            t = nc.tensor

            def turn():
                pe.nop().then_inc(ev("pe_turn"), 1)

            def x_transposes(ps_, b):
                for half in range(2):
                    if b:
                        pe.wait_ge(ev("x_lo"), ps_ * 4 + 1 + half)
                        turn()
                    for k in range(KH):
                        kk = half * KH + k
                        last = t.transpose(t_bank(half)[:, k * P:(k + 1) * P], xg[b][:, kk * P:(kk + 1) * P], ident[:])
                    last.then_inc(ev("x_trans"), 1)

            def body(e, nb, ps_, row0):
                def item(n, b):
                    p, kh = ITEMS[n]
                    hi, lo = (xhi[b], xlo[b]) if p < NPIECE else (ahi[b], alo[b])
                    o = mm_bank(p, b)
                    last_item = kh == 1 and p >= NPIECE
                    for part in range(3):
                        if n < 2:
                            pe.wait_ge(ev("x_lo" if part == 2 else "x_hi"), ps_ * 4 + 2 * b + n + 1)
                        elif n >= 8 and part != 1:
                            pe.wait_ge(ev("a_lo" if part == 2 else "a_hi"), ps_ * 8 + (4 if kh == 0 else 8))
                        for k in range(KH):
                            kk = kh * KH + k
                            last = t.matmul(o, (lo if part == 2 else hi)[:, kk],
                                            (wlo if part == 1 else whi)[:, n % NHL, k],
                                            start=kh == 0 and part == 0 and k == 0,
                                            stop=last_item and part == 2 and k == KH - 1)
                    if kh == 1 and p < NPIECE:
                        pe.wait_ge(ev("picked"), ps_ + 1)
                        last = t.matmul(o, pick[:], bparts[:, p * PC:(p + 1) * PC], start=False, stop=True)
                    step(last, "mm_done", b, nb)

                def a_transposes(p):
                    for b in range(nb):
                        pe.wait_ge(ev("a_made"), ps_ * 8 + 2 * p + b + 1)
                        if p == 0:
                            pe.wait_ge(ev("x_lo"), ps_ * 4 + 4)
                        before = p - (1 if nb == 2 else 2)
                        if before >= 0:
                            pe.wait_ge(ev("a_lo"), ps_ * 8 + 2 * before + b + 1)
                        turn()
                        for q in range(2):
                            last = t.transpose(gu_bank(nb, p, b)[:, q * P:(q + 1) * P],
                                               am[b][:, p % 2, q * P:(q + 1) * P], ident[:])
                        step(last, "a_trans", b, nb)

                for n in range(NI):
                    if n == 2:
                        pe.wait_ge(ev("y_made"), ps_ * 4 + 2)
                    if n == 4:
                        pe.wait_ge(ev("y_made"), ps_ * 4 + 4)
                    pe.wait_ge(ev("lo_made"), ps_ * NI + NRAW + n + 1)
                    for b in range(nb):
                        item(n, b)
                    if n in turned(nb):
                        a_transposes(turned(nb).index(n))
                    if n == 10:
                        pe.wait_ge(ev("gathered"), (ps_ + 1) * 32 + 32)
                        pe.wait_ge(ev("a_lo"), ps_ * 8 + 8)
                        turn()
                    if n >= 10:
                        x_transposes(ps_ + 1, n - 10)

            pe.sem_inc(ev("x_trans"), 4)
            pe.sem_inc(ev("mm_done"), 2)
            pe.wait_ge(ev("gathered"), 32)
            for b in range(2):
                x_transposes(0, b)
            over_passes(pe, "pe_pass", body)

        @block.scalar
        def _(act):
            a = nc.scalar

            def split(value, n):
                act.wait_ge(ev(f"raw{n % NRAW}"), value["raw"])
                if value["mm"] is not None:
                    act.wait_ge(ev("mm_done"), value["mm"])
                a.copy(whi[:, n % NHL], raw[:, n % NRAW]).then_inc(ev("hi_made"), 1)

            def x_split(ps_, b):
                for half in range(2):
                    act.wait_ge(ev("x_trans"), ps_ * 4 + 2 * b + half + 5)
                    a.copy(xhi[b][:, half * KH:(half + 1) * KH].rearrange("p k n -> p (k n)"), t_bank(half))\
                        .then_inc(ev("x_hi"), 1)

            def body(e, nb, ps_, row0):
                def ahead(n):
                    m = n + AHEAD
                    split({"raw": 16 * (ps_ * (NI // NRAW) + m // NRAW + 1), "mm": ps_ * 24 + 2 * (m - NHL) + 4}, m)

                for n in range(NI):
                    ahead(n)
                    if n in (1, 3, 5, 7):
                        p = n // 2
                        for b in range(nb):
                            act.wait_ge(ev("mm_done"), ps_ * 24 + 2 * n + b + 3)
                            step(a.activation(sg[b][:, p % 2], mm_bank(p, b)[:, 0:PC:2], ACT.Sigmoid, scale=ALPHA),
                                 "sg_made", b, nb)
                    if n in turned(nb):
                        p = turned(nb).index(n)
                        for b in range(nb):
                            act.wait_ge(ev("a_trans"), ps_ * 8 + 2 * p + b + 1)
                            step(a.copy(ahi[b][:, 2 * p:2 * p + 2].rearrange("p k n -> p (k n)"),
                                        gu_bank(nb, p, b)[:, 0:2 * P]), "a_hi", b, nb)
                    if n >= 10:
                        x_split(ps_ + 1, n - 10)
                        if n == 10:
                            act.wait_ge(ev("y_stored"), ps_ * 32 + 32)
                        q = n - 10
                        for b in range(nb):
                            act.wait_ge(ev("mm_done"), ps_ * 24 + 2 * n + b + 3)
                            step(a.copy(y_[b][:, q * PC:(q + 1) * PC], mm_bank(4 + q, b)), "y_made", b, nb)

            act.sem_inc(ev("y_made"), 4)
            for n in range(AHEAD):
                split({"raw": 16 * (n // NRAW + 1), "mm": None}, n)
            for b in range(2):
                x_split(0, b)
            over_passes(act, "act_pass", body)

        @block.vector
        def _(dve):
            v = nc.vector

            def split(n, value):
                dve.wait_ge(ev("hi_made"), value)
                v.tensor_tensor(wlo[:, n % NHL], raw[:, n % NRAW], whi[:, n % NHL].bitcast(F32), ALU.subtract)\
                    .then_inc(ev("lo_made"), 1)

            def x_rest(ps_, b):
                for half in range(2):
                    dve.wait_ge(ev("x_hi"), ps_ * 4 + 2 * b + half + 1)
                    hs = slice(half * KH, (half + 1) * KH)
                    v.tensor_tensor(xlo[b][:, hs].rearrange("p k n -> p (k n)"), t_bank(half),
                                    xhi[b][:, hs].rearrange("p k n -> p (k n)").bitcast(F32), ALU.subtract)\
                        .then_inc(ev("x_lo"), 1)

            def body(e, nb, ps_, row0):
                def ahead(n):
                    m = n + AHEAD
                    split(m, ps_ * NI + m + 1)

                v.tensor_copy(pick[:], pickf[:, bass.ds(e, 1)].broadcast_to([2 * E, P])).then_inc(ev("picked"), 1)

                def product(p, b):
                    g, up = mm_bank(p, b)[:, 0:PC:2], mm_bank(p, b)[:, 1:PC:2]
                    dve.wait_ge(ev("sg_made"), ps_ * 8 + 2 * p + b + 1)
                    step(v.tensor_scalar(u_[b][:], up, LIMU, 2.0 - LIMU, ALU.min, ALU.max), "u_made", b, nb)
                    dve.wait_ge(ev("u_made"), ps_ * 8 + 2 * p + b + 1)
                    step(v.scalar_tensor_tensor(u_[b][:], g, LIMIT, u_[b][:], ALU.min, ALU.mult), "ug_made", b, nb)
                    dve.wait_ge(ev("ug_made"), ps_ * 8 + 2 * p + b + 1)
                    step(v.scalar_tensor_tensor(am[b][:, p % 2], sg[b][:, p % 2], SMAX, u_[b][:], ALU.min, ALU.mult),
                         "a_made", b, nb)

                def rest(p, b):
                    dve.wait_ge(ev("a_hi"), ps_ * 8 + 2 * p + b + 1)
                    step(v.tensor_tensor(alo[b][:, 2 * p:2 * p + 2].rearrange("p k n -> p (k n)"),
                                         gu_bank(nb, p, b)[:, 0:2 * P],
                                         ahi[b][:, 2 * p:2 * p + 2].rearrange("p k n -> p (k n)").bitcast(F32),
                                         ALU.subtract), "a_lo", b, nb)

                for n in range(NI):
                    ahead(n)
                    if n in (1, 3, 5, 7):
                        for b in range(nb):
                            product(n // 2, b)
                    if n in turned(nb):
                        for b in range(nb):
                            rest(turned(nb).index(n), b)
                    if n >= 10:
                        x_rest(ps_ + 1, n - 10)

            dve.sem_inc(ev("lo_made"), NRAW)
            for n in range(AHEAD):
                split(n, n + 1)
            for b in range(2):
                x_rest(0, b)
            over_passes(dve, "dve_pass", body)


def combine(nc, ins, d, ev, dest, gw, eps2, out):
    with ExitStack() as ctx:
        def sb(name, shape, dt=F32):
            return ctx.enter_context(nc.sbuf_tensor(name, shape, dt))

        NBUF = 4
        yg = sb("yg", [P, NBUF, TOPK, D])
        acc = sb("acc", [P, NBUF, D])
        sq = sb("sq", [P, D])
        nfin = sb("nfin", [P, D])
        s2 = sb("s2", [P, NT, 2])
        block = ctx.enter_context(nc.Block())
        hrows = d["hb"].rearrange("(i p) n -> i p n", p=P)
        yrows = d["y"].rearrange("(k i p) n -> i p k n", k=TOPK, p=P)
        orows = out.rearrange("(i p) n -> i p n", p=P)

        @block.sync
        def _(sp):
            sp.dma_start(nfin[:], ins["norm_final"].rearrange("(o n) -> o n", o=1).broadcast_to([P, D])).then_inc(ev("nfin"), 16)
            for i in range(NT):
                if i >= NBUF:
                    sp.wait_ge(ev(f"out_stored{i % NBUF}"), 16 * (i // NBUF))
                sp.dma_start(acc[:, i % NBUF], hrows[i]).then_inc(ev(f"hl{i % NBUF}"), 16)
                sp.dma_start(yg[:, i % NBUF], yrows[i]).then_inc(ev(f"yg{i % NBUF}"), 16)
                if i >= 1:
                    sp.wait_ge(ev("final"), i)
                    sp.dma_start(orows[i - 1], acc[:, (i - 1) % NBUF]).then_inc(ev(f"out_stored{(i - 1) % NBUF}"), 16)
            sp.wait_ge(ev("final"), NT)
            sp.dma_start(orows[NT - 1], acc[:, (NT - 1) % NBUF]).then_inc(ev(f"out_stored{(NT - 1) % NBUF}"), 16)
            for b in range(NBUF):
                sp.wait_ge(ev(f"out_stored{b}"), 16 * (NT // NBUF))

        @block.vector
        def _(dve):
            v = nc.vector
            n = [0]

            def link(ins_):
                n[0] += 1
                ins_.then_inc(ev("c_step"), 1)
                dve.wait_ge(ev("c_step"), n[0])

            dve.wait_ge(ev("nfin"), 16)
            for i in range(NT):
                b = i % NBUF
                dve.wait_ge(ev(f"hl{b}"), 16 * (i // NBUF + 1))
                dve.wait_ge(ev(f"yg{b}"), 16 * (i // NBUF + 1))
                for k in range(TOPK):
                    link(v.scalar_tensor_tensor(acc[:, b], yg[:, b, k], gw[:, i, k:k + 1], acc[:, b], ALU.mult, ALU.add))
                dve.sem_inc(ev("summed"), 1)
                dve.wait_ge(ev("c_rms"), i + 1)
                link(v.reciprocal(s2[:, i, 1:2], s2[:, i, 0:1]))
                link(v.scalar_tensor_tensor(acc[:, b], acc[:, b], s2[:, i, 1:2], nfin[:], ALU.mult, ALU.mult))
                dve.sem_inc(ev("final"), 1)

        @block.scalar
        def _(act):
            a = nc.scalar
            for i in range(NT):
                act.wait_ge(ev("summed"), i + 1)
                a.activation(sq[:], acc[:, i % NBUF], ACT.Square, accum_out=s2[:, i, 0:1]).then_inc(ev("c_sq"), 1)
                act.wait_ge(ev("c_sq"), i + 1)
                a.activation(s2[:, i, 0:1], s2[:, i, 0:1], ACT.Sqrt, scale=1.0 / D, bias=eps2[:, 0:1]).then_inc(ev("c_rms"), 1)


_SMALL = ["hg_lb_logits", "norm_mix", "w_in", "hg_norm", "ml_conv_w", "ml_conv_b", "ml_wq", "ml_wk", "ml_wv",
          "ml_gate_b", "ml_norm", "ml_skip", "w_branch_hg", "w_branch_ml", "w_out", "norm_ffn", "router_w",
          "router_b", "exp_w_gu", "exp_b_gu", "exp_w_down", "exp_b_down", "norm_final"]


def kernel(**inputs):
    import concourse.bacc as bacc
    from concourse.bass_utils import run_bass_kernel_spmd

    nc = bacc.Bacc("TRN2", target_bir_lowering=False, num_devices=1)
    arrays = {n: np.ascontiguousarray(inputs[n]) for n in _SMALL}
    x, meta = np.asarray(inputs["x"]), np.asarray(inputs["meta_tokens"])
    arrays["rows"] = np.concatenate([np.zeros((PAD, D), x.dtype), meta, x[0]], axis=0)
    ins = {n: nc.dram_tensor(n, a.shape, mybir.dt.from_np(a.dtype), kind="ExternalInput").ap() for n, a in arrays.items()}
    out = nc.dram_tensor("out", [SEQ, D], F32, kind="ExternalOutput").ap()
    build(nc, ins, out)
    r = run_bass_kernel_spmd(nc, [arrays], core_ids=[0])
    return r.results[0]["out"].reshape(1, SEQ, D)
```

```python
import numpy as np
import concourse.bass as bass
from concourse import mybir
from contextlib import ExitStack

F32 = mybir.dt.float32
R32 = mybir.dt.float32r
I32 = mybir.dt.int32
U32 = mybir.dt.uint32
ALU = mybir.AluOpType
ACT = mybir.ActivationFunctionType
AX = mybir.AxisListType

P = 128
D = 1024
KD = D // P
META, SEQ = 16, 1024
CH = 128
NCH = 3
SPAN = NCH * CH
NSPAN = 3
ROWS = NSPAN * SPAN
LEAD = ROWS - SEQ
PAD = LEAD - META
H = 4
W = 512
QK = 64
SUB = 16
NSUB = CH // SUB
EPS = 1e-6
NEG = -1e30
BIG = 1e34

E = 32
TOPK = 4
FF = 1024
CAP = 1024
NT = SEQ // P
NPASS = CAP // (2 * P)
TAB = E * CAP + 256
LIMIT, ALPHA = 7.0, 1.702
NOROW = 1 << 20

WC = 256
SPLIT = ("mm", "hf", "hi", "hq", "hg", "mo", "g0", "g1")
NRING = 4
C_HQ, C_HF, C_HI, C_HG, C_MM, C_MO, C_IF, C_G0 = 0, 512, 1024, 1536, 2048, 2560, 3072, 3080
C_G1 = C_G0 + D


class Events:

    def __init__(self, nc, ctx):
        self.nc, self.ctx, self.made = nc, ctx, {}

    def __call__(self, name):
        if name not in self.made:
            self.made[name] = self.ctx.enter_context(self.nc.semaphore(name))
        return self.made[name]


class Banks:

    def __init__(self, nbanks):
        self.n, self.at, self.jobs, self.count, self.owner = nbanks, 0, {}, {"A": 0, "D": 0}, {}
        self.total = 0

    def add(self, name, engine, width=1):
        at = self.at if self.at + width <= self.n else 0
        before = [self.owner[b] for b in range(at, at + width) if b in self.owner]
        waits = {}
        for e, c in before:
            waits[e] = max(waits.get(e, 0), c)
        self.count[engine] += 1
        self.total += 1
        for b in range(at, at + width):
            self.owner[b] = (engine, self.count[engine])
        self.at = at + width
        self.jobs[name] = (at, self.total, waits, engine)

    def bank(self, name):
        return self.jobs[name][0]

    def ready(self, name):
        return self.jobs[name][1]


def turned_after(u):
    return range(max(2 * u - 2, 0), 2 * u if u < 3 else 8)


def span_jobs():
    b = Banks(8)
    for k in range(KD):
        b.add(("xT", k), "D")
    b.add("gi", "D")
    b.add("gf", "D")
    for j in range(H):
        b.add(("mm", j), "D")
    for j in range(H):
        b.add(("hf", j), "A")
    for u in range(4):
        for i in range(NCH):
            b.add(("hi", u, i), "A")
    for j in range(H):
        b.add(("hq", j), "D")
    for j in range(H):
        b.add(("hg", j), "D")
    for j in range(H):
        b.add(("qm", j), "A")
        b.add(("km", j), "A")
    for i in range(NCH):
        b.add(("kt", i), "A")
        b.add(("vm", i), "D")
    for j in range(H):
        b.add(("mo", j), "A")
    b.add("cols", "D")
    b.add("wp", "D")
    for c in range(NCH):
        b.add(("ko", c), "A")
        b.add(("mb", c), "D")
        b.add(("sc", c), "D")
        b.add(("qk", c), "D")
        if c:
            b.add(("yh", c - 1), "D")
            b.add(("ym", c - 1), "D")
        b.add(("oh", c), "A")
        b.add(("ds", c), "D")
        b.add(("inter", c), "A", 2)
        b.add(("intra", c), "D", 2)
        b.add(("dm", c), "D", 2)
    for m in range(4):
        for j in range(2):
            b.add(("g0", m, j), "A")
        for j in range(2):
            b.add(("g1", m, j), "A")
        if m == 0:
            b.add(("yh", NCH - 1), "D")
            b.add(("ym", NCH - 1), "D")
        for j in range(2):
            b.add(("b0", m, j), "D")
        for j in range(2):
            b.add(("b1", m, j), "D")
    for u in range(4):
        for i in range(NCH):
            b.add(("wo", u, i), "D")
        for k in turned_after(u):
            b.add(("nT", k), "A")
    for i in range(NCH):
        b.add(("lg", i), "D")
    return b


def weight_chunks():
    out = []
    for name, c0 in (("mm", C_MM), ("hf", C_HF), ("hi", C_HI), ("hq", C_HQ), ("hg", C_HG), ("mo", C_MO)):
        for u in range(4):
            out.append((name, u, c0 + u * P))
    for m in range(4):
        out += [(g, 2 * m + j, c + (2 * m + j) * P) for g, c in (("g0", C_G0), ("g1", C_G1)) for j in range(2)]
        out += [("b0", m, m * WC), ("b1", m, m * WC)]
    for u in range(4):
        out.append(("wo", u, u * WC))
    return out


def build(nc, ins, out, dbg=None):
    with ExitStack() as top:
        ev = Events(nc, top)

        def dram(name, shape, dt=F32):
            return nc.dram_tensor(name, shape, dt, kind="ExternalOutput" if dbg else "Internal").ap()

        d = {
            "h": dram("h_rows", [ROWS, D]),
            "sum": dram("sum_rows", [SEQ, D]),
            "xn": dram("xn_rows", [ROWS, D]),
            "table": dram("row_table", [TAB, 3], I32),
        }
        lg = top.enter_context(nc.sbuf_tensor("lg", [P, NSPAN * NCH, E], F32))
        ident = top.enter_context(nc.sbuf_tensor("ident", [P, P], F32))
        mixer(nc, ins, d, lg, ident, ev)
        if dbg != "mixer":
            from_routing(nc, ins, d, lg, ident, ev, out)


def mixer(nc, ins, d, lg, ident, ev):
    with ExitStack() as ctx:
        def sb(name, shape, dt=F32):
            return ctx.enter_context(nc.sbuf_tensor(name, shape, dt))

        def shared(name, shape, parts_shape):
            offset = -(-nc.sbuf_base // 32) * 32
            plain = sb(name, shape)
            assert nc.sbuf_base == offset + 4 * int(np.prod(shape[1:]))
            return plain, nc.alloc_sbuf_tensor_at(name + "_parts", parts_shape, R32, offset=offset)

        xrow, xhi = shared("xrow", [P, NCH, D], [P, KD, SPAN])
        region = sb("region", [P, H * NSUB * CH])
        hrow = region[:, 0:NCH * D].rearrange("p (i n) -> p i n", i=NCH)
        kdec = region[:, :].rearrange("p (h i s) -> p h i s", h=H, i=NSUB)
        xT, xlo = shared("xT", [P, KD, SPAN], [P, KD, SPAN])
        tmp = sb("tmp", [P, 2, H, SPAN])
        tmp1, kout = tmp[:, 0], tmp[:, 1]
        merged = tmp[:, :, :, :].rearrange("p a h s -> p (a h) s")
        xn = tmp[:, :, :, :].rearrange("p a h s -> p (a h s)").rearrange("p (i n) -> p i n", i=NCH)
        qin, qdec, kh, bh = (sb(n, [P, H, SPAN]) for n in ("qin", "qdec", "kh", "bh"))
        xs = [b[:, :, :].rearrange("p h s -> p (h s)")[:, 0:D] for b in (kh, bh, qdec)]
        sgh, conv, smo = (sb(n, [P, H, SPAN]) for n in ("sgh", "conv", "smo"))
        mmT = sb("mmT", [P, H, 3 + SPAN])
        qm, km = sb("qm", [QK, H, SPAN]), sb("km", [QK, H, SPAN])
        kt = sb("kt", [P, NCH, H, QK])
        VA = P + 2
        va = sb("va", [P, NCH, H, VA])
        vh = sb("vh", [P, NCH, W])
        sct, wgt, ktok = sb("sct", [P, H, CH]), sb("wgt", [P, H, CH]), sb("ktok", [P, H, CH])
        kw = sb("kw", [P, H, QK])
        nd = sb("nd", [P, H, VA])
        oh, om = sb("oh", [P, H, CH]), sb("om", [P, H, CH])
        ring, ring_parts = shared("ring", [P, NRING, KD, WC], [P, NRING, 2, KD, P])
        sh, sm = sb("sh", [P, H, P]), sb("sm", [QK, H, VA])
        mst = sb("mst", [H, NCH + 1])
        ra, rb, rc, rm, rd = (sb(n, [H, SPAN]) for n in ("ra", "rb", "rc", "rm", "rd"))
        padneg, keep4 = sb("padneg", [H, SPAN]), sb("keep4", [H, SPAN])
        mneg = sb("mneg", [H, NCH])
        dwp = sb("dwp", [H, NCH, H])
        cols, wpb, ebl = sb("cols", [P, NCH, 4, H]), sb("wpb", [QK, NCH, H]), sb("ebl", [P, H, NCH])
        ss = sb("ss", [P, NCH, 4])
        hs = sb("hs", [P, 6, H])
        keep = sb("keep", [P, CH])
        mge = sb("mge", [P, CH])
        mask = sb("mask", [P, CH], I32)
        sel = sb("sel", [H, H, P])
        ones4 = sb("ones4", [H, QK])
        epsc = sb("epsc", [P, 1])
        wif = sb("wif", [P, KD, 2 * H])
        wifh, wifl = sb("wifh", [P, KD, 2 * H], R32), sb("wifl", [P, KD, 2 * H], R32)
        wq, wk, wv = sb("wq", [P, H, QK]), sb("wk", [P, H, QK]), sb("wv", [P, H, P])
        rw, rbias = sb("rw", [P, KD, E]), sb("rbias", [P, E])
        nmix, nffn, nffnT = sb("nmix", [P, KD]), sb("nffn", [P, D]), sb("nffnT", [P, KD])
        cw, cb = sb("cw", [P, 4, H]), sb("cb", [P, H])
        hgn, mln, skp = sb("hgn", [P, H]), sb("mln", [P, H]), sb("skp", [P, H])
        lb, oml, lgt = sb("lb", [P, H]), sb("oml", [P, H]), sb("lgt", [P, 2, H])
        gbi, gbf = sb("gbi", [H, 1]), sb("gbf", [H, 1])
        ps = ctx.enter_context(nc.psum_tensor("ps", [P, 8, 512], F32))

        gate0, gate1 = kh, bh

        def ml_gated(m):
            return (qin, qdec)[m // 4][:, m % 4]

        J = span_jobs()
        L = weight_chunks()
        at = {(n, u): i for i, (n, u, _) in enumerate(L)}

        def last_use(name, u):
            if name in ("hi", "wo"):
                return name, u, NCH - 1
            if name in ("b0", "b1"):
                return name, u, 1
            return (name, u // 2, u % 2) if name in ("g0", "g1") else (name, u)

        def slot(n, u):
            return ring[:, at[n, u] % NRING]

        def raw_part(n):
            return ring[:, n % NRING].rearrange("p k n -> p (k n)")[:, 0:KD * P].rearrange("p (k n) -> p k n", k=KD)

        def lo_part(n):
            return ring_parts[:, n % NRING, 0]

        def hi_part(n):
            return ring_parts[:, n % NRING, 1]

        order = [n for n, c in enumerate(L) if c[0] in SPLIT]

        def bank(name, parts=P, w=512):
            return ps[0:parts, J.bank(name), 0:w]

        def two(name, parts=P):
            b = J.bank(name)
            return ps[0:parts, b:b + 2, :].rearrange("p b (a v) -> p b a v", a=2)[:, :, :, 0:P + 1]

        SETUP = ("const", "smallw", "lbs")
        small = [
            (wif[:, :, :], ins["w_in"][:, :, C_IF:C_IF + 2 * H].rearrange("l (k p) n -> p (l k) n", p=P)),
            (wq[:, :, :], ins["ml_wq"].rearrange("l h c d -> c (l h) d")),
            (wk[:, :, :], ins["ml_wk"].rearrange("l h c d -> c (l h) d")),
            (wv[:, :, :], ins["ml_wv"].rearrange("l h c d -> c (l h) d")),
            (rw[:, :, :], ins["router_w"].rearrange("l (k p) e -> p (l k) e", p=P)),
            (rbias[:, :], ins["router_b"].broadcast_to([P, E])),
            (nffn[:, :], ins["norm_ffn"].broadcast_to([P, D])),
            (nmix[:, :], ins["norm_mix"].rearrange("l (k p) -> p (l k)", p=P)),
            (nffnT[:, :], ins["norm_ffn"].rearrange("l (k p) -> p (l k)", p=P)),
            (cb[:, :], ins["ml_conv_b"].rearrange("l (h p) -> p (l h)", p=P)),
            (hgn[:, :], ins["hg_norm"].rearrange("l (h p) -> p (l h)", p=P)),
            (mln[:, :], ins["ml_norm"].rearrange("l (h p) -> p (l h)", p=P)),
            (skp[:, :], ins["ml_skip"].rearrange("l (h p) -> p (l h)", p=P)),
            (gbi[:, :], ins["ml_gate_b"][0:1, 0:H].rearrange("l h -> h l")),
            (gbf[:, :], ins["ml_gate_b"][0:1, H:2 * H].rearrange("l h -> h l")),
        ] + [(cw[:, w], ins["ml_conv_w"][0, w].rearrange("(h p) -> p h", p=P)) for w in range(4)] \
          + [(lgt[:, r], ins["hg_lb_logits"][r].rearrange("(h p) -> p h", p=P)) for r in range(2)]

        ENGINES = 5

        def span_end(eng, s):
            eng.nop().then_inc(ev("span_ended"), 1)
            eng.wait_ge(ev("span_cleared"), s + 1)
            eng.nop()

        w_in = ins["w_in"].rearrange("l (k p) n -> p (l k) n", p=P)
        wbh = ins["w_branch_hg"].rearrange("l (k p) n -> p (l k) n", p=P)
        wbm = ins["w_branch_ml"].rearrange("l (k p) n -> p (l k) n", p=P)
        w_out = ins["w_out"].rearrange("l (k p) n -> p (l k) n", p=P)
        xin = ins["rows"].rearrange("(i p) n -> p i n", p=P)
        hrows = d["h"].rearrange("(i p) n -> p i n", p=P)
        nrows = d["xn"].rearrange("(i p) n -> p i n", p=P)

        block = ctx.enter_context(nc.Block())

        @block.gpsimd
        def _(pool):
            g = nc.gpsimd
            n = [0]

            def link(ins_):
                n[0] += 1
                ins_.then_inc(ev("pool_const"), 1)
                pool.wait_ge(ev("pool_const"), n[0])

            link(g.memset(ident[:], 0.0))
            link(g.affine_select(out=ident[:], in_=ident[:], compare_op=ALU.not_equal, fill=1.0, base=0,
                                 pattern=[[-1, P]], channel_multiplier=1))
            link(g.memset(mge[:], 0.0))
            link(g.affine_select(out=mge[:], in_=mge[:], compare_op=ALU.is_ge, fill=NEG, base=0,
                                 pattern=[[1, CH]], channel_multiplier=-1))
            link(g.memset(mask[:], 1))
            link(g.affine_select(out=mask[:], in_=mask[:], compare_op=ALU.is_ge, fill=0.0, base=0,
                                 pattern=[[1, CH]], channel_multiplier=-1))
            link(g.memset(keep[:], 1.0))
            link(g.memset(keep[:, 0:1], 0.0))
            link(g.memset(keep4[:], 1.0))
            for c in range(NCH):
                link(g.memset(keep4[:, c * CH:c * CH + 1], 0.0))
            link(g.memset(padneg[:], 0.0))
            link(g.memset(padneg[:, 0:PAD], NEG))
            link(g.memset(sel[:], 0.0))
            link(g.affine_select(out=sel[:], in_=sel[:], compare_op=ALU.not_equal, fill=-1.0, base=0,
                                 pattern=[[-1, H], [0, P]], channel_multiplier=1))
            link(g.memset(ones4[:], 1.0))
            link(g.memset(epsc[:], EPS))
            link(g.memset(sh[:], 0.0))
            link(g.memset(sm[:], 0.0))
            link(g.memset(mst[:], 0.0))
            link(g.memset(mmT[:], 0.0))
            link(g.memset(va[:], 1.0))
            g.memset(sct[:], 0.0).then_inc(ev("const"), 1)
            with pool.Fori(0, NSPAN) as s:
                def lo(n):
                    pool.wait_ge(ev("w_hi"), order.index(n) + 1)
                    g.tensor_tensor(lo_part(n), raw_part(n), hi_part(n).bitcast(F32), ALU.subtract)\
                        .then_inc(ev("w_lo"), 1)

                first_gates = at["g0", 0]
                for n in range(first_gates):
                    lo(n)
                pool.wait_ge(ev("bh_ready"), 1)
                pool.wait_ge(ev("stored_before"), 1)
                g.memset(region[:], 0.0).then_inc(ev("kdec_zero"), 1)
                pool.wait_ge(ev("kdec_zero"), 1)
                for c in range(NCH):
                    for i in range(NSUB):
                        if c and i < NSUB - 1:
                            pool.wait_ge(ev("keys_read"), (c - 1) * (NSUB - 1) + i + 1)
                        elif c:
                            pool.wait_ge(ev("ps_ready"), J.ready(("sc", c - 1)))
                        n_s = (i + 1) * SUB
                        ref = bh[:, :, c * CH + i * SUB + SUB // 2 - 1:c * CH + i * SUB + SUB // 2]
                        g.tensor_tensor(kdec[:, :, i, 0:n_s], ref.broadcast_to([P, H, n_s]),
                                        bh[:, :, c * CH:c * CH + n_s], ALU.subtract).then_inc(ev("kexp_arg"), 1)
                    if c == 0:
                        for n in range(first_gates, first_gates + 4):
                            lo(n)
                for m in range(8):
                    if m % 2 == 0 and m < 6:
                        for n in range(at["g0", m + 2], at["g0", m + 2] + 4):
                            lo(n)
                    pool.wait_ge(ev("branches"), m + 1)
                    g.tensor_tensor(merged[:, m], merged[:, m], ml_gated(m), ALU.add).then_inc(ev("merged"), 1)
                span_end(pool, s)

        @block.vector
        def _(dve):
            v = nc.vector
            seq = [0]

            def link(ins_, *also):
                seq[0] += 1
                ins_.then_inc(ev("dve_step"), 1)
                dve.wait_ge(ev("dve_step"), seq[0])
                for name in also:
                    dve.sem_inc(ev(name), 1)

            def freed(name):
                assert J.jobs[name][3] == "D"
                dve.sem_inc(ev("D_freed"), 1)

            def ready(name):
                dve.wait_ge(ev("ps_ready"), J.ready(name))

            dve.wait_ge(ev("const"), 1)
            dve.wait_ge(ev("smallw"), 16 * len(small))
            v.tensor_tensor(lb[:], lgt[:, 1], lgt[:, 0], ALU.subtract).then_inc(ev("lbd"), 1)
            dve.wait_ge(ev("lbs"), 1)
            v.tensor_scalar(oml[:], lb[:], -1.0, 1.0, ALU.mult, ALU.add).then_inc(ev("oml"), 1)
            dve.wait_ge(ev("oml"), 1)
            v.tensor_copy(wifh[:], wif[:]).then_inc(ev("wif_parts"), 1)
            dve.wait_ge(ev("wif_parts"), 1)
            v.tensor_tensor(wifl[:], wif[:], wifh[:].bitcast(F32), ALU.subtract).then_inc(ev("wif_parts"), 1)
            dve.wait_ge(ev("wif_parts"), 2)
            for i in range(NCH):
                dve.wait_ge(ev("ss0"), i + 1)
                v.reciprocal(ss[:, i, 1:2], ss[:, i, 0:1]).then_inc(ev("r0"), 1)
                dve.wait_ge(ev("r0"), i + 1)
                v.tensor_scalar(xs[i], xrow[:, i], ss[:, i, 1:2], None, ALU.mult).then_inc(ev("xs0"), 1)
            dve.wait_ge(ev("xs0"), NCH)
            with dve.Fori(0, NSPAN) as s:
                for k in range(KD):
                    dve.wait_ge(ev("x_hi"), k + 1)
                    link(v.scalar_tensor_tensor(xlo[:, k], bank(("xT", k), P, SPAN), nmix[:, k:k + 1],
                                                xhi[:, k].bitcast(F32), ALU.mult, ALU.subtract), "x_lo")
                    freed(("xT", k))
                ready("gi")
                link(v.scalar_tensor_tensor(rc[:], bank("gi", H, SPAN), gbi[:, 0:1], padneg[:], ALU.add, ALU.add))
                freed("gi")
                ready("gf")
                link(v.tensor_scalar(ra[:], bank("gf", H, SPAN), gbf[:, 0:1], None, ALU.add), "gf_sum")
                freed("gf")
                link(v.tensor_copy(mmT[:, :, 0:3], mmT[:, :, SPAN:SPAN + 3]))
                for j in range(H):
                    ready(("mm", j))
                    link(v.tensor_copy(mmT[:, j, 3:3 + SPAN], bank(("mm", j), P, SPAN)), "mmT")
                    freed(("mm", j))
                for j in range(H):
                    link(v.tensor_scalar(conv[:, j], mmT[:, j, 0:SPAN], cw[:, 0, j:j + 1], cb[:, j:j + 1],
                                         ALU.mult, ALU.add))
                    for w in range(1, 4):
                        link(v.scalar_tensor_tensor(conv[:, j], mmT[:, j, w:w + SPAN], cw[:, w, j:j + 1],
                                                    conv[:, j], ALU.mult, ALU.add))
                    dve.sem_inc(ev("conv_lin"), 1)
                for j in range(H):
                    dve.wait_ge(ev("hf_sig"), j + 1)
                    link(v.tensor_scalar(tmp1[:, j], tmp1[:, j], oml[:, j:j + 1], lb[:, j:j + 1], ALU.mult, ALU.add))
                dve.sem_inc(ev("f_ready"), 1)
                link(v.tensor_scalar(kh[:], tmp1, -1.0, 1.0, ALU.mult, ALU.add))
                for j in range(H):
                    dve.wait_ge(ev("conv_sig"), j + 1)
                    link(v.tensor_tensor(conv[:, j], conv[:, j], smo[:, j], ALU.mult), "conv_ready")
                for j in range(H):
                    dve.wait_ge(ev("hq_sig"), j + 1)
                    link(v.tensor_tensor(qin[:, j], bank(("hq", j), P, SPAN), qin[:, j], ALU.mult))
                    freed(("hq", j))
                for j in range(H):
                    dve.wait_ge(ev("hg_sig"), j + 1)
                    link(v.tensor_tensor(sgh[:, j], bank(("hg", j), P, SPAN), sgh[:, j], ALU.mult))
                    freed(("hg", j))
                dve.wait_ge(ev("logf"), 1)
                for j in range(H):
                    for c in range(NCH):
                        cs = slice(c * CH, (c + 1) * CH)
                        last = v.tensor_tensor_scan(bh[:, j, cs], keep[:], kout[:, j, cs], 0.0, ALU.mult, ALU.add)
                link(last, "bh_ready")
                b4 = bh[:].rearrange("p h (n s) -> p (h n) s", s=SUB)
                t4 = tmp1.rearrange("p h (n s) -> p (h n) s", s=SUB)
                mid = b4[:, :, SUB // 2 - 1:SUB // 2].broadcast_to([P, H * NCH * NSUB, SUB])
                link(v.tensor_tensor(t4, b4, mid, ALU.subtract), "qexp_arg")
                b3 = bh[:].rearrange("p h (n s) -> p (h n) s", s=CH)
                k3 = kout.rearrange("p h (n s) -> p (h n) s", s=CH)
                lastb = b3[:, :, CH - 1:CH].broadcast_to([P, H * NCH, CH])
                link(v.tensor_tensor(k3, lastb, b3, ALU.subtract), "kout_arg")
                dve.wait_ge(ev("qexp"), 1)
                link(v.scalar_tensor_tensor(qdec[:], tmp1, BIG, qin[:], ALU.min, ALU.mult), "qdec")
                dve.wait_ge(ev("qin_exp"), 1)
                link(v.tensor_tensor(qin[:], qin[:], tmp1, ALU.mult), "qin")
                dve.wait_ge(ev("kout_exp"), 1)
                link(v.tensor_tensor(kout, kout, kh[:], ALU.mult), "kout")
                for i in range(NCH):
                    ready(("vm", i))
                    link(v.tensor_copy(va[:, i, :, 0:P], bank(("vm", i)).rearrange("p (h v) -> p h v", h=H)), "vm")
                    freed(("vm", i))
                dve.wait_ge(ev("lf_log"), 1)
                link(v.scalar_tensor_tensor(ra[:], ra[:], 0.0, rb[:], ALU.min, ALU.subtract))
                link(v.tensor_tensor_scan(rb[:], keep4[:], ra[:], 0.0, ALU.mult, ALU.add))
                link(v.tensor_tensor(rc[:], rc[:], rb[:], ALU.subtract))
                link(v.tensor_copy(mst[:, 0:1], mst[:, NCH:NCH + 1]))
                for c in range(NCH):
                    cs = slice(c * CH, (c + 1) * CH)
                    end = slice((c + 1) * CH - 1, (c + 1) * CH)
                    link(v.tensor_tensor_scan(rm[:, cs], rc[:, cs], rc[:, cs], mst[:, c:c + 1], ALU.max, ALU.max))
                    link(v.tensor_tensor(mst[:, c + 1:c + 2], rb[:, end], rm[:, end], ALU.add))
                    link(v.tensor_scalar(mneg[:, c:c + 1], rm[:, end], -1.0, None, ALU.mult))
                link(v.tensor_tensor(rb[:], rb[:], rm[:], ALU.add), "rows")
                link(v.memset(padneg[:], 0.0))
                def decayed_keys(c):
                    for i in range(NSUB):
                        n_s = (i + 1) * SUB
                        dve.wait_ge(ev("kexp"), c * NSUB + i + 1)
                        link(v.scalar_tensor_tensor(kdec[:, :, i, 0:n_s], kdec[:, :, i, 0:n_s], BIG,
                                                    kh[:, :, c * CH:c * CH + n_s], ALU.min, ALU.mult))
                    dve.sem_inc(ev("kdec"), 1)

                decayed_keys(0)
                dve.wait_ge(ev("row_exps"), 1)
                for c in range(NCH):
                    end = slice((c + 1) * CH - 1, (c + 1) * CH)
                    link(v.tensor_scalar(dwp[:, c], ident[0:H, 0:H], ra[:, end], None, ALU.mult))
                dve.sem_inc(ev("dwp"), 1)
                ready("cols")
                link(v.tensor_copy(cols[:].rearrange("p c k h -> p (c k h)"), bank("cols", P, NCH * 16)), "cols")
                freed("cols")
                ready("wp")
                link(v.tensor_copy(wpb[:].rearrange("p c h -> p (c h)"), bank("wp", QK, NCH * H)))
                freed("wp")
                for j in range(H):
                    link(v.tensor_scalar(conv[:, j], conv[:, j], skp[:, j:j + 1], None, ALU.mult))

                def norms_out(c):
                    dve.wait_ge(ev("o_rms"), 2 * c + 1)
                    link(v.tensor_tensor(oh[:], oh[:], hs[:, 2].rearrange("p (h o) -> p h o", o=1)
                                         .broadcast_to([P, H, P]), ALU.mult), "oh_n")
                    dve.wait_ge(ev("o_rms"), 2 * c + 2)
                    link(v.tensor_tensor(om[:], om[:], hs[:, 4].rearrange("p (h o) -> p h o", o=1)
                                         .broadcast_to([P, H, P]), ALU.mult), "om_n")

                def branches_out(c):
                    cs = slice(c * CH, (c + 1) * CH)
                    ready(("yh", c))
                    for h in range(H):
                        link(v.scalar_tensor_tensor(sgh[:, h, cs], bank(("yh", c))[:, h * P:(h + 1) * P],
                                                    hgn[:, h:h + 1], sgh[:, h, cs], ALU.mult, ALU.mult))
                    freed(("yh", c))
                    ready(("ym", c))
                    for h in range(H):
                        link(v.scalar_tensor_tensor(conv[:, h, cs], bank(("ym", c))[:, h * P:(h + 1) * P],
                                                    mln[:, h:h + 1], conv[:, h, cs], ALU.mult, ALU.add))
                    freed(("ym", c))
                    link(v.tensor_tensor(smo[:, :, cs], conv[:, :, cs], smo[:, :, cs], ALU.mult), "y_ready")

                for c in range(NCH):
                    cs = slice(c * CH, (c + 1) * CH)
                    ready(("mb", c))
                    if c:
                        dve.wait_ge(ev("ps_ready"), J.ready(("intra", c - 1)))
                    for h in range(H):
                        link(v.scalar_tensor_tensor(wgt[:, h], bank(("mb", c)).rearrange("p (h t) -> p h t", h=H)[:, h],
                                                    cols[:, c, 0, h:h + 1], mge[:], ALU.add, ALU.min))
                    dve.sem_inc(ev("wexp_arg"), 1)
                    freed(("mb", c))
                    link(v.tensor_tensor(kw[:], kt[:, c], cols[:, c, 3].rearrange("p (h o) -> p h o", o=1)
                                         .broadcast_to([P, H, QK]), ALU.mult), "kw")
                    if c:
                        norms_out(c - 1)
                    if c + 1 < NCH:
                        decayed_keys(c + 1)
                    ready(("sc", c))
                    link(v.copy_predicated(sct[:], mask[:].rearrange("p (o t) -> p o t", o=1).broadcast_to([P, H, CH]),
                                           bank(("sc", c)).rearrange("p (h t) -> p h t", h=H)), "sct")
                    freed(("sc", c))
                    ready(("qk", c))
                    dve.wait_ge(ev("wexp"), c + 1)
                    link(v.tensor_tensor(wgt[:], wgt[:], bank(("qk", c)).rearrange("p (h t) -> p h t", h=H), ALU.mult),
                         "wgt")
                    freed(("qk", c))
                    if c:
                        branches_out(c - 1)
                    ready(("ds", c))
                    for h in range(H):
                        link(v.scalar_tensor_tensor(sh[:, h], sh[:, h], ebl[:, h, c:c + 1],
                                                    bank(("ds", c)).rearrange("p (h t) -> p h t", h=H)[:, h],
                                                    ALU.mult, ALU.add))
                    dve.sem_inc(ev("sh_new"), 1)
                    freed(("ds", c))
                    dve.wait_ge(ev("inter_sc"), c + 1)
                    ready(("intra", c))
                    nd4 = nd[:].rearrange("p (b a) v -> p b a v", a=2)[:, :, :, 0:P + 1]
                    for b2 in range(2):
                        link(v.tensor_tensor(nd4[:, b2], nd4[:, b2], two(("intra", c))[:, b2], ALU.add))
                    freed(("intra", c))
                    ready(("dm", c))
                    for h in range(H):
                        link(v.scalar_tensor_tensor(sm[:, h, 0:P + 1], sm[:, h, 0:P + 1], wpb[:, c, h:h + 1],
                                                    two(("dm", c), QK)[:, h // 2, h % 2], ALU.mult, ALU.add))
                    dve.sem_inc(ev("sm_new"), 1)
                    freed(("dm", c))
                    den = nd[:, :, P:P + 1].rearrange("p h o -> p (h o)")
                    link(v.scalar_tensor_tensor(hs[:, 0], den, -1.0, den, ALU.mult, ALU.max))
                    link(v.tensor_tensor(hs[:, 0], hs[:, 0], cols[:, c, 2], ALU.max))
                    link(v.reciprocal(hs[:, 0], hs[:, 0]))
                    if c:
                        dve.wait_ge(ev("ps_ready"), J.ready(("ym", c - 1)))
                    link(v.tensor_tensor(om[:], nd[:, :, 0:P], hs[:, 0].rearrange("p (h o) -> p h o", o=1)
                                         .broadcast_to([P, H, P]), ALU.mult), "om")
                norms_out(NCH - 1)
                branches_out(NCH - 1)

                for m in range(4):
                    for j in range(2):
                        t = 2 * m + j
                        ready(("b0", m, j))
                        dve.wait_ge(ev("gates"), 4 * m + j + 1)
                        link(v.tensor_tensor(merged[:, t], bank(("b0", m, j), P, SPAN), gate0[:, t % 4], ALU.mult))
                        freed(("b0", m, j))
                    for j in range(2):
                        t = 2 * m + j
                        ready(("b1", m, j))
                        dve.wait_ge(ev("gates"), 4 * m + 2 + j + 1)
                        link(v.tensor_tensor(ml_gated(t), bank(("b1", m, j), P, SPAN), gate1[:, t % 4], ALU.mult),
                             "branches")
                        freed(("b1", m, j))
                dve.wait_ge(ev("x_again"), 16)
                for u in range(4):
                    for i in range(NCH):
                        us = slice(u * WC, (u + 1) * WC)
                        ready(("wo", u, i))
                        link(v.tensor_tensor(hrow[:, i, us], bank(("wo", u, i), P, WC), xrow[:, i, us], ALU.add))
                        freed(("wo", u, i))
                    dve.sem_inc(ev("h_part"), 1)
                for i in range(NCH):
                    dve.wait_ge(ev("ss2"), i + 1)
                    link(v.reciprocal(ss[:, i, 3:4], ss[:, i, 2:3]))
                for i in range(NCH):
                    link(v.scalar_tensor_tensor(xn[:, i], hrow[:, i], ss[:, i, 3:4], nffn[:], ALU.mult, ALU.mult),
                         "xn_ready")
                for i in range(NCH):
                    ready(("lg", i))
                    link(v.scalar_tensor_tensor(lg[:, bass.ds(s * NCH + i, 1), :].rearrange("p o e -> p (o e)"),
                                                bank(("lg", i), P, E), ss[:, i, 3:4], rbias[:], ALU.mult, ALU.add))
                    freed(("lg", i))
                for i in range(NCH):
                    dve.wait_ge(ev("ss1"), i + 1)
                    link(v.reciprocal(ss[:, i, 1:2], ss[:, i, 0:1]))
                    link(v.tensor_scalar(xs[i], xrow[:, i], ss[:, i, 1:2], None, ALU.mult))
                span_end(dve, s)

        @block.scalar
        def _(act):
            a = nc.scalar
            seq = [0]

            def link(ins_, *also):
                seq[0] += 1
                ins_.then_inc(ev("act_step"), 1)
                act.wait_ge(ev("act_step"), seq[0])
                for name in also:
                    act.sem_inc(ev(name), 1)

            def freed(name):
                assert J.jobs[name][3] == "A"
                act.sem_inc(ev("A_freed"), 1)

            def ready(name):
                act.wait_ge(ev("ps_ready"), J.ready(name))

            act.wait_ge(ev("lbd"), 1)
            a.activation(lb[:], lb[:], ACT.Sigmoid, scale=-1.0).then_inc(ev("lbs"), 1)
            act.wait_ge(ev("const"), 1)
            act.wait_ge(ev("x_loaded"), 16)
            for i in range(NCH):
                a.activation(xs[i], xrow[:, i], ACT.Square, accum_out=ss[:, i, 0:1]).then_inc(ev("sq0"), 1)
            act.wait_ge(ev("sq0"), NCH)
            for i in range(NCH):
                a.activation(ss[:, i, 0:1], ss[:, i, 0:1], ACT.Sqrt, scale=1.0 / D, bias=epsc[:, 0:1])\
                    .then_inc(ev("ss0"), 1)
            act.wait_ge(ev("ss0"), NCH)
            with act.Fori(0, NSPAN) as s:
                def hi(n):
                    act.wait_ge(ev(f"w_loaded{n % NRING}"), 16 * (n // NRING + 1))
                    link(a.copy(hi_part(n), raw_part(n)), "w_hi")

                for k in range(KD):
                    ready(("xT", k))
                    link(a.activation(xhi[:, k], bank(("xT", k), P, SPAN), ACT.Copy, scale=nmix[:, k:k + 1]), "x_hi")
                AHEAD = 3
                for n in range(at["hf", 0] + AHEAD):
                    hi(n)
                act.wait_ge(ev("stored_before"), 1)
                for j in range(H):
                    hi(at["hf", j] + AHEAD)
                    ready(("hf", j))
                    link(a.activation(tmp1[:, j], bank(("hf", j), P, SPAN), ACT.Sigmoid), "hf_sig")
                    freed(("hf", j))
                for j in range(H):
                    act.wait_ge(ev("conv_lin"), j + 1)
                    link(a.activation(smo[:, j], conv[:, j], ACT.Sigmoid), "conv_sig")
                for u in range(4):
                    hi(at["hi", u] + AHEAD)
                    for i in range(NCH):
                        ready(("hi", u, i))
                        link(a.copy(vh[:, i, u * P:(u + 1) * P], bank(("hi", u, i), P, P)), "vh")
                        freed(("hi", u, i))
                for j in range(H):
                    hi(at["hq", j] + AHEAD)
                    ready(("hq", j))
                    link(a.activation(qin[:, j], bank(("hq", j), P, SPAN), ACT.Sigmoid), "hq_sig")
                for j in range(H):
                    hi(at["hg", j] + AHEAD)
                    ready(("hg", j))
                    link(a.activation(sgh[:, j], bank(("hg", j), P, SPAN), ACT.Sigmoid), "hg_sig")
                hi(at["mo", 3])
                act.wait_ge(ev("f_ready"), 1)
                link(a.activation(kout, tmp1, ACT.Ln), "logf")
                for j in range(H):
                    ready(("qm", j))
                    link(a.mul(qm[:, j], bank(("qm", j), QK, SPAN), QK ** -0.5))
                    freed(("qm", j))
                    ready(("km", j))
                    link(a.copy(km[:, j], bank(("km", j), QK, SPAN)), "qkm")
                    freed(("km", j))
                act.wait_ge(ev("gf_sum"), 1)
                link(a.activation(rb[:], ra[:], ACT.Abs))
                link(a.activation(rb[:], rb[:], ACT.Exp, scale=-1.0))
                link(a.activation(rb[:], rb[:], ACT.Ln, bias=1.0), "lf_log")
                act.wait_ge(ev("qexp_arg"), 1)
                link(a.activation(tmp1, tmp1, ACT.Exp), "qexp")
                act.wait_ge(ev("kout_arg"), 1)
                link(a.activation(kout, kout, ACT.Exp), "kout_exp")
                act.wait_ge(ev("qdec"), 1)
                link(a.activation(tmp1, bh[:], ACT.Exp), "qin_exp")
                link(a.activation(ebl[:].rearrange("p h c -> p (h c)"),
                                  bh[:].rearrange("p h (n s) -> p (h n) s", s=CH)[:, :, CH - 1:CH]
                                  .rearrange("p n o -> p (n o)"), ACT.Exp))
                for i in range(NCH):
                    ready(("kt", i))
                    link(a.copy(kt[:, i].rearrange("p h d -> p (h d)"), bank(("kt", i), P, H * QK)), "kt")
                    freed(("kt", i))
                def key_exps(c):
                    for i in range(NSUB):
                        n_s = (i + 1) * SUB
                        act.wait_ge(ev("kexp_arg"), c * NSUB + i + 1)
                        link(a.activation(kdec[:, :, i, 0:n_s], kdec[:, :, i, 0:n_s], ACT.Exp), "kexp")

                key_exps(0)
                act.wait_ge(ev("rows"), 1)
                for c in range(NCH):
                    cs = slice(c * CH, (c + 1) * CH)
                    a.activation(ra[:, cs], rm[:, cs], ACT.Exp, scale=-1.0, bias=mst[:, c:c + 1])
                    a.activation(rd[:, cs], rc[:, cs], ACT.Exp, bias=mneg[:, c:c + 1])
                link(a.activation(rb[:], rb[:], ACT.Exp, scale=-1.0), "row_exps")
                act.wait_ge(ev("conv_ready"), H)
                for j in range(H):
                    hi(at["g0", 0] + j)
                    ready(("mo", j))
                    link(a.activation(smo[:, j], bank(("mo", j), P, SPAN), ACT.Sigmoid))
                    freed(("mo", j))

                def rms_of_om(c):
                    act.wait_ge(ev("om"), c + 1)
                    for h in range(H):
                        a.activation(tmp1[:, h, 0:CH], om[:, h], ACT.Square, accum_out=hs[:, 3, h:h + 1])
                    link(a.activation(epsc[:, 0:1], epsc[:, 0:1], ACT.Copy))
                    link(a.activation(hs[:, 3], hs[:, 3], ACT.Ln, scale=1.0 / P, bias=epsc[:, 0:1]))
                    link(a.activation(hs[:, 4], hs[:, 3], ACT.Exp, scale=-0.5), "o_rms")

                for c in range(NCH):
                    if c:
                        rms_of_om(c - 1)
                    ready(("ko", c))
                    link(a.copy(ktok[:].rearrange("p h d -> p (h d)"), bank(("ko", c))), "ktok")
                    freed(("ko", c))
                    act.wait_ge(ev("wexp_arg"), c + 1)
                    link(a.activation(wgt[:], wgt[:], ACT.Exp), "wexp")
                    if c + 1 < NCH:
                        key_exps(c + 1)
                    ready(("oh", c))
                    if c:
                        act.wait_ge(ev("ps_ready"), J.ready(("yh", c - 1)))
                    link(a.copy(oh[:].rearrange("p h d -> p (h d)"), bank(("oh", c))))
                    freed(("oh", c))
                    for h in range(H):
                        a.activation(tmp1[:, h, 0:CH], oh[:, h], ACT.Square, accum_out=hs[:, 1, h:h + 1])
                    link(a.activation(epsc[:, 0:1], epsc[:, 0:1], ACT.Copy))
                    link(a.activation(hs[:, 1], hs[:, 1], ACT.Ln, scale=1.0 / P, bias=epsc[:, 0:1]))
                    link(a.activation(hs[:, 2], hs[:, 1], ACT.Exp, scale=-0.5), "o_rms")
                    ready(("inter", c))
                    for h in range(H):
                        last = a.activation(nd[:, h, 0:P + 1], two(("inter", c))[:, h // 2, h % 2], ACT.Copy,
                                            scale=cols[:, c, 1, h:h + 1])
                    link(last, "inter_sc")
                    freed(("inter", c))
                rms_of_om(NCH - 1)
                for m in range(4):
                    if m >= 2:
                        act.wait_ge(ev("branches"), 2 * (m - 1))
                    for w, g in (("g0", gate0), ("g1", gate1)):
                        for j in range(2):
                            ready((w, m, j))
                            link(a.activation(g[:, (2 * m + j) % 4], bank((w, m, j), P, SPAN), ACT.Sigmoid), "gates")
                            freed((w, m, j))
                    if m < 3:
                        for n in range(at["g0", 2 * m + 2], at["g0", 2 * m + 2] + 4):
                            hi(n)
                for u in range(4):
                    for k in turned_after(u):
                        ready(("nT", k))
                        link(a.activation(xT[:, k], bank(("nT", k), P, SPAN), ACT.Copy, scale=nffnT[:, k:k + 1]), "nT")
                        freed(("nT", k))
                act.wait_ge(ev("merged"), 8)
                for i in range(NCH):
                    link(a.activation(xs[i], hrow[:, i], ACT.Square, accum_out=ss[:, i, 2:3]))
                for i in range(NCH):
                    link(a.activation(ss[:, i, 2:3], ss[:, i, 2:3], ACT.Sqrt, scale=1.0 / D, bias=epsc[:, 0:1]), "ss2")
                act.wait_ge(ev("x_loaded"), s * 16 + 32)
                for i in range(NCH):
                    link(a.activation(xs[i], xrow[:, i], ACT.Square, accum_out=ss[:, i, 0:1]))
                for i in range(NCH):
                    link(a.activation(ss[:, i, 0:1], ss[:, i, 0:1], ACT.Sqrt, scale=1.0 / D, bias=epsc[:, 0:1]), "ss1")
                span_end(act, s)

        @block.tensor
        def _(pe):
            t = nc.tensor

            def begin(name):
                for e, c in J.jobs[name][2].items():
                    pe.wait_ge(ev(f"{e}_freed"), c)

            def done(last):
                last.then_inc(ev("ps_ready"), 1)

            def weights(name, u):
                n = at[name, u]
                pe.wait_ge(ev(f"w_loaded{n % NRING}"), 16 * (n // NRING + 1))

            pe.wait_ge(ev("const"), 1)
            pe.wait_ge(ev("smallw"), 16 * len(small))
            pe.wait_ge(ev("xs0"), NCH)
            with pe.Fori(0, NSPAN) as s:
                for k in range(KD):
                    begin(("xT", k))
                    for i in range(NCH):
                        last = t.transpose(bank(("xT", k))[:, i * P:(i + 1) * P], xs[i][:, k * P:(k + 1) * P], ident[:])
                    done(last)
                pe.wait_ge(ev("x_lo"), KD)

                def three(o, left, right):
                    for a, b in ((0, 0), (1, 0), (0, 1)):
                        for k in range(KD):
                            last = t.matmul(o, left[a](k), right[b](k), start=a + b + k == 0,
                                            stop=b == 1 and k == KD - 1)
                    done(last)

                xp = (lambda k: xhi[:, k], lambda k: xlo[:, k])
                for name, o in (("gi", 0), ("gf", H)):
                    begin(name)
                    three(bank(name, H, SPAN), (lambda k: wifh[:, k, o:o + H], lambda k: wifl[:, k, o:o + H]), xp)

                def parts(name, u):
                    n = at[name, u]
                    pe.wait_ge(ev("w_lo"), order.index(n) + 1)
                    return lambda k: hi_part(n)[:, k], lambda k: lo_part(n)[:, k]

                def project_split(name, u, job):
                    w = parts(name, u)
                    begin(job)
                    three(bank(job, P, SPAN), w, xp)

                def rows_split(name, u, jobs):
                    w = parts(name, u)
                    for i in range(NCH):
                        begin(jobs[i])
                        rs = slice(i * P, (i + 1) * P)
                        three(bank(jobs[i], P, P), (lambda k: xhi[:, k, rs], lambda k: xlo[:, k, rs]), w)

                def project(name, u, jobs, kt_, rhs):
                    weights(name, u)
                    for j in range(2):
                        begin(jobs[j])
                        for k in range(kt_):
                            last = t.matmul(bank(jobs[j], P, SPAN), slot(name, u)[:, k, j * P:(j + 1) * P], rhs[:, k],
                                            start=k == 0, stop=k == kt_ - 1)
                        done(last)

                def rows(name, u, jobs, lhs):
                    weights(name, u)
                    for i in range(NCH):
                        begin(jobs[i])
                        for k in range(KD):
                            last = t.matmul(bank(jobs[i], P, WC), lhs[:, k, i * P:(i + 1) * P], slot(name, u)[:, k],
                                            start=k == 0, stop=k == KD - 1)
                        done(last)

                for name in ("mm", "hf", "hi", "hq", "hg"):
                    for u in range(4):
                        if name == "hi":
                            rows_split(name, u, [("hi", u, i) for i in range(NCH)])
                        else:
                            project_split(name, u, (name, u))
                pe.wait_ge(ev("conv_ready"), H)
                for h in range(H):
                    for name, w in (("qm", wq), ("km", wk)):
                        begin((name, h))
                        done(t.matmul(bank((name, h), QK, SPAN), w[:, h], conv[:, h], start=True, stop=True))
                for i in range(NCH):
                    begin(("kt", i))
                    for h in range(H):
                        last = t.matmul(bank(("kt", i))[:, h * QK:(h + 1) * QK], conv[:, h, i * P:(i + 1) * P], wk[:, h],
                                        start=True, stop=True)
                    done(last)
                    begin(("vm", i))
                    for h in range(H):
                        last = t.matmul(bank(("vm", i))[:, h * P:(h + 1) * P], mmT[:, h, 3 + i * P:3 + (i + 1) * P],
                                        wv[:, h], start=True, stop=True)
                    done(last)
                for u in range(4):
                    project_split("mo", u, ("mo", u))
                pe.wait_ge(ev("row_exps"), 1)
                begin("cols")
                for c in range(NCH):
                    for n, r in enumerate((rc, ra, rb, rd)):
                        o = (c * 4 + n) * H
                        last = t.transpose(bank("cols")[:, o:o + H], r[:, c * CH:(c + 1) * CH], ident[0:H, 0:H])
                done(last)
                begin("wp")
                pe.wait_ge(ev("dwp"), 1)
                done(t.matmul(bank("wp", QK, NCH * H), ones4[:], dwp[:].rearrange("p c h -> p (c h)"),
                              start=True, stop=True))
                pe.wait_ge(ev("kout"), 1)
                pe.wait_ge(ev("qin"), 1)
                pe.wait_ge(ev("vh"), 4 * NCH)
                pe.wait_ge(ev("qkm"), H)
                pe.wait_ge(ev("vm"), NCH)

                def turn_outputs(c):
                    begin(("yh", c))
                    pe.wait_ge(ev("oh_n"), c + 1)
                    for h in range(H):
                        last = t.transpose(bank(("yh", c))[:, h * P:(h + 1) * P], oh[:, h], ident[:])
                    done(last)
                    begin(("ym", c))
                    pe.wait_ge(ev("om_n"), c + 1)
                    for h in range(H):
                        last = t.transpose(bank(("ym", c))[:, h * P:(h + 1) * P], om[:, h], ident[:])
                    done(last)

                for c in range(NCH):
                    cs = slice(c * CH, (c + 1) * CH)
                    begin(("ko", c))
                    for h in range(H):
                        last = t.transpose(bank(("ko", c))[:, h * P:(h + 1) * P], kout[:, h, cs], ident[:])
                    done(last)
                    begin(("mb", c))
                    for h in range(H):
                        last = t.matmul(bank(("mb", c))[:, h * P:(h + 1) * P], sel[:, h], rm[:, cs], start=True, stop=True)
                    done(last)
                    begin(("sc", c))
                    pe.wait_ge(ev("kdec"), c + 1)
                    for i in range(NSUB):
                        for h in range(H):
                            last = t.matmul(bank(("sc", c))[:, h * P + i * SUB:h * P + (i + 1) * SUB], kdec[:, h, i],
                                            qdec[:, h, c * CH + i * SUB:c * CH + (i + 1) * SUB], start=True, stop=True)
                        if i < NSUB - 1:
                            last.then_inc(ev("keys_read"), 1)
                    done(last)
                    begin(("qk", c))
                    for h in range(H):
                        last = t.matmul(bank(("qk", c))[:, h * P:(h + 1) * P], km[:, h, cs], qm[:, h, cs],
                                        start=True, stop=True)
                    done(last)
                    if c:
                        turn_outputs(c - 1)
                    begin(("oh", c))
                    if c:
                        pe.wait_ge(ev("sh_new"), c)
                    pe.wait_ge(ev("sct"), c + 1)
                    for h in range(H):
                        hv = slice(h * P, (h + 1) * P)
                        t.matmul(bank(("oh", c))[:, hv], qin[:, h, cs], sh[:, h], start=True, stop=False)
                        last = t.matmul(bank(("oh", c))[:, hv], sct[:, h], vh[:, c, hv], start=False, stop=True)
                    done(last)
                    begin(("ds", c))
                    pe.wait_ge(ev("ktok"), c + 1)
                    for h in range(H):
                        hv = slice(h * P, (h + 1) * P)
                        last = t.matmul(bank(("ds", c))[:, hv], ktok[:, h], vh[:, c, hv], start=True, stop=True)
                    done(last)
                    begin(("inter", c))
                    if c:
                        pe.wait_ge(ev("sm_new"), c)
                    for h in range(H):
                        last = t.matmul(two(("inter", c))[:, h // 2, h % 2], qm[:, h, cs], sm[:, h, 0:P + 1],
                                        start=True, stop=True)
                    done(last)
                    begin(("intra", c))
                    pe.wait_ge(ev("wgt"), c + 1)
                    for h in range(H):
                        last = t.matmul(two(("intra", c))[:, h // 2, h % 2], wgt[:, h], va[:, c, h, 0:P + 1],
                                        start=True, stop=True)
                    done(last)
                    begin(("dm", c))
                    pe.wait_ge(ev("kw"), c + 1)
                    for h in range(H):
                        last = t.matmul(two(("dm", c), QK)[:, h // 2, h % 2], kw[:, h], va[:, c, h, 0:P + 1],
                                        start=True, stop=True)
                    done(last)
                for m in range(4):
                    for g in ("g0", "g1"):
                        for j in range(2):
                            project_split(g, 2 * m + j, (g, m, j))
                    if m == 0:
                        turn_outputs(NCH - 1)
                        pe.wait_ge(ev("y_ready"), NCH)
                    project("b0", m, [("b0", m, j) for j in range(2)], H, sgh)
                    project("b1", m, [("b1", m, j) for j in range(2)], H, smo)
                pe.wait_ge(ev("merged"), 8)
                for u in range(4):
                    rows("wo", u, [("wo", u, i) for i in range(NCH)], merged)
                    for k in turned_after(u):
                        pe.wait_ge(ev("h_part"), k // 2 + 1)
                        begin(("nT", k))
                        for i in range(NCH):
                            last = t.transpose(bank(("nT", k))[:, i * P:(i + 1) * P], hrow[:, i, k * P:(k + 1) * P], ident[:])
                        done(last)
                pe.wait_ge(ev("nT"), KD)
                for i in range(NCH):
                    begin(("lg", i))
                    for k in range(KD):
                        last = t.matmul(bank(("lg", i), P, E), xT[:, k, i * P:(i + 1) * P], rw[:, k],
                                        start=k == 0, stop=k == KD - 1)
                    done(last)
                span_end(pe, s)

        @block.sync
        def _(sp):
            for dst, src in small:
                sp.dma_start(dst, src, allow_slow_non_contiguous=True).then_inc(ev("smallw"), 16)
            setup = {"const", "smallw", "lbs", "lbd", "oml", "pool_const", "x_loaded",
                     "rows_stored", "stored_seen", "ss0", "sq0", "r0", "xs0", "wif_parts", "span_ended", "span_cleared",
                     "span_clearing"}
            sp.dma_start(xrow[:], xin[:, 0:NCH, :]).then_inc(ev("x_loaded"), 16)
            with sp.Fori(0, NSPAN) as s:
                for n, (name, u, c0) in enumerate(L):
                    src = {"b0": wbh, "b1": wbm, "wo": w_out}.get(name, w_in)
                    kt_ = H if name in ("b0", "b1") else KD
                    if n >= NRING:
                        sp.wait_ge(ev("ps_ready"), J.ready(last_use(*L[n - NRING][0:2])))
                    if n == NRING:
                        with sp.If(s > 0):
                            sp.wait_ge(ev("rows_stored"), s * 32)
                            sp.nop().then_inc(ev("stored_seen"), 1)
                        with sp.Else():
                            sp.nop()
                        sp.nop().then_inc(ev("stored_before"), 1)
                    if (name, u) == ("wo", 1):
                        sp.dma_start(xrow[:], xin[:, bass.ds(s * NCH, NCH), :]).then_inc(ev("x_again"), 16)
                    dst, w = (raw_part(n), P) if name in SPLIT else (ring[:, n % NRING, 0:kt_, :], WC)
                    sp.dma_start(dst, src[:, :, c0:c0 + w]).then_inc(ev(f"w_loaded{n % NRING}"), 16)
                sp.wait_ge(ev("h_part"), 4)
                sp.dma_start(xrow[:], xin[:, bass.ds(s * NCH + NCH, NCH), :]).then_inc(ev("x_loaded"), 16)
                sp.dma_start(hrows[:, bass.ds(s * NCH, NCH), :], hrow).then_inc(ev("rows_stored"), 16)
                sp.wait_ge(ev("xn_ready"), NCH)
                sp.dma_start(nrows[:, bass.ds(s * NCH, NCH), :], xn).then_inc(ev("rows_stored"), 16)
                sp.nop().then_inc(ev("span_ended"), 1)
                sp.wait_ge(ev("span_ended"), ENGINES * (s + 1))
                sp.nop().then_inc(ev("span_clearing"), 1)
                for name in [m for m in ev.made if m not in setup]:
                    sp.sem_clear(ev(name))
                sp.nop().then_inc(ev("span_cleared"), 1)
            sp.wait_ge(ev("rows_stored"), 32 * NSPAN)
            sp.wait_ge(ev("x_loaded"), 16 * (NSPAN + 1))


def from_routing(nc, ins, d, lg, ident, ev, out):
    with ExitStack() as ctx:
        def sb(name, shape, dt=F32):
            return ctx.enter_context(nc.sbuf_tensor(name, shape, dt))

        npass = sb("npass", [1, 2, E], I32)
        bparts = sb("bparts", [2 * E, 2 * FF], R32)
        pickf = sb("pickf", [2 * E, E])
        eps2 = sb("eps2", [P, 1])
        routing(nc, ins, d, lg, ident, ev, npass, bparts, pickf, eps2)
        experts(nc, ins, d, ident, ev, npass, bparts, pickf)
        final_norm(nc, ins, d, ev, eps2, out)


def routing(nc, ins, d, lg, ident, ev, npass, bparts, pickf, eps2):
    with ExitStack() as ctx:
        def sb(name, shape, dt=F32):
            return ctx.enter_context(nc.sbuf_tensor(name, shape, dt))

        top, topi, topf = sb("top", [P, NT, 8]), sb("topi", [P, NT, 8], U32), sb("topf", [P, NT, 8])
        iota_i, iota = sb("iota_i", [P, E], I32), sb("iota", [P, E])
        ebase = sb("ebase", [P, E])
        hot = sb("hot", [P, TOPK, NT, E])
        chosen = sb("chosen", [P, NT, E])
        before = sb("before", [P, NT + 1, E])
        prod = sb("prod", [P, NT, E])
        destf = sb("destf", [P, TOPK, NT])
        wsum = sb("wsum", [P, NT, 1])
        tri, ones = sb("tri", [P, P]), sb("ones", [P, P])
        dest = sb("dest", [P, TOPK, NT], I32)
        gw = sb("gw", [P, NT, TOPK])
        rowid = sb("rowid", [P, TOPK, NT, 3], I32)
        blank = sb("blank", [P, TAB // P, 3], I32)
        cntf = sb("cntf", [1, 3, E])
        hrow = sb("hrow", [P, NT, D])
        share = sb("share", [P, NT, E])
        shareT = sb("shareT", [E, NT, P])
        bgu, bdn = sb("bgu", [2 * E, 2 * FF]), sb("bdn", [E, D])
        ps = ctx.enter_context(nc.psum_tensor("rps", [P, 8, 512], F32))
        hrows = d["h"][LEAD:ROWS].rearrange("(i p) n -> p i n", p=P)
        hbrows = d["sum"].rearrange("(i p) n -> p i n", p=P)
        block = ctx.enter_context(nc.Block())

        @block.sync
        def _(sp):
            for r in range(2):
                sp.dma_start(bgu[r * E:(r + 1) * E, :], ins["exp_b_gu"].rearrange("l e n -> (l e) n"))\
                    .then_inc(ev("biases"), 16)
            sp.dma_start(bdn[:], ins["exp_b_down"].rearrange("l e n -> (l e) n")).then_inc(ev("biases"), 16)
            sp.dma_start(hrow[:], hrows).then_inc(ev("hrow"), 16)
            sp.wait_ge(ev("r_blank"), 3)
            sp.dma_start(d["table"].rearrange("(p n) o -> p (n o)", p=P),
                         blank[:].rearrange("p n o -> p (n o)")).then_inc(ev("table_blank"), 16)
            for i in range(NT):
                sp.wait_ge(ev("hb_made"), 2 * (i + 1))
                sp.dma_start(hbrows[:, i], hrow[:, i]).then_inc(ev("hb_stored"), 16)
            sp.wait_ge(ev("hb_stored"), 16 * NT)

        @block.gpsimd
        def _(pool):
            g = nc.gpsimd
            g.memset(blank[:, :, 0:1], 0).then_inc(ev("r_blank"), 1)
            g.memset(blank[:, :, 1:2], NOROW).then_inc(ev("r_blank"), 1)
            g.memset(blank[:, :, 2:3], 0).then_inc(ev("r_blank"), 1)
            g.iota(iota_i[:], pattern=[[1, E]], base=0, channel_multiplier=0).then_inc(ev("r_iota"), 1)
            for k in range(TOPK):
                g.iota(rowid[:, k, :, 0:1], pattern=[[P, NT], [0, 1]], base=LEAD, channel_multiplier=1)\
                    .then_inc(ev("rowid"), 1)
                g.iota(rowid[:, k, :, 1:2], pattern=[[P, NT], [0, 1]], base=0, channel_multiplier=1)\
                    .then_inc(ev("rowid"), 1)
            g.memset(eps2[:], EPS)
            g.memset(ones[:], 1.0).then_inc(ev("r_const"), 1)
            g.memset(tri[:], 1.0).then_inc(ev("r_const"), 1)
            pool.wait_ge(ev("r_const"), 2)
            g.affine_select(out=tri[:], in_=tri[:], compare_op=ALU.is_gt, fill=0.0, base=0,
                            pattern=[[1, P]], channel_multiplier=-1).then_inc(ev("r_const"), 1)
            pool.wait_ge(ev("table_blank"), 16)
            pool.wait_ge(ev("dest"), 1)
            pool.wait_ge(ev("rowid"), 2 * TOPK)
            for k in range(TOPK):
                for i in range(NT):
                    g.indirect_dma_start(out=d["table"], out_offset=bass.IndirectOffsetOnAxis(ap=dest[:, k, i:i + 1], axis=0),
                                         in_=rowid[:, k, i], in_offset=None).then_inc(ev("table"), 16)
            pool.wait_ge(ev("table"), 16 * TOPK * NT)

        @block.vector
        def _(dve):
            v = nc.vector
            n = [0]

            def link(ins_):
                n[0] += 1
                ins_.then_inc(ev("r_step"), 1)
                dve.wait_ge(ev("r_step"), n[0])

            for i in range(NT):
                link(v.max(top[:, i], lg[:, NSPAN * NCH - NT + i]))
                link(v.max_index(topi[:, i], top[:, i], lg[:, NSPAN * NCH - NT + i]))
            link(v.tensor_copy(topf[:], topi[:]))
            dve.wait_ge(ev("r_iota"), 1)
            link(v.tensor_copy(iota[:], iota_i[:]))
            link(v.tensor_scalar(ebase[:], iota[:], float(CAP), None, ALU.mult))
            every = iota[:].rearrange("p (o e) -> p o e", o=1).broadcast_to([P, NT, E])
            for k in range(TOPK):
                link(v.tensor_tensor(hot[:, k], every, topf[:, :, k:k + 1].broadcast_to([P, NT, E]), ALU.is_equal))
            link(v.tensor_tensor(chosen[:], hot[:, 0], hot[:, 1], ALU.add))
            for k in range(2, TOPK):
                link(v.tensor_tensor(chosen[:], chosen[:], hot[:, k], ALU.add))
            link(v.memset(before[:, 0], 0.0))
            for i in range(NT):
                link(v.tensor_tensor(before[:, i + 1], before[:, i], chosen[:, i], ALU.add))
            dve.sem_inc(ev("chosen"), 1)
            link(v.tensor_tensor(gw[:], top[:, :, 0:TOPK], top[:, :, 0:1].broadcast_to([P, NT, TOPK]), ALU.subtract))
            dve.sem_inc(ev("gw_arg"), 1)
            dve.wait_ge(ev("gw_exp"), 1)
            link(v.tensor_reduce(wsum[:].rearrange("p t o -> p (t o)"), gw[:], AX.X, ALU.add))
            link(v.reciprocal(wsum[:], wsum[:]))
            link(v.tensor_tensor(gw[:], gw[:], wsum[:].broadcast_to([P, NT, TOPK]), ALU.mult))
            for k in range(TOPK):
                dst = share if k == 0 else prod
                link(v.tensor_tensor(dst[:], hot[:, k], gw[:, :, k:k + 1].broadcast_to([P, NT, E]), ALU.mult))
                if k:
                    link(v.tensor_tensor(share[:], share[:], prod[:], ALU.add))
            dve.sem_inc(ev("share"), 1)
            for k in range(TOPK):
                link(v.tensor_copy(rowid[:, k, :, 2:3].bitcast(F32), gw[:, :, k:k + 1]))
            dve.wait_ge(ev("ranks"), 1)
            rank = ps[:, 0, 0:NT * E].rearrange("p (t e) -> p t e", e=E)
            link(v.tensor_tensor(before[:, 0:NT], rank, ebase[:].rearrange("p (o e) -> p o e", o=1)
                                 .broadcast_to([P, NT, E]), ALU.add))
            for k in range(TOPK):
                link(v.tensor_tensor(prod[:], hot[:, k], before[:, 0:NT], ALU.mult))
                link(v.tensor_reduce(destf[:, k], prod[:], AX.X, ALU.add))
            link(v.tensor_copy(dest[:], destf[:]))
            dve.sem_inc(ev("dest"), 1)
            link(v.tensor_copy(cntf[:, 0], ps[0:1, 1, 0:E]))
            link(v.memset(cntf[:, 1], 0.0))
            link(v.memset(cntf[:, 2], 1.0))
            for m in range(NPASS):
                link(v.scalar_tensor_tensor(cntf[:, 1], cntf[:, 0], float(P + m * 2 * P), cntf[:, 1],
                                            ALU.is_gt, ALU.add))
                if m:
                    link(v.scalar_tensor_tensor(cntf[:, 2], cntf[:, 0], float(m * 2 * P), cntf[:, 2],
                                                ALU.is_gt, ALU.add))
            link(v.tensor_tensor(cntf[:, 2], cntf[:, 2], cntf[:, 1], ALU.subtract))
            link(v.tensor_copy(npass[:], cntf[:, 1:3]))
            dve.wait_ge(ev("biases"), 48)
            link(v.tensor_scalar(bgu[:, 1:2 * FF:2], bgu[:, 1:2 * FF:2], 1.0, None, ALU.add))
            link(v.tensor_copy(bparts[:], bgu[:]))
            link(v.tensor_tensor(bparts[E:2 * E, :], bgu[E:2 * E, :], bparts[E:2 * E, :].bitcast(F32), ALU.subtract))
            for r in range(2):
                link(v.tensor_copy(pickf[r * E:(r + 1) * E, :], ident[0:E, 0:E]))
            dve.wait_ge(ev("shareT_ps"), 1)
            for q in range(2):
                link(v.tensor_copy(shareT[:, 4 * q:4 * q + 4].rearrange("e i p -> e (i p)"), ps[0:E, 4 + q]))
            dve.sem_inc(ev("shareT"), 1)
            dve.wait_ge(ev("hrow"), 16)
            for m in range(2 * NT):
                dve.wait_ge(ev("hb_ps"), m + 1)
                half = hrow[:, m // 2, (m % 2) * 512:(m % 2 + 1) * 512]
                link(v.tensor_tensor(half, half, ps[:, 6 + m % 2], ALU.add))
                dve.sem_inc(ev("hb_made"), 1)

        @block.scalar
        def _(act):
            act.wait_ge(ev("gw_arg"), 1)
            nc.scalar.activation(gw[:], gw[:], ACT.Exp).then_inc(ev("gw_exp"), 1)

        @block.tensor
        def _(pe):
            t = nc.tensor
            pe.wait_ge(ev("biases"), 48)
            pe.wait_ge(ev("chosen"), 1)
            pe.wait_ge(ev("r_const"), 3)
            for i in range(NT):
                o = ps[:, 0, i * E:(i + 1) * E]
                t.matmul(o, tri[:], chosen[:, i], start=True, stop=False)
                t.matmul(o, ones[:], before[:, i], start=False, stop=True)
            t.matmul(ps[:, 1, 0:E], ones[:], before[:, NT], start=True, stop=True).then_inc(ev("ranks"), 1)
            pe.wait_ge(ev("share"), 1)
            for i in range(NT):
                last = t.transpose(ps[0:E, 4 + i // 4, (i % 4) * P:(i % 4 + 1) * P], share[:, i], ident[:])
            last.then_inc(ev("shareT_ps"), 1)
            pe.wait_ge(ev("shareT"), 1)
            for n in range(2 * NT):
                if n >= 2:
                    pe.wait_ge(ev("hb_made"), n - 1)
                t.matmul(ps[:, 6 + n % 2], shareT[:, n // 2], bdn[:, (n % 2) * 512:(n % 2 + 1) * 512],
                         start=True, stop=True).then_inc(ev("hb_ps"), 1)


def experts(nc, ins, d, ident, ev, npass, bparts, pickf):
    with ExitStack() as ctx:
        def sb(name, shape, dt=F32):
            return ctx.enter_context(nc.sbuf_tensor(name, shape, dt))

        PC, KH = 512, KD // 2
        NPIECE = 4
        ITEMS = [(p, kh) for p in range(NPIECE) for kh in range(2)] + [(4, 0), (5, 0), (4, 1), (5, 1)]
        NI = len(ITEMS)
        NRAW, NHL, AHEAD = 4, 6, 5

        TURNED = (2, 4, 6, 8)

        LIMU = LIMIT + 1.0

        raw = sb("raw", [P, NRAW, KH, PC])
        whi, wlo = sb("whi", [P, NHL, KH, PC], R32), sb("wlo", [P, NHL, KH, PC], R32)
        ids = [sb(f"ids{b}", [P, 3], I32) for b in "AB"]
        to = [sb(f"to{b}", [P, 1], I32) for b in "AB"]
        share = [sb(f"share{b}", [P, 1]) for b in "AB"]
        xg = [sb(f"xg{b}", [P, D]) for b in "AB"]
        xhi, xlo = ([sb(f"{n}{b}", [P, KD, P], R32) for b in "AB"] for n in ("xhi", "xlo"))
        sg, am = ([sb(f"{n}{b}", [P, 2, PC // 2]) for b in "AB"] for n in ("sg", "am"))
        u_ = [sb(f"u{b}", [P, PC // 2]) for b in "AB"]
        ahi, alo = ([sb(f"{n}{b}", [P, KD, P], R32) for b in "AB"] for n in ("ahi", "alo"))
        y_ = [sb(f"y{b}", [P, D]) for b in "AB"]
        pick = sb("pick", [2 * E, P], R32)
        ps = ctx.enter_context(nc.psum_tensor("eps", [P, 8, 512], F32))

        def mm_bank(piece, b):
            return ps[:, 2 * (piece % 3) + b]

        def t_bank(b):
            return ps[:, 6 + b]

        SMAX = float(1.0 / (1.0 + np.exp(-ALPHA * LIMIT)))

        def gu_bank(nb, p, b):
            return t_bank(b if nb == 2 else p % 2)

        wgu_v = ins["exp_w_gu"].rearrange("l e (k p) n -> p (l e) k n", p=P)
        wdn_v = ins["exp_w_down"].rearrange("l e (k p) n -> p (l e) k n", p=P)

        def over_passes(eng, name, body):
            reg = eng.alloc_register(name)
            eng.reg_mov(reg, 0)
            most = E * NPASS
            with eng.Fori(0, E) as e:
                two = eng.value_load(npass[0:1, 0, bass.ds(e, 1)], min_val=0, max_val=NPASS)
                one = eng.value_load(npass[0:1, 1, bass.ds(e, 1)], min_val=0, max_val=1)
                with eng.If(two > 0):
                    with eng.Fori(0, two) as i:
                        body(e, 2, eng.snap(reg, min_val=0, max_val=most), e * CAP + i * 2 * P)
                        eng.reg_add(reg, reg, 1)
                with eng.Else():
                    eng.nop()
                with eng.If(one > 0):
                    body(e, 1, eng.snap(reg, min_val=0, max_val=most), e * CAP + two * 2 * P)
                    eng.reg_add(reg, reg, 1)
                with eng.Else():
                    eng.nop()
            return eng.snap(reg, min_val=0, max_val=most)

        def step(ins_, name, b, nb, extra=1):
            ins_.then_inc(ev(name), 1 if nb == 2 else 1 + (extra if b == 0 else 0))

        block = ctx.enter_context(nc.Block())

        @block.sync
        def _(sp):
            def load(e, n):
                p, kh = ITEMS[n]
                ks = slice(kh * KH, (kh + 1) * KH)
                if p < NPIECE:
                    src = wgu_v[:, bass.ds(e, 1), ks, p * PC:(p + 1) * PC]
                else:
                    src = wdn_v[:, bass.ds(e, 1), ks, (p - NPIECE) * PC:(p - NPIECE + 1) * PC]
                sp.dma_start(raw[:, n % NRAW], src.rearrange("p o k n -> p (o k) n")).then_inc(ev(f"raw{n % NRAW}"), 16)

            def body(e, nb, ps_, row0):
                for n in range(NI):
                    sp.wait_ge(ev("lo_made"), ps_ * NI + n + 1)
                    sp.nop().then_inc(ev("sp_turn"), 1)
                    load(e, n)

            total = over_passes(sp, "sp_pass", body)
            for n in range(AHEAD):
                sp.wait_ge(ev("lo_made"), total * NI + n + 1)
                sp.nop().then_inc(ev("sp_turn"), 1)
                load(0, n)

        @block.gpsimd
        def _(pool):
            g = nc.gpsimd

            def turn():
                pool.nop().then_inc(ev("pool_turn"), 1)

            def gather():
                for b in range(2):
                    g.indirect_dma_start(out=xg[b][:], out_offset=None, in_=d["xn"],
                                         in_offset=bass.IndirectOffsetOnAxis(ap=ids[b][:, 0:1], axis=0))\
                        .then_inc(ev("gathered"), 16)

            def store_rows():
                for b in range(2):
                    g.indirect_dma_start(out=d["sum"], out_offset=bass.IndirectOffsetOnAxis(ap=to[b][:], axis=0),
                                         in_=y_[b][:], in_offset=None, bounds_check=SEQ - 1, oob_is_err=False,
                                         compute_op=ALU.add).then_inc(ev("y_stored"), 16)

            def body(e, nb, ps_, row0):
                for b in range(2):
                    g.dma_start(ids[b][:], d["table"][bass.ds(row0 + b * P, P), :]).then_inc(ev("ids"), 16)
                pool.wait_ge(ev("ids"), ps_ * 32 + 32)
                pool.wait_ge(ev("x_trans"), ps_ * 4 + 4)
                turn()
                gather()
                pool.wait_ge(ev("y_made"), ps_ * 4 + 4)
                turn()
                store_rows()
                pool.wait_ge(ev("y_stored"), ps_ * 32 + 32)
                turn()
                for b in range(nb):
                    step(g.tensor_copy(share[b][:], ids[b][:, 2:3].bitcast(F32)), "share_set", b, nb)
                for b in range(2):
                    if b < nb:
                        g.tensor_copy(to[b][:], ids[b][:, 1:2]).then_inc(ev("to_set"), 1)
                    else:
                        g.memset(to[b][:], NOROW).then_inc(ev("to_set"), 1)
                pool.wait_ge(ev("to_set"), ps_ * 2 + 4)
                pool.wait_ge(ev("share_set"), ps_ * 2 + 2)
                pool.wait_ge(ev("gathered"), ps_ * 32 + 32)
                turn()

            for b in range(2):
                g.memset(to[b][:], NOROW).then_inc(ev("to_set"), 1)
            pool.wait_ge(ev("to_set"), 2)
            pool.wait_ge(ev("y_blank"), 2)
            total = over_passes(pool, "pool_pass", body)
            pool.wait_ge(ev("x_trans"), total * 4 + 4)
            turn()
            gather()
            pool.wait_ge(ev("y_made"), total * 4 + 4)
            turn()
            store_rows()
            pool.wait_ge(ev("y_stored"), total * 32 + 32)
            pool.wait_ge(ev("gathered"), total * 32 + 32)
            turn()

        @block.tensor
        def _(pe):
            t = nc.tensor

            def turn():
                pe.nop().then_inc(ev("pe_turn"), 1)

            def x_transposes(ps_, b):
                for half in range(2):
                    if b:
                        pe.wait_ge(ev("x_lo"), ps_ * 4 + 1 + half)
                        turn()
                    for k in range(KH):
                        kk = half * KH + k
                        last = t.transpose(t_bank(half)[:, k * P:(k + 1) * P], xg[b][:, kk * P:(kk + 1) * P], ident[:])
                    last.then_inc(ev("x_trans"), 1)

            def body(e, nb, ps_, row0):
                def item(n, b):
                    p, kh = ITEMS[n]
                    hi, lo = (xhi[b], xlo[b]) if p < NPIECE else (ahi[b], alo[b])
                    o = mm_bank(p, b)
                    last_item = kh == 1 and p >= NPIECE
                    for part in range(3):
                        if n < 2:
                            pe.wait_ge(ev("x_lo" if part == 2 else "x_hi"), ps_ * 4 + 2 * b + n + 1)
                        elif n >= 8 and part != 1:
                            pe.wait_ge(ev("a_lo" if part == 2 else "a_hi"), ps_ * 8 + (4 if kh == 0 else 8))
                        for k in range(KH):
                            kk = kh * KH + k
                            last = t.matmul(o, (lo if part == 2 else hi)[:, kk],
                                            (wlo if part == 1 else whi)[:, n % NHL, k],
                                            start=kh == 0 and part == 0 and k == 0,
                                            stop=last_item and part == 2 and k == KH - 1)
                    if kh == 1 and p < NPIECE:
                        pe.wait_ge(ev("picked"), ps_ + 1)
                        last = t.matmul(o, pick[:], bparts[:, p * PC:(p + 1) * PC], start=False, stop=True)
                    step(last, "mm_done", b, nb)

                def a_transposes(p):
                    for b in range(nb):
                        pe.wait_ge(ev("a_made"), ps_ * 8 + 2 * p + b + 1)
                        if p == 0:
                            pe.wait_ge(ev("x_lo"), ps_ * 4 + 4)
                        before = p - (1 if nb == 2 else 2)
                        if before >= 0:
                            pe.wait_ge(ev("a_lo"), ps_ * 8 + 2 * before + b + 1)
                        turn()
                        for q in range(2):
                            last = t.transpose(gu_bank(nb, p, b)[:, q * P:(q + 1) * P],
                                               am[b][:, p % 2, q * P:(q + 1) * P], ident[:])
                        step(last, "a_trans", b, nb)

                for n in range(NI):
                    if n == 2:
                        pe.wait_ge(ev("y_made"), ps_ * 4 + 2)
                    if n == 4:
                        pe.wait_ge(ev("y_made"), ps_ * 4 + 4)
                    pe.wait_ge(ev("lo_made"), ps_ * NI + NRAW + n + 1)
                    for b in range(nb):
                        item(n, b)
                    if n in TURNED:
                        a_transposes(TURNED.index(n))
                    if n == 10:
                        pe.wait_ge(ev("gathered"), (ps_ + 1) * 32 + 32)
                        pe.wait_ge(ev("a_lo"), ps_ * 8 + 8)
                        turn()
                    if n >= 10:
                        x_transposes(ps_ + 1, n - 10)

            pe.sem_inc(ev("x_trans"), 4)
            pe.sem_inc(ev("mm_done"), 2)
            pe.wait_ge(ev("gathered"), 32)
            for b in range(2):
                x_transposes(0, b)
            over_passes(pe, "pe_pass", body)

        @block.scalar
        def _(act):
            a = nc.scalar

            def split(value, n):
                act.wait_ge(ev(f"raw{n % NRAW}"), value["raw"])
                if value["mm"] is not None:
                    act.wait_ge(ev("mm_done"), value["mm"])
                a.copy(whi[:, n % NHL], raw[:, n % NRAW]).then_inc(ev("hi_made"), 1)

            def x_split(ps_, b):
                for half in range(2):
                    act.wait_ge(ev("x_trans"), ps_ * 4 + 2 * b + half + 5)
                    a.copy(xhi[b][:, half * KH:(half + 1) * KH].rearrange("p k n -> p (k n)"), t_bank(half))\
                        .then_inc(ev("x_hi"), 1)

            def body(e, nb, ps_, row0):
                def ahead(n):
                    m = n + AHEAD
                    split({"raw": 16 * (ps_ * (NI // NRAW) + m // NRAW + 1), "mm": ps_ * 24 + 2 * (m - NHL) + 4}, m)

                for n in range(NI):
                    ahead(n)
                    if n in (1, 3, 5, 7):
                        p = n // 2
                        for b in range(nb):
                            act.wait_ge(ev("mm_done"), ps_ * 24 + 2 * n + b + 3)
                            step(a.activation(sg[b][:, p % 2], mm_bank(p, b)[:, 0:PC:2], ACT.Sigmoid, scale=ALPHA),
                                 "sg_made", b, nb)
                    if n in TURNED:
                        p = TURNED.index(n)
                        for b in range(nb):
                            act.wait_ge(ev("a_trans"), ps_ * 8 + 2 * p + b + 1)
                            step(a.copy(ahi[b][:, 2 * p:2 * p + 2].rearrange("p k n -> p (k n)"),
                                        gu_bank(nb, p, b)[:, 0:2 * P]), "a_hi", b, nb)
                    if n >= 10:
                        x_split(ps_ + 1, n - 10)
                        if n == 10:
                            act.wait_ge(ev("y_stored"), ps_ * 32 + 32)
                            act.wait_ge(ev("share_set"), ps_ * 2 + 2)
                        q = n - 10
                        for b in range(nb):
                            act.wait_ge(ev("mm_done"), ps_ * 24 + 2 * n + b + 3)
                            step(a.mul(y_[b][:, q * PC:(q + 1) * PC], mm_bank(4 + q, b), share[b][:, 0:1]), "y_made", b, nb)

            act.sem_inc(ev("y_made"), 4)
            for n in range(AHEAD):
                split({"raw": 16 * (n // NRAW + 1), "mm": None}, n)
                if n in (1, 2):
                    x_split(0, n - 1)
            over_passes(act, "act_pass", body)

        @block.vector
        def _(dve):
            v = nc.vector

            def split(n, value):
                dve.wait_ge(ev("hi_made"), value)
                v.tensor_tensor(wlo[:, n % NHL], raw[:, n % NRAW], whi[:, n % NHL].bitcast(F32), ALU.subtract)\
                    .then_inc(ev("lo_made"), 1)

            def x_rest(ps_, b):
                for half in range(2):
                    dve.wait_ge(ev("x_hi"), ps_ * 4 + 2 * b + half + 1)
                    hs = slice(half * KH, (half + 1) * KH)
                    v.tensor_tensor(xlo[b][:, hs].rearrange("p k n -> p (k n)"), t_bank(half),
                                    xhi[b][:, hs].rearrange("p k n -> p (k n)").bitcast(F32), ALU.subtract)\
                        .then_inc(ev("x_lo"), 1)

            def body(e, nb, ps_, row0):
                def ahead(n):
                    m = n + AHEAD
                    split(m, ps_ * NI + m + 1)

                v.tensor_copy(pick[:], pickf[:, bass.ds(e, 1)].broadcast_to([2 * E, P])).then_inc(ev("picked"), 1)

                def product(p, b):
                    g, up = mm_bank(p, b)[:, 0:PC:2], mm_bank(p, b)[:, 1:PC:2]
                    dve.wait_ge(ev("sg_made"), ps_ * 8 + 2 * p + b + 1)
                    step(v.tensor_scalar(u_[b][:], up, LIMU, 2.0 - LIMU, ALU.min, ALU.max), "u_made", b, nb)
                    dve.wait_ge(ev("u_made"), ps_ * 8 + 2 * p + b + 1)
                    step(v.scalar_tensor_tensor(u_[b][:], g, LIMIT, u_[b][:], ALU.min, ALU.mult), "ug_made", b, nb)
                    dve.wait_ge(ev("ug_made"), ps_ * 8 + 2 * p + b + 1)
                    step(v.scalar_tensor_tensor(am[b][:, p % 2], sg[b][:, p % 2], SMAX, u_[b][:], ALU.min, ALU.mult),
                         "a_made", b, nb)

                def rest(p, b):
                    dve.wait_ge(ev("a_hi"), ps_ * 8 + 2 * p + b + 1)
                    step(v.tensor_tensor(alo[b][:, 2 * p:2 * p + 2].rearrange("p k n -> p (k n)"),
                                         gu_bank(nb, p, b)[:, 0:2 * P],
                                         ahi[b][:, 2 * p:2 * p + 2].rearrange("p k n -> p (k n)").bitcast(F32),
                                         ALU.subtract), "a_lo", b, nb)

                for n in range(NI):
                    ahead(n)
                    if n in (1, 3, 5, 7):
                        for b in range(nb):
                            product(n // 2, b)
                    if n in TURNED:
                        for b in range(nb):
                            rest(TURNED.index(n), b)
                    if n >= 10:
                        x_rest(ps_ + 1, n - 10)

            dve.sem_inc(ev("lo_made"), NRAW)
            for b in range(2):
                v.memset(y_[b][:], 0.0).then_inc(ev("y_blank"), 1)
            for n in range(AHEAD):
                split(n, n + 1)
                if n in (1, 2):
                    x_rest(0, n - 1)
            over_passes(dve, "dve_pass", body)


def final_norm(nc, ins, d, ev, eps2, out):
    with ExitStack() as ctx:
        def sb(name, shape, dt=F32):
            return ctx.enter_context(nc.sbuf_tensor(name, shape, dt))

        acc = sb("acc", [P, NT, D])
        sq = sb("sq", [P, D])
        nfin = sb("nfin", [P, D])
        s2 = sb("s2", [P, NT, 2])
        block = ctx.enter_context(nc.Block())
        hrows = d["sum"].rearrange("(i p) n -> i p n", p=P)
        orows = out.rearrange("(i p) n -> i p n", p=P)

        @block.sync
        def _(sp):
            sp.dma_start(nfin[:], ins["norm_final"].rearrange("(o n) -> o n", o=1).broadcast_to([P, D])).then_inc(ev("nfin"), 16)
            for i in range(NT):
                sp.dma_start(acc[:, i], hrows[i]).then_inc(ev(f"sum_loaded{i}"), 16)
            for i in range(NT):
                sp.wait_ge(ev("final"), i + 1)
                sp.dma_start(orows[i], acc[:, i]).then_inc(ev("out_stored"), 16)
            sp.wait_ge(ev("out_stored"), 16 * NT)

        @block.vector
        def _(dve):
            v = nc.vector
            n = [0]

            def link(ins_):
                n[0] += 1
                ins_.then_inc(ev("c_step"), 1)
                dve.wait_ge(ev("c_step"), n[0])

            dve.wait_ge(ev("nfin"), 16)
            for i in range(NT):
                dve.wait_ge(ev("c_rms"), i + 1)
                link(v.reciprocal(s2[:, i, 1:2], s2[:, i, 0:1]))
                link(v.scalar_tensor_tensor(acc[:, i], acc[:, i], s2[:, i, 1:2], nfin[:], ALU.mult, ALU.mult))
                dve.sem_inc(ev("final"), 1)

        @block.scalar
        def _(act):
            a = nc.scalar
            for i in range(NT):
                act.wait_ge(ev(f"sum_loaded{i}"), 16)
                a.activation(sq[:], acc[:, i], ACT.Square, accum_out=s2[:, i, 0:1]).then_inc(ev("c_sq"), 1)
                act.wait_ge(ev("c_sq"), i + 1)
                a.activation(s2[:, i, 0:1], s2[:, i, 0:1], ACT.Sqrt, scale=1.0 / D, bias=eps2[:, 0:1]).then_inc(ev("c_rms"), 1)


_SMALL = ["hg_lb_logits", "norm_mix", "w_in", "hg_norm", "ml_conv_w", "ml_conv_b", "ml_wq", "ml_wk", "ml_wv",
          "ml_gate_b", "ml_norm", "ml_skip", "w_branch_hg", "w_branch_ml", "w_out", "norm_ffn", "router_w",
          "router_b", "exp_w_gu", "exp_b_gu", "exp_w_down", "exp_b_down", "norm_final"]


def kernel(**inputs):
    import concourse.bacc as bacc
    from concourse.bass_utils import run_bass_kernel_spmd

    nc = bacc.Bacc("TRN2", target_bir_lowering=False, num_devices=1)
    arrays = {n: np.ascontiguousarray(inputs[n]) for n in _SMALL}
    x, meta = np.asarray(inputs["x"]), np.asarray(inputs["meta_tokens"])
    arrays["rows"] = np.concatenate([np.zeros((PAD, D), x.dtype), meta, x[0], np.zeros((SPAN, D), x.dtype)], axis=0)
    ins = {n: nc.dram_tensor(n, a.shape, mybir.dt.from_np(a.dtype), kind="ExternalInput").ap() for n, a in arrays.items()}
    out = nc.dram_tensor("out", [SEQ, D], F32, kind="ExternalOutput").ap()
    build(nc, ins, out)
    r = run_bass_kernel_spmd(nc, [arrays], core_ids=[0])
    return r.results[0]["out"].reshape(1, SEQ, D)
```
